# Optimizing a Trainium2 kernel written in Bass

```python
import jax, jax.numpy as jnp
from jax import lax
import numpy as np
import math

D_MODEL = 1024
BATCH = 1
SEQ = 2048
DEPTH = 2

GRID_W = 64
CTX_LEN = 256
D_MIX = D_MODEL
HEAD_DIM = 64
ATT_W = D_MIX // 2
N_HEADS = ATT_W // HEAD_DIM
N_KV_HEADS = 2
GQA_GROUP = N_HEADS // N_KV_HEADS
KV_W = N_KV_HEADS * HEAD_DIM
CONV_W = D_MIX // 4
FOUR_W = D_MIX - ATT_W - CONV_W
FOUR_HEADS = 4
FOUR_HEAD_DIM = FOUR_W // FOUR_HEADS
CONV_K = 31
WINDOW = 128
BLOCK = 128
ROPE_BASE = 10000.0
EPS = 1e-6
NEG_INF = -1e30
SPLITS = (ATT_W, KV_W, KV_W, ATT_W, CONV_W, CONV_W, CONV_W, FOUR_W, FOUR_W)
IN_W = ATT_W + 2 * KV_W + ATT_W + 3 * CONV_W + 2 * FOUR_W


def rms_norm(x, g):
    xf = x.astype(jnp.float32)
    y = xf * lax.rsqrt(jnp.mean(xf * xf, axis=-1, keepdims=True) + EPS)
    return (y * g.astype(jnp.float32)).astype(x.dtype)

def layer_norm(x, g, b):
    xf = x.astype(jnp.float32)
    mu = jnp.mean(xf, axis=-1, keepdims=True)
    var = jnp.mean(jnp.square(xf - mu), axis=-1, keepdims=True)
    y = (xf - mu) * lax.rsqrt(var + EPS)
    return (y * g.astype(jnp.float32) + b.astype(jnp.float32)).astype(x.dtype)

def split_cols(p):
    outs = []
    off = 0
    for w in SPLITS:
        outs.append(p[..., off:off + w])
        off += w
    return outs

def rope_axis(x, pos):
    half = x.shape[-1] // 2
    freqs = ROPE_BASE ** (-jnp.arange(half, dtype=jnp.float32) / half)
    ang = pos[:, None] * freqs[None, :]
    cos = jnp.cos(ang)[:, None, :].astype(x.dtype)
    sin = jnp.sin(ang)[:, None, :].astype(x.dtype)
    x1, x2 = x[..., :half], x[..., half:]
    return jnp.concatenate([x1 * cos - x2 * sin, x1 * sin + x2 * cos], axis=-1)

def rope_2d(x, row, col):
    h = x.shape[-1] // 2
    return jnp.concatenate([rope_axis(x[..., :h], row), rope_axis(x[..., h:], col)], axis=-1)

def windowed_attention(q, k, v, kc, vc, sink):
    bn, s = q.shape[0], q.shape[1]
    nb = s // BLOCK
    n_ctx = kc.shape[1]
    scale = HEAD_DIM ** -0.5
    qb = q.reshape(bn, nb, BLOCK, N_KV_HEADS, GQA_GROUP, HEAD_DIM)
    pad = ((0, 0), (BLOCK, BLOCK), (0, 0), (0, 0))
    kp = jnp.pad(k, pad).reshape(bn, nb + 2, BLOCK, N_KV_HEADS, HEAD_DIM)
    vp = jnp.pad(v, pad).reshape(bn, nb + 2, BLOCK, N_KV_HEADS, HEAD_DIM)
    kw = jnp.concatenate([kp[:, :-2], kp[:, 1:-1], kp[:, 2:]], axis=2)
    vw = jnp.concatenate([vp[:, :-2], vp[:, 1:-1], vp[:, 2:]], axis=2)
    s_loc = jnp.einsum('bnqhgd,bnkhd->bnhgqk', qb, kw).astype(jnp.float32) * scale
    q_rel = jnp.arange(BLOCK) + BLOCK
    k_rel = jnp.arange(3 * BLOCK)
    band = jnp.abs(q_rel[:, None] - k_rel[None, :]) <= WINDOW
    k_abs = jnp.arange(nb)[:, None] * BLOCK - BLOCK + k_rel[None, :]
    valid = (k_abs >= 0) & (k_abs < s)
    mask = band[None, :, :] & valid[:, None, :]
    s_loc = jnp.where(mask[None, :, None, None], s_loc, NEG_INF)
    s_ctx = jnp.einsum('bnqhgd,blhd->bnhgql', qb, kc).astype(jnp.float32) * scale
    s_sink = jnp.broadcast_to(
        sink.astype(jnp.float32).reshape(1, 1, N_KV_HEADS, GQA_GROUP, 1, 1),
        s_loc.shape[:-1] + (1,))
    p = jax.nn.softmax(jnp.concatenate([s_loc, s_ctx, s_sink], axis=-1), axis=-1)
    p_loc = p[..., :3 * BLOCK].astype(v.dtype)
    p_ctx = p[..., 3 * BLOCK:3 * BLOCK + n_ctx].astype(v.dtype)
    o = (jnp.einsum('bnhgqk,bnkhd->bnqhgd', p_loc, vw)
         + jnp.einsum('bnhgql,blhd->bnqhgd', p_ctx, vc))
    return o.reshape(bn, s, ATT_W)

def context_attention(q, k, v, sink):
    bn, n_ctx = q.shape[0], q.shape[1]
    scale = HEAD_DIM ** -0.5
    qh = q.reshape(bn, n_ctx, N_KV_HEADS, GQA_GROUP, HEAD_DIM)
    sc = jnp.einsum('blhgd,bmhd->bhglm', qh, k).astype(jnp.float32) * scale
    s_sink = jnp.broadcast_to(
        sink.astype(jnp.float32).reshape(1, N_KV_HEADS, GQA_GROUP, 1, 1), sc.shape[:-1] + (1,))
    p = jax.nn.softmax(jnp.concatenate([sc, s_sink], axis=-1), axis=-1)
    o = jnp.einsum('bhglm,bmhd->blhgd', p[..., :n_ctx].astype(v.dtype), v)
    return o.reshape(bn, n_ctx, ATT_W)

def conformer_conv(a, b_glu, conv_w, conv_b, ln_g, ln_b):
    u = a * jax.nn.sigmoid(b_glu)
    y = lax.conv_general_dilated(
        u, conv_w[:, None, :], window_strides=(1,),
        padding=[(CONV_K // 2, CONV_K // 2)],
        dimension_numbers=('NWC', 'WIO', 'NWC'),
        feature_group_count=CONV_W) + conv_b
    return jax.nn.silu(layer_norm(y, ln_g, ln_b))

def fourier_mix(u, w_four, b_four):
    bn, n = u.shape[0], u.shape[1]
    uh = u.reshape(bn, n, FOUR_HEADS, FOUR_HEAD_DIM).astype(jnp.float32)
    f = jnp.fft.fftn(uh, axes=(1, 3), norm='ortho').real
    f = f.reshape(bn, n, FOUR_W).astype(u.dtype)
    return f @ w_four + b_four

def mixer_out(attn, parts, conv_w, conv_b, ln_g, ln_b, w_four, b_four, w_out):
    _, _, _, g_att, c_a, c_b, g_conv, f_u, g_four = parts
    y_conv = conformer_conv(c_a, c_b, conv_w, conv_b, ln_g, ln_b)
    y_four = fourier_mix(f_u, w_four, b_four)
    y = jnp.concatenate([attn * jax.nn.silu(g_att),
                         y_conv * jax.nn.silu(g_conv),
                         y_four * jax.nn.silu(g_four)], axis=-1)
    return y @ w_out

def first_inputs(seed: int = 0) -> dict:
    key = jax.random.key(seed)
    ks = jax.random.split(key, 20)
    f32 = jnp.float32
    nrm = lambda k, shp, s: jax.random.normal(k, shp, f32) * s
    return {
        'x': nrm(ks[0], (BATCH, SEQ, D_MODEL), 1.0),
        'c': nrm(ks[1], (BATCH, D_MODEL), 1.0),
        'ctx': nrm(ks[2], (BATCH, CTX_LEN, D_MODEL), 1.0),
        'c_ctx': nrm(ks[3], (D_MODEL,), 1.0),
        'w_ada': nrm(ks[4], (DEPTH, D_MODEL, 3 * D_MODEL), 0.5 * D_MODEL ** -0.5),
        'b_ada': nrm(ks[5], (DEPTH, 3 * D_MODEL), 0.02),
        'norm_g': 1.0 + nrm(ks[6], (DEPTH, D_MODEL), 0.02),
        'w_in': nrm(ks[7], (DEPTH, D_MODEL, IN_W), D_MODEL ** -0.5),
        'attn_sink': nrm(ks[8], (DEPTH, N_HEADS), 0.5),
        'conv_w': nrm(ks[9], (DEPTH, CONV_K, CONV_W), CONV_K ** -0.5),
        'conv_b': nrm(ks[10], (DEPTH, CONV_W), 0.02),
        'conv_ln_g': 1.0 + nrm(ks[11], (DEPTH, CONV_W), 0.02),
        'conv_ln_b': nrm(ks[12], (DEPTH, CONV_W), 0.02),
        'w_four': nrm(ks[13], (DEPTH, FOUR_W, FOUR_W), FOUR_W ** -0.5),
        'b_four': nrm(ks[14], (DEPTH, FOUR_W), 0.02),
        'w_out': nrm(ks[15], (DEPTH, D_MIX, D_MODEL), D_MIX ** -0.5),
        'final_g': 1.0 + nrm(ks[16], (D_MODEL,), 0.02),
    }

def first_block(x, c, ctx, c_ctx, w_ada, b_ada, norm_g, w_in, attn_sink, conv_w, conv_b,
              conv_ln_g, conv_ln_b, w_four, b_four, w_out, final_g):
    bn, s, _ = x.shape
    n_ctx = ctx.shape[1]
    ROWS = s // GRID_W
    row_pos = jnp.repeat(jnp.arange(ROWS, dtype=jnp.float32), GRID_W)
    col_pos = jnp.tile(jnp.arange(GRID_W, dtype=jnp.float32), ROWS)
    sc = jax.nn.silu(c)
    scc = jax.nn.silu(c_ctx)
    h_ctx = ctx
    for l in range(DEPTH):
        shift, scale, gate = jnp.split(sc @ w_ada[l] + b_ada[l], 3, axis=-1)
        shift_c, scale_c, gate_c = jnp.split(scc @ w_ada[l] + b_ada[l], 3, axis=-1)
        hc = rms_norm(h_ctx, norm_g[l]) * (1.0 + scale_c) + shift_c
        if l < DEPTH - 1:
            pc = split_cols(hc @ w_in[l])
            kc_raw, vc_raw = pc[1], pc[2]
        else:
            kv = hc @ w_in[l][:, ATT_W:ATT_W + 2 * KV_W]
            kc_raw, vc_raw = kv[..., :KV_W], kv[..., KV_W:]
        kc = kc_raw.reshape(bn, n_ctx, N_KV_HEADS, HEAD_DIM)
        vc = vc_raw.reshape(bn, n_ctx, N_KV_HEADS, HEAD_DIM)

        hx = rms_norm(x, norm_g[l]) * (1.0 + scale[:, None, :]) + shift[:, None, :]
        px = split_cols(hx @ w_in[l])
        q = rope_2d(px[0].reshape(bn, s, N_HEADS, HEAD_DIM), row_pos, col_pos)
        k = rope_2d(px[1].reshape(bn, s, N_KV_HEADS, HEAD_DIM), row_pos, col_pos)
        v = px[2].reshape(bn, s, N_KV_HEADS, HEAD_DIM)
        attn = windowed_attention(q, k, v, kc, vc, attn_sink[l])
        y = mixer_out(attn, px, conv_w[l], conv_b[l], conv_ln_g[l], conv_ln_b[l],
                      w_four[l], b_four[l], w_out[l])

        if l < DEPTH - 1:
            qc = pc[0].reshape(bn, n_ctx, N_HEADS, HEAD_DIM)
            attn_c = context_attention(qc, kc, vc, attn_sink[l])
            yc = mixer_out(attn_c, pc, conv_w[l], conv_b[l], conv_ln_g[l], conv_ln_b[l],
                           w_four[l], b_four[l], w_out[l])
            h_ctx = h_ctx + gate_c * yc
        x = x + gate[:, None, :] * y
    return rms_norm(x, final_g)


DEPTH_2 = 1

D_INNER = 2 * D_MODEL
CONV_WIDTH = 4
LRU_WIDTH = D_INNER // 4
LRU_HEADS = 8
LRU_HEAD_DIM = LRU_WIDTH // LRU_HEADS
LRU_C = 8.0
HG_WIDTH = D_INNER // 4
HG_HEAD_DIM = 128
HG_HEADS = HG_WIDTH // HG_HEAD_DIM
HG_CHUNK = 64
SSD_WIDTH = D_INNER // 2
SSD_HEAD_DIM = 64
SSD_HEADS = SSD_WIDTH // SSD_HEAD_DIM
SSD_GROUPS = 2
SSD_STATE = 128
SSD_CHUNK = 128
SSD_CONV_DIM = SSD_WIDTH + 2 * SSD_GROUPS * SSD_STATE
SPLIT_SIZES = (LRU_WIDTH, LRU_WIDTH,
               HG_WIDTH, HG_WIDTH, HG_WIDTH, HG_WIDTH,
               SSD_WIDTH, SSD_CONV_DIM, SSD_HEADS)
N_IN = sum(SPLIT_SIZES)


def _split_points():
    return [int(v) for v in np.cumsum(SPLIT_SIZES)[:-1]]

def rmsnorm(x, w):
    xf = x.astype(jnp.float32)
    inv = lax.rsqrt(jnp.mean(xf * xf, axis=-1, keepdims=True) + EPS)
    return (xf * inv).astype(x.dtype) * w

def causal_conv(x, w, b):
    K = w.shape[0]
    S = x.shape[1]
    xp = jnp.pad(x, ((0, 0), (K - 1, 0), (0, 0)))
    out = b
    for k in range(K):
        out = out + xp[:, k:k + S] * w[k]
    return out

def rg_lru(x, wa, ba, wx, bx, lam):
    B, S, _ = x.shape
    xh = x.reshape(B, S, LRU_HEADS, LRU_HEAD_DIM)
    r = jax.nn.sigmoid(jnp.einsum('bshi,hij->bshj', xh, wa) + ba).reshape(B, S, LRU_WIDTH)
    i = jax.nn.sigmoid(jnp.einsum('bshi,hij->bshj', xh, wx) + bx).reshape(B, S, LRU_WIDTH)
    log_a = -LRU_C * r * jax.nn.softplus(-lam)
    a = jnp.exp(log_a)
    mult = jnp.sqrt(-jnp.expm1(2.0 * log_a))
    b = mult * (i * x)

    def combine(left, right):
        a1, b1 = left
        a2, b2 = right
        return a1 * a2, a2 * b1 + b2

    _, h = lax.associative_scan(combine, (a, b), axis=1)
    return h

def hgrn2_chunked(q, k, v, log_f):
    dtype = v.dtype
    q, k, v, log_f = (t.astype(jnp.float32) for t in (q, k, v, log_f))
    B, S, H, DK = q.shape
    DV = v.shape[-1]
    n = S // HG_CHUNK

    def to_chunks(t):
        return t.reshape(B, n, HG_CHUNK, H, t.shape[-1]).transpose(1, 0, 3, 2, 4)

    qc, kc, vc, lc = (to_chunks(t) for t in (q, k, v, log_f))
    causal = jnp.tril(jnp.ones((HG_CHUNK, HG_CHUNK), bool))[:, :, None]

    def step(state, inp):
        qi, ki, vi, li = inp
        cum = jnp.cumsum(li, axis=2)
        diff = cum[:, :, :, None, :] - cum[:, :, None, :, :]
        decay = jnp.where(causal, jnp.exp(jnp.where(causal, diff, 0.0)), 0.0)
        scores = jnp.einsum('bhtd,bhsd,bhtsd->bhts', qi, ki, decay)
        o = (jnp.einsum('bhts,bhsv->bhtv', scores, vi)
             + jnp.einsum('bhtd,bhdv->bhtv', qi * jnp.exp(cum), state))
        last = cum[:, :, -1:, :]
        state = (state * jnp.exp(last[:, :, 0, :, None])
                 + jnp.einsum('bhsd,bhsv->bhdv', ki * jnp.exp(last - cum), vi))
        return state, o

    s0 = jnp.zeros((B, H, DK, DV), jnp.float32)
    _, o = lax.scan(step, s0, (qc, kc, vc, lc))
    return o.transpose(1, 0, 3, 2, 4).reshape(B, S, H, DV).astype(dtype)

def ssd_chunked(x, dt, A, Bm, Cm):
    dtype = x.dtype
    x, dt, A, Bm, Cm = (t.astype(jnp.float32) for t in (x, dt, A, Bm, Cm))
    B, S, H, P = x.shape
    G, N = Bm.shape[2], Bm.shape[3]
    J = H // G
    C = SSD_CHUNK
    n = S // C
    xdt = (x * dt[..., None]).reshape(B, n, C, G, J, P).transpose(1, 0, 2, 3, 4, 5)
    dA = (dt * A).reshape(B, n, C, G, J).transpose(1, 0, 2, 3, 4)
    Bc = Bm.reshape(B, n, C, G, N).transpose(1, 0, 2, 3, 4)
    Cc = Cm.reshape(B, n, C, G, N).transpose(1, 0, 2, 3, 4)
    causal = jnp.tril(jnp.ones((C, C), bool))[:, :, None, None]

    def step(state, inp):
        xi, ai, bi, ci = inp
        cum = jnp.cumsum(ai, axis=1)
        diff = cum[:, :, None] - cum[:, None, :]
        L = jnp.where(causal, jnp.exp(jnp.where(causal, diff, 0.0)), 0.0)
        cb = jnp.einsum('btgn,bsgn->btsg', ci, bi)
        y = jnp.einsum('btsg,btsgj,bsgjp->btgjp', cb, L, xi)
        y = y + jnp.einsum('btgn,bgjpn,btgj->btgjp', ci, state, jnp.exp(cum))
        last = cum[:, -1]
        state = (state * jnp.exp(last)[..., None, None]
                 + jnp.einsum('bsgn,bsgj,bsgjp->bgjpn', bi, jnp.exp(last[:, None] - cum), xi))
        return state, y

    s0 = jnp.zeros((B, G, J, P, N), jnp.float32)
    _, y = lax.scan(step, s0, (xdt, dA, Bc, Cc))
    return y.transpose(1, 0, 2, 3, 4, 5).reshape(B, S, H, P).astype(dtype)

def second_inputs(seed: int = 0) -> dict:
    key = jax.random.key(seed)
    ks = jax.random.split(key, 24)
    f32 = jnp.float32

    def nrm(k, shape, scale):
        return jax.random.normal(k, shape, f32) * scale

    x = nrm(ks[0], (BATCH, SEQ, D_MODEL), 1.0)
    c = nrm(ks[1], (BATCH, D_MODEL), 1.0)
    norm_w = 1.0 + nrm(ks[2], (DEPTH_2, D_MODEL), 0.01)
    w_ada = nrm(ks[3], (DEPTH_2, D_MODEL, 3 * D_MODEL), 0.5 * D_MODEL ** -0.5)
    b_ada = nrm(ks[4], (DEPTH_2, 3 * D_MODEL), 0.01)
    w_in = nrm(ks[5], (DEPTH_2, D_MODEL, N_IN), D_MODEL ** -0.5)
    lru_conv_w = nrm(ks[6], (DEPTH_2, CONV_WIDTH, LRU_WIDTH), CONV_WIDTH ** -0.5)
    lru_conv_b = nrm(ks[7], (DEPTH_2, LRU_WIDTH), 0.01)
    lru_wa = nrm(ks[8], (DEPTH_2, LRU_HEADS, LRU_HEAD_DIM, LRU_HEAD_DIM), LRU_HEAD_DIM ** -0.5)
    lru_ba = nrm(ks[9], (DEPTH_2, LRU_HEADS, LRU_HEAD_DIM), 0.01)
    lru_wx = nrm(ks[10], (DEPTH_2, LRU_HEADS, LRU_HEAD_DIM, LRU_HEAD_DIM), LRU_HEAD_DIM ** -0.5)
    lru_bx = nrm(ks[11], (DEPTH_2, LRU_HEADS, LRU_HEAD_DIM), 0.01)
    u = jax.random.uniform(ks[12], (DEPTH_2, LRU_WIDTH), f32, 0.9, 0.999) ** (1.0 / LRU_C)
    lru_lambda = jnp.log(u) - jnp.log1p(-u)
    hg_lb_logits = nrm(ks[13], (DEPTH_2, HG_WIDTH), 0.5)
    hg_norm_w = 1.0 + nrm(ks[14], (DEPTH_2, HG_WIDTH), 0.01)
    ssd_conv_w = nrm(ks[15], (DEPTH_2, CONV_WIDTH, SSD_CONV_DIM), CONV_WIDTH ** -0.5)
    ssd_conv_b = nrm(ks[16], (DEPTH_2, SSD_CONV_DIM), 0.01)
    dt0 = jnp.exp(jax.random.uniform(ks[17], (DEPTH_2, SSD_HEADS), f32, math.log(1e-3), math.log(1e-1)))
    ssd_dt_bias = dt0 + jnp.log(-jnp.expm1(-dt0))
    ssd_a_log = jnp.log(jax.random.uniform(ks[18], (DEPTH_2, SSD_HEADS), f32, 1.0, 16.0))
    ssd_d = 1.0 + nrm(ks[19], (DEPTH_2, SSD_HEADS), 0.01)
    ssd_norm_w = 1.0 + nrm(ks[20], (DEPTH_2, SSD_WIDTH), 0.01)
    w_out = nrm(ks[21], (DEPTH_2, D_INNER, D_MODEL), D_INNER ** -0.5)
    final_norm_w = 1.0 + nrm(ks[22], (D_MODEL,), 0.01)
    return {"x": x, "c": c, "norm_w": norm_w, "w_ada": w_ada, "b_ada": b_ada,
            "w_in": w_in, "lru_conv_w": lru_conv_w, "lru_conv_b": lru_conv_b,
            "lru_wa": lru_wa, "lru_ba": lru_ba, "lru_wx": lru_wx, "lru_bx": lru_bx,
            "lru_lambda": lru_lambda, "hg_lb_logits": hg_lb_logits, "hg_norm_w": hg_norm_w,
            "ssd_conv_w": ssd_conv_w, "ssd_conv_b": ssd_conv_b, "ssd_dt_bias": ssd_dt_bias,
            "ssd_a_log": ssd_a_log, "ssd_d": ssd_d, "ssd_norm_w": ssd_norm_w,
            "w_out": w_out, "final_norm_w": final_norm_w}

def second_block(x, c, norm_w, w_ada, b_ada, w_in, lru_conv_w, lru_conv_b, lru_wa, lru_ba,
              lru_wx, lru_bx, lru_lambda, hg_lb_logits, hg_norm_w, ssd_conv_w, ssd_conv_b,
              ssd_dt_bias, ssd_a_log, ssd_d, ssd_norm_w, w_out, final_norm_w):
    B, S, _ = x.shape
    split_points = _split_points()
    cond = jax.nn.silu(c)
    p = jax.nn.softmax(hg_lb_logits.astype(jnp.float32), axis=0)
    lower_bounds = jnp.cumsum(p, axis=0) - p[0]

    for l in range(DEPTH_2):
        mod = cond @ w_ada[l] + b_ada[l]
        shift, scale, gate = jnp.split(mod, 3, axis=-1)
        h = rmsnorm(x, norm_w[l]) * (1.0 + scale[:, None]) + shift[:, None]
        u = h @ w_in[l]
        a_x, a_g, hg_q, hg_f, hg_i, hg_g, ssd_z, ssd_xbc, ssd_dt = jnp.split(u, split_points, axis=-1)

        xa = causal_conv(a_x, lru_conv_w[l], lru_conv_b[l])
        ya = rg_lru(xa, lru_wa[l], lru_ba[l], lru_wx[l], lru_bx[l], lru_lambda[l]) * jax.nn.silu(a_g)

        lb = lower_bounds[l]
        hf = hg_f.astype(jnp.float32)
        f = lb + (1.0 - lb) * jax.nn.sigmoid(hf)
        log_f = jnp.log(f)
        k_in = (1.0 - lb) * jax.nn.sigmoid(-hf)
        q_h = jax.nn.silu(hg_q).reshape(B, S, HG_HEADS, HG_HEAD_DIM)
        o_b = hgrn2_chunked(q_h, k_in.reshape(B, S, HG_HEADS, HG_HEAD_DIM),
                            hg_i.reshape(B, S, HG_HEADS, HG_HEAD_DIM),
                            log_f.reshape(B, S, HG_HEADS, HG_HEAD_DIM))
        yb = rmsnorm(o_b.reshape(B, S, HG_WIDTH), hg_norm_w[l]) * jax.nn.silu(hg_g)

        xbc = jax.nn.silu(causal_conv(ssd_xbc, ssd_conv_w[l], ssd_conv_b[l]))
        xs, Bm, Cm = jnp.split(xbc, [SSD_WIDTH, SSD_WIDTH + SSD_GROUPS * SSD_STATE], axis=-1)
        dt = jax.nn.softplus(ssd_dt + ssd_dt_bias[l])
        A = -jnp.exp(ssd_a_log[l])
        xs_h = xs.reshape(B, S, SSD_HEADS, SSD_HEAD_DIM)
        yc = ssd_chunked(xs_h, dt, A, Bm.reshape(B, S, SSD_GROUPS, SSD_STATE),
                         Cm.reshape(B, S, SSD_GROUPS, SSD_STATE))
        yc = (yc + ssd_d[l][:, None] * xs_h).reshape(B, S, SSD_WIDTH) * jax.nn.silu(ssd_z)
        yc = rmsnorm(yc.reshape(B, S, SSD_GROUPS, SSD_WIDTH // SSD_GROUPS),
                     ssd_norm_w[l].reshape(SSD_GROUPS, SSD_WIDTH // SSD_GROUPS)).reshape(B, S, SSD_WIDTH)

        y = jnp.concatenate([ya, yb, yc], axis=-1) @ w_out[l]
        x = x + gate[:, None] * y

    return rmsnorm(x, final_norm_w)


_first_inputs = second_inputs


def second_inputs(seed=0):
    import zlib

    import numpy as np

    out = dict(_first_inputs(seed))
    spreads = {}
    factors = {'norm_w': 8.0,
     'b_ada': 4.32,
     'lru_conv_b': 8.0,
     'lru_ba': 8.0,
     'lru_bx': 8.0,
     'hg_norm_w': 8.0,
     'ssd_conv_b': 8.0,
     'ssd_d': 8.0,
     'ssd_norm_w': 8.0,
     'final_norm_w': 5.651}
    for name, (base, spread) in spreads.items():
        noise = np.random.default_rng([zlib.crc32(name.encode()), seed]).standard_normal(out[name].shape)
        drawn = base * np.exp(spread * noise) if base else spread * noise
        out[name] = __import__('jax').numpy.asarray(drawn.astype(out[name].dtype))
    for name, factor in factors.items():
        out[name] = (out[name] * factor).astype(out[name].dtype)
    return out


_narrow_inputs = second_inputs


def second_inputs(seed=0):

    out = dict(_narrow_inputs(seed))
    wider = {'norm_w': 4.05,
     'lru_ba': 12.0,
     'lru_bx': 10.62,
     'hg_norm_w': 9.96,
     'ssd_conv_b': 12.0,
     'ssd_d': 12.0,
     'ssd_norm_w': 12.0,
     'final_norm_w': 6.28}
    for name, times in wider.items():
        mean = out[name].mean()
        out[name] = (mean + times * (out[name] - mean)).astype(out[name].dtype)
    return out


def setup_inputs(seed=0):
    out = dict(first_inputs(seed))
    for name, value in second_inputs(seed + 1).items():
        if name != "x":
            out[name + "_2"] = value
    return out


def reference(
    x, c, ctx, c_ctx, w_ada, b_ada, norm_g, w_in, attn_sink, conv_w, conv_b, conv_ln_g,
    conv_ln_b, w_four, b_four, w_out, final_g, c_2, norm_w_2, w_ada_2, b_ada_2, w_in_2,
    lru_conv_w_2, lru_conv_b_2, lru_wa_2, lru_ba_2, lru_wx_2, lru_bx_2, lru_lambda_2,
    hg_lb_logits_2, hg_norm_w_2, ssd_conv_w_2, ssd_conv_b_2, ssd_dt_bias_2, ssd_a_log_2,
    ssd_d_2, ssd_norm_w_2, w_out_2, final_norm_w_2,
):
    x = first_block(
        x, c, ctx, c_ctx, w_ada, b_ada, norm_g, w_in, attn_sink, conv_w, conv_b, conv_ln_g,
        conv_ln_b, w_four, b_four, w_out, final_g,
    )
    return second_block(
        x, c_2, norm_w_2, w_ada_2, b_ada_2, w_in_2, lru_conv_w_2, lru_conv_b_2, lru_wa_2,
        lru_ba_2, lru_wx_2, lru_bx_2, lru_lambda_2, hg_lb_logits_2, hg_norm_w_2, ssd_conv_w_2,
        ssd_conv_b_2, ssd_dt_bias_2, ssd_a_log_2, ssd_d_2, ssd_norm_w_2, w_out_2,
        final_norm_w_2,
    )


_drawn_inputs = setup_inputs


def setup_inputs(seed=0):
    import zlib

    import numpy as np

    out = dict(_drawn_inputs(seed))
    spreads = {}
    factors = {'b_ada': 2.789,
     'norm_g': 8.0,
     'attn_sink': 8.0,
     'conv_b': 8.0,
     'conv_ln_g': 8.0,
     'conv_ln_b': 8.0,
     'b_four': 8.0,
     'ssd_conv_b_2': 2.704,
     'ssd_d_2': 8.0,
     'ssd_norm_w_2': 2.96}
    for name, (base, spread) in spreads.items():
        noise = np.random.default_rng([zlib.crc32(name.encode()), seed]).standard_normal(out[name].shape)
        drawn = base * np.exp(spread * noise) if base else spread * noise
        out[name] = __import__('jax').numpy.asarray(drawn.astype(out[name].dtype))
    for name, factor in factors.items():
        out[name] = (out[name] * factor).astype(out[name].dtype)
    return out
```

```python
from contextlib import ExitStack

import numpy as np

import concourse.bass as bass
import concourse.mybir as mybir

F32 = mybir.dt.float32
BF16 = mybir.dt.bfloat16
I32 = mybir.dt.int32
ALU = mybir.AluOpType
ACT = mybir.ActivationFunctionType
AX = mybir.AxisListType
ds = bass.ds

P = 128
D = 1024
KT = D // P
SEQ = 2048
CTX = 256
DEPTH = 2
CH = 512
EPS = 1e-6
NEG = -1e30

HD = 64
NH = 8
ATT = NH * HD
NKV = 2
GQ = NH // NKV
SCALE = HD ** -0.5
CONV_K = 31
FH = 64

LW = 512
HW = 512
HGH = HW // P
SW = 1024
SH = 16
SG = 2
SXBC = SW + 2 * SG * P
TAPS = 4
LRU_C = 8.0


def wait(eng, sem, value):
    if not (isinstance(value, int) and value <= 0):
        eng.wait_ge(sem, value)


def wait_apart(eng, sem, value, passed):
    wait(eng, sem, value)
    eng.sem_inc(passed, 1)


def steps(eng, n, body):
    first = min(n, 2)
    for b in range(first):
        body(b, b % 2)
    pairs = n // 2
    if pairs > 2:
        with eng.Fori(1, pairs - 1, 1) as i:
            for q in range(2):
                body(i * 2 + q, q)
    for b in range(max(first, n - 2), n):
        body(b, b % 2)


class Stage:

    def __init__(self, nc, name):
        self.nc, self.name, self.ctx, self.taken = nc, name, ExitStack(), []

    def __enter__(self):
        self.ctx.__enter__()
        return self

    def __exit__(self, *a):
        self.ctx.__exit__(*a)
        if a[0] is None:
            self.nc.clear_and_free_semaphores(self.taken)
            self.nc.all_engine_barrier()

    def sb(self, name, shape, dt=F32):
        return self.ctx.enter_context(self.nc.sbuf_tensor(f"{self.name}_{name}", shape, dt))

    def ps(self, name, shape, dt=F32):
        return self.ctx.enter_context(self.nc.psum_tensor(f"{self.name}_{name}", shape, dt))

    def sem(self, name):
        self.taken.append(self.nc.alloc_semaphore(f"{self.name}_{name}"))
        return self.taken[-1]

    def sems(self, name, n):
        return [self.sem(f"{name}{i}") for i in range(n)]

    def block(self):
        return self.ctx.enter_context(self.nc.Block())


def bcast(ap, n, axis=1):
    a = ap.unsqueeze(axis)
    shape = list(a.shape)
    shape[axis] = n
    return a.broadcast_to(shape)



def modulation(nc, name, cond, w, b, g, mod, gain, ncond):
    NJ, NB = 3 * KT, 4
    with Stage(nc, name) as s:
        c = s.sb("c", [P, KT, ncond])
        sc = s.sb("sc", [P, KT, ncond])
        bb, gg = s.sb("b", [P, NJ]), s.sb("g", [P, KT])
        wt = s.sb("w", [P, NB, KT, P])
        ps = s.ps("ps", [P, NJ, ncond])
        c_in, silu_done, mm_done = s.sem("c_in"), s.sem("silu_done"), s.sem("mm_done")
        done = s.sem("done")
        w_in = s.sems("w_in", NB)
        block = s.block()

        @block.sync
        def _(sp):
            sp.dma_start(c[:], cond).then_inc(c_in, 16)
            sp.dma_start(bb[:], b).then_inc(c_in, 16)
            sp.dma_start(gg[:], g).then_inc(c_in, 16)
            for q in range(NB):
                sp.dma_start(wt[:, q], w[q]).then_inc(w_in[q], 16)
            with sp.Fori(1, NJ // NB, 1) as i:
                for q in range(NB):
                    sp.wait_ge(mm_done, i * NB + (q + 1 - NB))
                    sp.dma_start(wt[:, q], w[i * NB + q]).then_inc(w_in[q], 16)

        @block.scalar
        def _(act):
            act.wait_ge(c_in, 48)
            nc.scalar.activation(sc[:], c[:], ACT.Silu).then_inc(silu_done, 1)

        @block.tensor
        def _(pe):
            pe.wait_ge(silu_done, 1)
            with pe.Fori(0, NJ // NB, 1) as i:
                for q in range(NB):
                    pe.wait_ge(w_in[q], i * 16 + 16)
                    for k in range(KT):
                        mm = nc.tensor.matmul(ps[:, ds(i * NB + q, 1), :].rearrange("p a n -> p (a n)"),
                                              wt[:, q, k], sc[:, k], start=(k == 0), stop=(k == KT - 1))
                    mm.then_inc(mm_done, 1)

        @block.vector
        def _(dve):
            dve.wait_ge(mm_done, NJ)
            dve.wait_ge(c_in, 48)
            for n in range(ncond):
                last = nc.vector.tensor_tensor(mod[:, :, n], ps[:, :, n], bb[:], ALU.add)
            last.then_inc(done, 1)
            dve.wait_ge(done, 1)
            for n in range(ncond):
                nc.vector.scalar_tensor_tensor(gain[:, :, n], mod[:, KT:2 * KT, n], 1.0, gg[:], ALU.add, ALU.mult).then_inc(done, 1)



def norm(nc, name, xT, N, gain, out_sb=None, out_dram=None, shift=None, gate_d=None, K=KT):
    W = min(CH, N)
    NCH = N // W
    with Stage(nc, name) as s:
        x = s.sb("x", [P, 2, K, W])
        sq = s.sb("sq", [P, K, W])
        ones = s.sb("ones", [P, P])
        eps = s.sb("eps", [P, 1])
        root = s.sb("root", [P, 2, W])
        rstd = s.sb("rstd", [P, 2, W])
        o = None if out_dram is None else s.sb("o", [P, 2, K, W])
        gb = None if gate_d is None else s.sb("g", [P, 2, K, W])
        ps = s.ps("ps", [P, 2, CH])
        x_in, g_in, o_out = s.sems("x_in", 2), s.sems("g_in", 2), s.sems("o_out", 2)
        const, sq_done, sum_done, root_done = s.sem("const"), s.sem("sq_done"), s.sem("sum_done"), s.sem("root_done")
        rstd_done, scaled, done = s.sem("rstd_done"), s.sem("scaled"), s.sem("done")
        block = s.block()

        def dst(c, k):
            return out_sb[:, k, c * W:(c + 1) * W] if o is None else o[:, c % 2, k]

        def store(sp, c):
            sp.wait_ge(done, c + 1)
            sp.dma_start(out_dram[:, :, c * W:(c + 1) * W].rearrange("k p t -> p k t"), o[:, c % 2]).then_inc(o_out[c % 2], 16)

        @block.sync
        def _(sp):
            for c in range(NCH):
                if c >= 2:
                    sp.wait_ge(scaled, c - 1)
                sp.dma_start(x[:, c % 2], xT[:, :, c * W:(c + 1) * W].rearrange("k p t -> p k t")).then_inc(x_in[c % 2], 16)
                if gb is not None:
                    if c >= 2:
                        sp.wait_ge(done, c - 1)
                    sp.dma_start(gb[:, c % 2], gate_d[:, :, c * W:(c + 1) * W].rearrange("k p t -> p k t")).then_inc(g_in[c % 2], 16)
                if o is not None and c >= 1:
                    store(sp, c - 1)
            if o is not None:
                store(sp, NCH - 1)
                for q in range(2):
                    n = (NCH + 1 - q) // 2
                    if n:
                        sp.wait_ge(o_out[q], 16 * n)

        @block.tensor
        def _(pe):
            pe.wait_ge(const, 2)
            for c in range(NCH):
                pe.wait_ge(sq_done, c + 1)
                if c >= 2:
                    pe.wait_ge(root_done, c - 1)
                for k in range(K):
                    mm = nc.tensor.matmul(ps[:, c % 2, :W], ones[:], sq[:, k], start=(k == 0), stop=(k == K - 1))
                mm.then_inc(sum_done, 1)

        @block.scalar
        def _(act):
            act.wait_ge(const, 2)

            def finish(c):
                act.wait_ge(scaled, c + 1)
                for k in range(K):
                    last = nc.scalar.activation(dst(c, k), dst(c, k), ACT.Identity, bias=shift[:, k:k + 1])
                last.then_inc(done, 1)

            for c in range(NCH):
                act.wait_ge(x_in[c % 2], 16 * (c // 2 + 1))
                if c >= 1:
                    act.wait_ge(sum_done, c)
                nc.scalar.activation(sq[:], x[:, c % 2], ACT.Square).then_inc(sq_done, 1)
                act.wait_ge(sum_done, c + 1)
                if c >= 2:
                    act.wait_ge(rstd_done, c - 1)
                nc.scalar.activation(root[:, c % 2], ps[:, c % 2, :W], ACT.Sqrt, bias=eps[:, 0:1]).then_inc(root_done, 1)
                if shift is not None and c >= 1:
                    finish(c - 1)
            if shift is not None:
                finish(NCH - 1)

        @block.vector
        def _(dve):
            nc.vector.memset(ones[:], 1.0 / (K * P)).then_inc(const, 1)
            nc.vector.memset(eps[:], EPS).then_inc(const, 1)
            for c in range(NCH):
                dve.wait_ge(root_done, c + 1)
                nc.vector.reciprocal(rstd[:, c % 2], root[:, c % 2]).then_inc(rstd_done, 1)
                dve.wait_ge(rstd_done, c + 1)
                if o is not None and c >= 2:
                    dve.wait_ge(o_out[c % 2], 16 * (c // 2))
                for k in range(K):
                    last = nc.vector.scalar_tensor_tensor(dst(c, k), x[:, c % 2, k], gain[:, k:k + 1], rstd[:, c % 2],
                                                          ALU.mult, ALU.mult)
                    if k == K - 1:
                        last.then_inc(scaled, 1)
                if gb is not None:
                    dve.wait_ge(scaled, c + 1)
                    dve.wait_ge(g_in[c % 2], 16 * (c // 2 + 1))
                    nc.vector.tensor_tensor(o[:, c % 2], o[:, c % 2], gb[:, c % 2], ALU.mult).then_inc(done, 1)
                elif shift is None:
                    dve.wait_ge(scaled, c + 1)
                    dve.engine_nop().then_inc(done, 1)



def project(nc, name, h, N, w, runs, tables=None):
    W = min(CH, N)
    NCH = N // W
    rope = any(r[0] == "rope" for r in runs)
    total = sum(r[1] for r in runs)
    with Stage(nc, name) as s:
        wt = s.sb("w", [P, 2, KT, P])
        ob = s.sb("ob", [P, 2, N])
        if rope:
            cs = s.sb("cs", [P, 2, N])
            raw = s.sb("raw", [P, 2, N])
            rot = s.sb("rot", [P, N])
            straight = s.sb("straight", [P, N])
        ps = s.ps("ps", [P, 2, SEQ])
        w_in, stored = s.sems("w_in", 2), s.sems("stored", 2)
        tab_in, mm_done, emptied, roped = s.sem("tab_in"), s.sem("mm_done"), s.sem("emptied"), s.sem("roped")
        swapped, turned = s.sem("swapped"), s.sem("turned")
        block = s.block()

        def tiles(eng, body, only=None):
            at, nrope = 0, 0
            for kind, count, out, scale in runs:
                pairs = count // 2
                if only is None or kind == only:
                    start = 0
                    if at == 0:
                        for q in range(min(2, count)):
                            body(kind, 0, q, q, out, True, q, scale)
                        start = 1
                    if pairs > start:
                        with eng.Fori(start, pairs, 1) as i:
                            for q in range(2):
                                body(kind, i + at, q, i * 2 + q, out, False, i * 2 + q, scale)
                    if count % 2 and count > 1:
                        body(kind, at + pairs, 0, count - 1, out, False, nrope + count - 1, scale)
                    elif count == 1 and at:
                        body(kind, at, 0, 0, out, False, nrope, scale)
                at += pairs
                nrope += count if kind == "rope" else 0

        @block.sync
        def _(sp):
            if rope:
                sp.dma_start(cs[:], tables.rearrange("a p t -> p a t")).then_inc(tab_in, 16)

            def load(kind, it, q, n, out, first, nth, scale):
                if not first:
                    sp.wait_ge(mm_done, it * 2 + (q - 1))
                sp.dma_start(wt[:, q], w[it * 2 + q]).then_inc(w_in[q], 16)
            tiles(sp, load)

        @block.tensor
        def _(pe):
            def products(kind, it, q, n, out, first, nth, scale):
                pe.wait_ge(w_in[q], it * 16 + 16)
                if not first:
                    pe.wait_ge(emptied, it * 2 + (q - 1))
                for c in range(NCH):
                    for k in range(KT):
                        mm = nc.tensor.matmul(ps[:, q, c * W:(c + 1) * W], wt[:, q, k], h[:, k, c * W:(c + 1) * W],
                                              start=(k == 0), stop=(k == KT - 1))
                mm.then_inc(mm_done, 1)
            tiles(pe, products)

        @block.scalar
        def _(act):
            def empty(kind, it, q, n, out, first, nth, scale):
                act.wait_ge(mm_done, it * 2 + (q + 1))
                if kind == "rope":
                    if not (isinstance(nth, int) and nth < 2):
                        act.wait_ge(roped, nth - 1)
                    nc.scalar.activation(raw[:, q], ps[:, q, :N], ACT.Copy, scale=scale).then_inc(emptied, 1)
                else:
                    if not first:
                        act.wait_ge(stored[q], it * 16)
                    nc.scalar.activation(ob[:, q], ps[:, q, :N], kind, scale=scale).then_inc(emptied, 1)
            tiles(act, empty)

        if rope:
            @block.vector
            def _(dve):
                swap = [(i + 16) % 32 for i in range(32)]
                dve.wait_ge(tab_in, 16)

                def turn(kind, it, q, n, out, first, nth, scale):
                    dve.wait_ge(emptied, it * 2 + (q + 1))
                    wait(dve, roped, nth)
                    nc.vector.stream_shuffle(rot[:], raw[:, q], swap).then_inc(swapped, 1)
                    nc.vector.tensor_tensor(straight[:], raw[:, q], cs[:, 0], ALU.mult).then_inc(turned, 1)
                    dve.wait_ge(swapped, nth + 1)
                    nc.vector.tensor_tensor(rot[:], rot[:], cs[:, 1], ALU.mult).then_inc(turned, 1)
                    dve.wait_ge(turned, nth * 2 + 2)
                    if not first:
                        dve.wait_ge(stored[q], it * 16)
                    nc.vector.tensor_tensor(ob[:, q], straight[:], rot[:], ALU.add).then_inc(roped, 1)
                tiles(dve, turn, only="rope")

        @block.gpsimd
        def _(pool):
            def store(kind, it, q, n, out, first, nth, scale):
                if kind == "rope":
                    pool.wait_ge(roped, nth + 1)
                else:
                    pool.wait_ge(emptied, it * 2 + (q + 1))
                pool.dma_start(out[n], ob[:, q]).then_inc(stored[q], 16)
            tiles(pool, store)
            for q in range(2):
                if (total + 1 - q) // 2:
                    pool.wait_ge(stored[q], 16 * ((total + 1 - q) // 2))


def project_tokens(nc, name, h, N, w, NW, outs):
    NT = N // P
    with Stage(nc, name) as s:
        wt = s.sb("w", [P, KT, NW])
        ob = s.sb("ob", [P, 4, NW])
        ps = s.ps("ps", [P, 4, CH])
        w_in, mm_done, emptied = s.sem("w_in"), s.sem("mm_done"), s.sem("emptied")
        stored = s.sems("stored", 4)
        block = s.block()

        @block.sync
        def _(sp):
            sp.dma_start(wt[:], w).then_inc(w_in, 16)
            for t in range(NT):
                sp.wait_ge(emptied, t + 1)
                for out, c0, n in outs:
                    sp.dma_start(out[t], ob[:, t % 4, c0:c0 + n]).then_inc(stored[t % 4], 16)
            for q in range(min(4, NT)):
                sp.wait_ge(stored[q], 16 * len(outs) * ((NT + 3 - q) // 4))

        @block.tensor
        def _(pe):
            pe.wait_ge(w_in, 16)
            for t in range(NT):
                if t >= 4:
                    pe.wait_ge(emptied, t - 3)
                for k in range(KT):
                    mm = nc.tensor.matmul(ps[:, t % 4, :NW], h[:, k, t * P:(t + 1) * P], wt[:, k],
                                          start=(k == 0), stop=(k == KT - 1))
                mm.then_inc(mm_done, 1)

        @block.scalar
        def _(act):
            for t in range(NT):
                act.wait_ge(mm_done, t + 1)
                if t >= 4:
                    act.wait_ge(stored[t % 4], 16 * len(outs) * (t // 4))
                nc.scalar.activation(ob[:, t % 4], ps[:, t % 4, :NW], ACT.Copy).then_inc(emptied, 1)



def attention(nc, name, N, q_d, kc_d, vc_d, sink_d, gate_d, out_d, k_d=None, v_d=None, mask_d=None):
    NB = N // P
    win = k_d is not None
    NW = 3 if win else 0
    NT = NW + 2
    NK = NT * P
    U = 2 * NT
    with Stage(nc, name) as s:
        qb, gb, ob = s.sb("q", [P, 2, 4, P]), s.sb("g", [P, 2, 4, P]), s.sb("o", [P, 2, 4, P])
        kc, vc = s.sb("kc", [P, CTX]), s.sb("vc", [P, 2, P])
        if win:
            kw, vw = s.sb("kw", [P, 2, 3 * P]), s.sb("vw", [P, 2, 3, P])
            idb, mk, mkf = s.sb("idb", [P, P], BF16), s.sb("mk", [P, 3, P], BF16), s.sb("mkf", [P, 3, P])
            masks_in = s.sem("masks_in")
        ident, ones, sink = s.sb("ident", [P, P]), s.sb("ones", [1, P]), s.sb("sink", [1, NH])
        prob = s.sb("prob", [P, 2, NH, NK + 1])
        pT = s.sb("pT", [P, 4, 4 * P])
        nmax, den, rden = s.sb("nmax", [P, 2, NH]), s.sb("den", [P, 2, NH]), s.sb("rden", [P, 2, NH])
        psS = s.ps("S", [P, 2, 2 * CH])
        psT = s.ps("T", [P, 2, CH])
        psO = s.ps("O", [P, 2, CH])
        const_in, const = s.sem("const_in"), s.sem("const")
        blk_in, stored = s.sems("blk_in", 2), s.sems("stored", 2)
        scored, maxed, expd, inverted, normed = (s.sem(x) for x in ("scored", "maxed", "expd", "inverted", "normed"))
        turned, movedD, movedA, summed, gated = (s.sem(x) for x in ("turned", "movedD", "movedA", "summed", "gated"))
        block = s.block()
        NIN = 4 if win else 2

        def shifted(eng, ahead, behind):
            ahead(0, 0)

            def body(b, q, last=False):
                if not last:
                    ahead(b + 1, 1 - q)
                behind(b, q)
            body(0, 0, NB == 1)
            body(1, 1, NB == 2)
            if NB > 4:
                with eng.Fori(1, NB // 2 - 1, 1) as i:
                    for q in range(2):
                        body(i * 2 + q, q)
            if NB > 2:
                body(NB - 2, 0)
                body(NB - 1, 1, True)

        @block.sync
        def _(sp):
            sp.dma_start(kc[:], kc_d).then_inc(const_in, 16)
            sp.dma_start(vc[:], vc_d.rearrange("t p d -> p t d")).then_inc(const_in, 16)
            sp.dma_start(sink[:], sink_d).then_inc(const_in, 16)
            if win:
                sp.dma_start(mkf[:], mask_d).then_inc(masks_in, 16)

            def load(b, q):
                wait(sp, gated, b - 1)
                at = ds(b * P, P)
                sp.dma_start(qb[:, q], q_d[:, :, at].rearrange("j p t -> p j t")).then_inc(blk_in[q], 16)
                sp.dma_start(gb[:, q], gate_d[:, :, at].rearrange("j p t -> p j t")).then_inc(blk_in[q], 16)
                if win:
                    sp.dma_start(kw[:, q], k_d[:, ds(b * P, 3 * P)]).then_inc(blk_in[q], 16)
                    sp.dma_start(vw[:, q], v_d[ds(b, 3)].rearrange("t p d -> p t d")).then_inc(blk_in[q], 16)
            steps(sp, NB, load)

        @block.gpsimd
        def _(pool):
            pool.memset(ident[:], 0.0).then_inc(const, 1)
            pool.wait_ge(const, 1)
            pool.affine_select(out=ident[:], in_=ident[:], compare_op=ALU.not_equal, fill=1.0, base=0,
                               pattern=[[-1, P]], channel_multiplier=1).then_inc(const, 1)
            pool.memset(ones[:], 1.0).then_inc(const, 1)
            if win:
                pool.wait_ge(const, 3)
                pool.tensor_copy(idb[:], ident[:]).then_inc(const, 1)
                pool.wait_ge(masks_in, 16)
                pool.tensor_copy(mk[:], mkf[:]).then_inc(const, 1)

            def store(b, q):
                pool.wait_ge(gated, b + 1)
                pool.dma_start(out_d[:, :, ds(b * P, P)].rearrange("j p t -> p j t"), ob[:, q]).then_inc(stored[q], 16)
            steps(pool, NB, store)
            for q in range(2):
                pool.wait_ge(stored[q], 16 * (NB // 2))

        @block.tensor
        def _(pe):
            pe.wait_ge(const, 5 if win else 3)
            pe.wait_ge(const_in, 48)

            def scores(b, q):
                pe.wait_ge(blk_in[q], (b // 2 if isinstance(b, int) else (b - q) // 2) * 16 * NIN + 16 * NIN)
                for hh in range(NH):
                    j, g = hh // 2, hh % 2
                    rows = slice(g * HD, g * HD + HD)
                    S = psS[:, hh % 2]
                    wait(pe, expd, b * NH + (hh - 1))
                    lhs = qb[rows, q, j]
                    c = 0
                    nc.tensor.matmul(S[:, 0:CTX], lhs, kc[rows, :], start=True, stop=True)
                    c = CTX
                    if win:
                        nc.tensor.matmul(S[:, c:c + 2 * P], lhs, kw[rows, q, 0:2 * P], start=True, stop=False)
                        nc.tensor.matmul(S[:, c:c + P], idb[:], mk[:, 2 if isinstance(b, int) and b == 0 else 0], start=False, stop=True)
                        c = CH
                        nc.tensor.matmul(S[:, c:c + P], lhs, kw[rows, q, 2 * P:3 * P], start=True, stop=False)
                        nc.tensor.matmul(S[:, c:c + P], idb[:], mk[:, 2 if isinstance(b, int) and b == NB - 1 else 1], start=False, stop=True)
                        c = CH + P
                    h = g * GQ + j
                    nc.tensor.matmul(S[:, c:c + 1], ones[:], sink[:, h:h + 1], start=True, stop=True).then_inc(scored, 1)

            def values(b, q):
                pe.wait_ge(normed, b * NH + NH)
                for u in range(U + 1):
                    if u < U:
                        kt, g = u // 2, u % 2
                        moved = (movedD, movedA)[g]
                        wait(pe, moved, b * NT + kt)
                        for j in range(4):
                            tr = nc.tensor.transpose(psT[:, g, j * P:(j + 1) * P], prob[:, q, 2 * j + g, kt * P:(kt + 1) * P], ident[:])
                        tr.then_inc(turned, 1)
                    if u == 1:
                        wait(pe, gated, b - 1)
                    if u >= 1:
                        kt, g = (u - 1) // 2, (u - 1) % 2
                        cols = slice(g * HD, g * HD + HD)
                        val = vc[:, kt, cols] if kt < 2 else vw[:, q, kt - 2, cols]
                        pe.wait_ge((movedD, movedA)[g], b * NT + (kt + 1))
                        nc.tensor.matmul(psO[cols, q], val, pT[:, (U * q + u - 1) % 4], start=(kt == 0),
                                         stop=(kt == NT - 1)).then_inc(summed, 1)
            shifted(pe, scores, values)

        def move(eng, b, q, u, op, moved):
            eng.wait_ge(turned, b * U + (u + 1))
            wait(eng, summed, b * U + (u - 3))
            op(pT[:, (U * q + u) % 4], psT[:, u % 2]).then_inc(moved, 1)

        @block.scalar
        def _(act):
            def exps(b, q):
                wait(act, turned, (b - 1) * U)
                for hh in range(NH):
                    act.wait_ge(maxed, b * NH + (hh + 1))
                    nc.scalar.activation(prob[:, q, hh], psS[:, hh % 2, 0:NK + 1], ACT.Exp, bias=nmax[:, q, hh:hh + 1],
                                         accum_out=den[:, q, hh:hh + 1]).then_inc(expd, 1)

            def moves(b, q):
                for u in range(1, U, 2):
                    move(act, b, q, u, nc.scalar.copy, movedA)
            shifted(act, exps, moves)

        @block.vector
        def _(dve):
            def maxes(b, q, hh):
                dve.wait_ge(scored, b * NH + (hh + 1))
                nc.vector.tensor_reduce(nmax[:, q, hh:hh + 1], psS[:, hh % 2, 0:NK + 1], AX.X, ALU.max,
                                        negate=True).then_inc(maxed, 1)

            def invert(b, q):
                dve.wait_ge(expd, b * NH + NH)
                nc.vector.reciprocal(rden[:, q], den[:, q]).then_inc(inverted, 1)
                dve.wait_ge(inverted, b + 1)

            def norms(b, q, hh):
                nc.vector.tensor_scalar(prob[:, q, hh, 0:NK], prob[:, q, hh, 0:NK], rden[:, q, hh:hh + 1], None,
                                        ALU.mult).then_inc(normed, 1)

            def rest(b, q):
                for u in range(0, U, 2):
                    move(dve, b, q, u, nc.vector.tensor_copy, movedD)
                dve.wait_ge(summed, b * U + U)
                wait(dve, stored[q], b // 2 * 16 if isinstance(b, int) else (b - q) // 2 * 16)
                nc.vector.tensor_tensor(ob[:, q].rearrange("p j t -> p (j t)"), psO[:, q],
                                        gb[:, q].rearrange("p j t -> p (j t)"), ALU.mult).then_inc(gated, 1)

            def body(b, q, last=False):
                invert(b, q)
                for hh in range(NH):
                    if not last:
                        maxes(b + 1, 1 - q, hh)
                    norms(b, q, hh)
                rest(b, q)
            for hh in range(NH):
                maxes(0, 0, hh)
            body(0, 0)
            body(1, 1, NB == 2)
            if NB > 4:
                with dve.Fori(1, NB // 2 - 1, 1) as i:
                    for q in range(2):
                        body(i * 2 + q, q)
            if NB > 2:
                body(NB - 2, 0)
                body(NB - 1, 1, True)



def fourier(nc, name, N, u_d, tab_d, headtab_d, wf_d, bf_d, gate_d, out_d):
    R = N // P
    W = min(CH, N)
    NCH = N // W
    C2 = 2 * P
    half = R // 2
    with Stage(nc, name) as s:
        u = s.sb("u", [P, R, C2])
        gr = s.sb("gr", [P, half + 1, C2])
        gi = s.sb("gi", [P, half + 1, C2]) if R > 2 else None
        tab = s.sb("tab", [P, 2, 2, 2 * P])
        ht, wf, bf = s.sb("ht", [P, 2, P]), s.sb("wf", [P, 2, C2]), s.sb("bf", [P, 2])
        wcs = s.sb("wcs", [P, 2, 2, C2])
        ab = s.sb("ab", [P, 2, 2, N])
        if R > 2:
            t8 = s.sb("t8", [P, 16, C2])
            t4 = s.sb("t4", [P, 8, C2])
            pq = s.sb("pq", [P, 6, C2])
        gate, ob = s.sb("gate", [P, 2, N]), s.sb("ob", [P, 2, 2, CH])
        psA = s.ps("A", [P, 4, CH])
        psW = s.ps("W", [P, 4, CH])
        u_in, const_in, gate_in = s.sem("u_in"), s.sem("const_in"), s.sem("gate_in")
        tab_in, stored = s.sems("tab_in", 2), s.sems("stored", 2)
        chain, bins, prod, wdone, wmoved = (s.sem(x) for x in ("chain", "bins", "prod", "wdone", "wmoved"))
        moved, mixed, gated = s.sem("moved"), s.sem("mixed"), s.sem("gated")
        block = s.block()
        NORM = 1.0 / np.sqrt(N * FH)

        @block.sync
        def _(sp):
            sp.dma_start(u[:], u_d.rearrange("r p c -> p r c")).then_inc(u_in, 16)
            sp.dma_start(ht[:], headtab_d).then_inc(const_in, 16)
            sp.dma_start(wf[:], wf_d.rearrange("(a p) n -> p a n", p=P)).then_inc(const_in, 16)
            sp.dma_start(bf[:], bf_d).then_inc(const_in, 16)

            def load(b, q):
                wait(sp, prod, b - 1)
                sp.dma_start(tab[:, q], tab_d[b].rearrange("p (a c) -> p a c", a=2)).then_inc(tab_in[q], 16)
            for b in range(2):
                load(b, b)
            sp.dma_start(gate[:], gate_d.rearrange("a p t -> p a t")).then_inc(gate_in, 16)
            for b in range(2, R):
                load(b, b % 2)
            for c in range(NCH):
                for m in range(2):
                    n = 2 * c + m
                    sp.wait_ge(gated, n + 1)
                    sp.dma_start(out_d[m, :, c * W:(c + 1) * W], ob[:, c % 2, m, :W]).then_inc(stored[c % 2], 16)
            for q in range(min(2, NCH)):
                sp.wait_ge(stored[q], 32 * ((NCH + 1 - q) // 2))

        @block.vector
        def _(dve):
            n = [0]

            def step(ins):
                n[0] += 1
                ins.then_inc(chain, 1)

            def settle():
                dve.wait_ge(chain, n[0])

            dve.wait_ge(u_in, 16)
            tt, stt, ts = nc.vector.tensor_tensor, nc.vector.scalar_tensor_tensor, nc.vector.tensor_scalar
            add, sub, mul = ALU.add, ALU.subtract, ALU.mult
            if R == 2:
                tt(gr[:, 0], u[:, 0], u[:, 1], add).then_inc(bins, 1)
                tt(gr[:, 1], u[:, 0], u[:, 1], sub).then_inc(bins, 1)
            else:
                step(tt(t8[:, 0:8], u[:, 0:8], u[:, 8:16], add))
                step(tt(t8[:, 8:16], u[:, 0:8], u[:, 8:16], sub))
                settle()
                step(tt(t4[:, 0:4], t8[:, 0:4], t8[:, 4:8], add))
                step(tt(t4[:, 4:8], t8[:, 0:4], t8[:, 4:8], sub))
                for m in (1, 2, 3):
                    step(tt(pq[:, m - 1], t8[:, 8 + m], t8[:, 16 - m], sub))
                    step(tt(pq[:, m + 2], t8[:, 8 + m], t8[:, 16 - m], add))
                settle()
                c, d = (lambda m: t4[:, m]), (lambda m: t4[:, 4 + m])
                step(tt(t8[:, 0], c(0), c(2), add))
                step(tt(t8[:, 1], c(1), c(3), add))
                step(tt(gr[:, 4], c(0), c(2), sub))
                step(tt(gi[:, 4], c(3), c(1), sub))
                step(tt(t8[:, 2], d(1), d(3), sub))
                step(tt(t8[:, 3], d(1), d(3), add))
                settle()
                r = float(np.sqrt(0.5))
                step(tt(gr[:, 0], t8[:, 0], t8[:, 1], add))
                step(tt(gr[:, 8], t8[:, 0], t8[:, 1], sub))
                step(stt(gr[:, 2], t8[:, 2], r, d(0), mul, add))
                step(stt(gr[:, 6], t8[:, 2], -r, d(0), mul, add))
                step(stt(gi[:, 2], t8[:, 3], -r, d(2), mul, sub))
                step(stt(gi[:, 6], t8[:, 3], -r, d(2), mul, add))
                for m in (1, 2, 3):
                    for k in (1, 3, 5, 7):
                        co, si = float(np.cos(np.pi * m * k / 8)), float(np.sin(np.pi * m * k / 8))
                        step(stt(gr[:, k], pq[:, m - 1], co, t8[:, 8] if m == 1 else gr[:, k], mul, add))
                        s4 = int(round(np.sin(np.pi * k / 2)))
                        if m == 1:
                            step(stt(gi[:, k], pq[:, m + 2], -si, t8[:, 12], mul, sub if s4 > 0 else add))
                        else:
                            step(stt(gi[:, k], pq[:, m + 2], -si, gi[:, k], mul, add))
                    settle()
                dve.engine_nop().then_inc(bins, 2)
            for b in range(1, R, 2):
                dve.wait_ge(prod, b + 1)
                for ct in range(2):
                    last = nc.vector.tensor_copy(ab[:, ct].rearrange("p a (k r) -> p a k r", r=R)[:, :, :, b],
                                                 psA[:, 2 + ct, 0:2 * P].rearrange("p (a k) -> p a k", a=2))
                last.then_inc(moved, 1)
            dve.wait_ge(gate_in, 16)
            dve.wait_ge(const_in, 48)
            for c in range(NCH):
                for m in range(2):
                    k = 2 * c + m
                    dve.wait_ge(mixed, k + 1)
                    if c >= 2:
                        dve.wait_ge(stored[c % 2], 32 * (c // 2))
                    stt(ob[:, c % 2, m, :W], psW[:, k % 4, :W], bf[:, m:m + 1], gate[:, m, c * W:(c + 1) * W], add, mul).then_inc(gated, 1)

        @block.scalar
        def _(act):
            act.wait_ge(wdone, 1)
            for cs in range(2):
                for ct in range(2):
                    last = nc.scalar.activation(wcs[:, cs, ct], psW[:, 2 * cs + ct, 0:C2], ACT.Copy,
                                                scale=float(NORM if cs == 0 else -NORM))
            last.then_inc(wmoved, 1)
            for b in range(0, R, 2):
                act.wait_ge(prod, b + 1)
                for ct in range(2):
                    last = nc.scalar.copy(ab[:, ct].rearrange("p a (k r) -> p a k r", r=R)[:, :, :, b],
                                          psA[:, ct, 0:2 * P].rearrange("p (a k) -> p a k", a=2))
                last.then_inc(wmoved, 1)

        @block.tensor
        def _(pe):
            pe.wait_ge(const_in, 48)
            for cs in range(2):
                for ct in range(2):
                    mm = nc.tensor.matmul(psW[:, 2 * cs + ct, 0:C2], ht[:, cs], wf[:, ct], start=True, stop=True)
            mm.then_inc(wdone, 1)
            pe.wait_ge(bins, 2)
            for b in range(R):
                k, real = min(b, R - b), b in (0, half)
                pe.wait_ge(tab_in[b % 2], 16 * (b // 2 + 1))
                if b >= 2:
                    pe.wait_ge(wmoved if b % 2 == 0 else moved, b // 2 + (1 if b % 2 == 0 else 0))
                for ct in range(2):
                    o = psA[:, 2 * (b % 2) + ct, 0:2 * P]
                    mm = nc.tensor.matmul(o, gr[:, k, ct * P:(ct + 1) * P], tab[:, b % 2, 0], start=True, stop=real)
                    if not real:
                        mm = nc.tensor.matmul(o, gi[:, k, ct * P:(ct + 1) * P], tab[:, b % 2, 1], start=False, stop=True)
                mm.then_inc(prod, 1)
            pe.wait_ge(wmoved, 1 + (R + 1) // 2)
            pe.wait_ge(moved, R // 2)
            for c in range(NCH):
                for m in range(2):
                    k = 2 * c + m
                    if k >= 4:
                        pe.wait_ge(gated, k - 3)
                    for i in range(4):
                        ct, cs = i // 2, i % 2
                        mm = nc.tensor.matmul(psW[:, k % 4, :W], wcs[:, cs, ct, m * P:(m + 1) * P], ab[:, ct, cs, c * W:(c + 1) * W],
                                              start=(i == 0), stop=(i == 3))
                    mm.then_inc(mixed, 1)



def conformer(nc, name, N, a_d, sig_d, cw_d, cb_d, lg_d, lb_d, gate_d, out_d):
    H = CONV_K // 2
    W = min(CH, N)
    NCH = N // W
    with Stage(nc, name) as s:
        u = s.sb("u", [P, 2, N + 2 * H])
        sg = s.sb("sg", [P, 2, N])
        y = s.sb("y", [P, 2, N])
        sq, xh = s.sb("sq", [P, 2, CH]), s.sb("xh", [P, 2, CH])
        cw, par = s.sb("cw", [P, 2, CONV_K]), s.sb("par", [P, 3, 2])
        ones, eps = s.sb("ones", [P, P]), s.sb("eps", [P, 1])
        root, rstd = s.sb("root", [P, CH]), s.sb("rstd", [P, CH])
        psM, psV = s.ps("M", [P, 2, CH]), s.ps("V", [P, 2, CH])
        a_in, g_in, const_in, stored = s.sem("a_in"), s.sem("g_in"), s.sem("const_in"), s.sem("stored")
        chain, conv, mean, centred, squared, var, rooted, scaled, silued, gated = (
            s.sem(x) for x in ("chain", "conv", "mean", "centred", "squared", "var", "rooted", "scaled", "silued", "gated"))
        block = s.block()

        @block.sync
        def _(sp):
            sp.dma_start(u[:, :, H:H + N], a_d.rearrange("a p t -> p a t")).then_inc(a_in, 16)
            sp.dma_start(sg[:], sig_d.rearrange("a p t -> p a t")).then_inc(a_in, 16)
            sp.dma_start(cw[:], cw_d).then_inc(const_in, 16)
            for i, v in enumerate((cb_d, lg_d, lb_d)):
                sp.dma_start(par[:, i], v).then_inc(const_in, 16)
            sp.wait_ge(chain, 3)
            sp.dma_start(sg[:], gate_d.rearrange("a p t -> p a t")).then_inc(g_in, 16)
            for c in range(NCH):
                sp.wait_ge(gated, c + 1)
                sp.dma_start(out_d[:, :, c * W:(c + 1) * W].rearrange("a p t -> p a t"), y[:, :, c * W:(c + 1) * W]).then_inc(stored, 16)
            sp.wait_ge(stored, 16 * NCH)

        @block.vector
        def _(dve):
            n = [0]

            def step(ins):
                n[0] += 1
                ins.then_inc(chain, 1)
                dve.wait_ge(chain, n[0])

            nc.vector.memset(ones[:], 1.0 / (2 * P))
            nc.vector.memset(eps[:], EPS)
            nc.vector.memset(u[:, :, 0:H], 0.0)
            step(nc.vector.memset(u[:, :, H + N:], 0.0))
            dve.wait_ge(a_in, 32)
            for t in range(2):
                step(nc.vector.tensor_tensor(u[:, t, H:H + N], u[:, t, H:H + N], sg[:, t], ALU.mult))
            dve.wait_ge(const_in, 64)
            for t in range(2):
                step(nc.vector.tensor_scalar(y[:, t], u[:, t, 0:N], cw[:, t, 0:1], par[:, 0, t:t + 1], ALU.mult, ALU.add))
                for k in range(1, CONV_K):
                    step(nc.vector.scalar_tensor_tensor(y[:, t], u[:, t, k:k + N], cw[:, t, k:k + 1], y[:, t], ALU.mult, ALU.add))
            dve.engine_nop().then_inc(conv, 1)
            dve.wait_ge(g_in, 16)
            for c in range(NCH):
                cc = slice(c * W, (c + 1) * W)
                dve.wait_ge(mean, c + 1)
                for t in range(2):
                    last = nc.vector.tensor_tensor(y[:, t, cc], y[:, t, cc], psM[:, c % 2, :W], ALU.subtract)
                last.then_inc(centred, 1)
                dve.wait_ge(rooted, c + 1)
                step(nc.vector.reciprocal(rstd[:, :W], root[:, :W]))
                dve.wait_ge(silued, c)
                for t in range(2):
                    last = nc.vector.scalar_tensor_tensor(xh[:, t, :W], y[:, t, cc], par[:, 1, t:t + 1], rstd[:, :W], ALU.mult, ALU.mult)
                last.then_inc(scaled, 1)
                dve.wait_ge(silued, c + 1)
                for t in range(2):
                    last = nc.vector.tensor_tensor(y[:, t, cc], xh[:, t, :W], sg[:, t, cc], ALU.mult)
                last.then_inc(gated, 1)

        @block.tensor
        def _(pe):
            pe.wait_ge(conv, 1)
            for c in range(NCH):
                if c >= 2:
                    pe.wait_ge(centred, c - 1)
                for t in range(2):
                    mm = nc.tensor.matmul(psM[:, c % 2, :W], ones[:], y[:, t, c * W:(c + 1) * W], start=(t == 0), stop=(t == 1))
                mm.then_inc(mean, 1)
                pe.wait_ge(squared, c + 1)
                if c >= 2:
                    pe.wait_ge(rooted, c - 1)
                for t in range(2):
                    mm = nc.tensor.matmul(psV[:, c % 2, :W], ones[:], sq[:, t, :W], start=(t == 0), stop=(t == 1))
                mm.then_inc(var, 1)

        @block.scalar
        def _(act):
            act.wait_ge(conv, 1)
            for c in range(NCH):
                cc = slice(c * W, (c + 1) * W)
                act.wait_ge(centred, c + 1)
                for t in range(2):
                    last = nc.scalar.activation(sq[:, t, :W], y[:, t, cc], ACT.Square)
                last.then_inc(squared, 1)
                act.wait_ge(var, c + 1)
                if c >= 1:
                    act.wait_ge(scaled, c)
                nc.scalar.activation(root[:, :W], psV[:, c % 2, :W], ACT.Sqrt, bias=eps[:, 0:1]).then_inc(rooted, 1)
                act.wait_ge(scaled, c + 1)
                for t in range(2):
                    last = nc.scalar.activation(xh[:, t, :W], xh[:, t, :W], ACT.Silu, bias=par[:, 2, t:t + 1])
                last.then_inc(silued, 1)



def project_out(nc, name, N, y_d, w_d, gate, x_d, out_d, KY):
    W = min(CH, N)
    NH2 = 2 if KY > 8 else 1
    NN = N // NH2
    NCH = NN // W
    with Stage(nc, name) as s:
        y = s.sb("y", [P, KY, NN])
        wt = s.sb("w", [P, 2, KY, P])
        xb = s.sb("x", [P, 2, NN])
        ps = s.ps("ps", [P, 2, SEQ])
        y_in = s.sem("y_in")
        w_in, x_in, stored = s.sems("w_in", 2), s.sems("x_in", 2), s.sems("stored", 2)
        mm_done, added = s.sem("mm_done"), s.sem("added")
        block = s.block()

        def fetch(sp, hf, i, q):
            t = i * 2 + (KT * hf + q)
            wait(sp, mm_done, t - 1)
            sp.dma_start(wt[:, q], w_d[i * 2 + q]).then_inc(w_in[q], 16)
            if not (isinstance(t, int) and t < 2):
                sp.wait_ge(stored[q], (i + (KT // 2) * hf) * 16)
            sp.dma_start(xb[:, q], x_d[i * 2 + q, :, hf * NN:(hf + 1) * NN]).then_inc(x_in[q], 16)

        @block.sync
        def _(sp):
            for hf in range(NH2):
                for q in range(2):
                    fetch(sp, hf, 0, q)
                if hf:
                    sp.wait_ge(mm_done, KT * hf)
                sp.dma_start(y[:], y_d[:, :, hf * NN:(hf + 1) * NN].rearrange("k p t -> p k t")).then_inc(y_in, 16)
                with sp.Fori(1, KT // 2, 1) as i:
                    for q in range(2):
                        fetch(sp, hf, i, q)

        @block.tensor
        def _(pe):
            def products(hf, i, q):
                t = i * 2 + (KT * hf + q)
                pe.wait_ge(w_in[q], (i + (KT // 2) * hf) * 16 + 16)
                wait(pe, added, t - 1)
                for c in range(NCH):
                    for k in range(KY):
                        mm = nc.tensor.matmul(ps[:, q, c * W:(c + 1) * W], wt[:, q, k], y[:, k, c * W:(c + 1) * W],
                                              start=(k == 0), stop=(k == KY - 1))
                mm.then_inc(mm_done, 1)
            for hf in range(NH2):
                pe.wait_ge(y_in, 16 * (hf + 1))
                for q in range(2):
                    products(hf, 0, q)
                with pe.Fori(1, KT // 2, 1) as i:
                    for q in range(2):
                        products(hf, i, q)

        @block.vector
        def _(dve):
            for hf in range(NH2):
                with dve.Fori(0, KT // 2, 1) as i:
                    for q in range(2):
                        t = i * 2 + (KT * hf + q)
                        dve.wait_ge(mm_done, t + 1)
                        dve.wait_ge(x_in[q], (i + (KT // 2) * hf) * 16 + 16)
                        nc.vector.scalar_tensor_tensor(xb[:, q], ps[:, q, :NN], gate[:, ds(i * 2 + q, 1)], xb[:, q],
                                                       ALU.mult, ALU.add).then_inc(added, 1)

        @block.scalar
        def _(act):
            for hf in range(NH2):
                with act.Fori(0, KT // 2, 1) as i:
                    for q in range(2):
                        act.wait_ge(added, i * 2 + (KT * hf + q + 1))
                        act.dma_start(out_d[i * 2 + q, :, hf * NN:(hf + 1) * NN], xb[:, q]).then_inc(stored[q], 16)
            for q in range(2):
                act.wait_ge(stored[q], 16 * (KT // 2) * NH2)



def causal_conv(nc, name, NT, x_d, cw_d, cb_d, out_d):
    N = SEQ
    with Stage(nc, name) as s:
        u = s.sb("u", [P, 2, N + TAPS - 1])
        y = s.sb("y", [P, 2, N])
        cw, cb = s.sb("cw", [P, NT, TAPS]), s.sb("cb", [P, NT])
        u_in, stored = s.sems("u_in", 2), s.sems("stored", 2)
        const_in, zeroed, tapped, conv, silued = (s.sem(x) for x in ("const_in", "zeroed", "tapped", "conv", "silued"))
        block = s.block()

        @block.sync
        def _(sp):
            sp.dma_start(cw[:], cw_d).then_inc(const_in, 16)
            sp.dma_start(cb[:], cb_d).then_inc(const_in, 16)

            def load(t, q):
                wait(sp, conv, t - 1)
                sp.dma_start(u[:, q, TAPS - 1:], x_d[t]).then_inc(u_in[q], 16)
            steps(sp, NT, load)

        @block.vector
        def _(dve):
            nc.vector.memset(u[:, :, 0:TAPS - 1], 0.0).then_inc(zeroed, 1)
            dve.wait_ge(zeroed, 1)
            dve.wait_ge(const_in, 32)

            def conv4(t, q):
                half = t // 2 if isinstance(t, int) else (t - q) // 2
                dve.wait_ge(u_in[q], half * 16 + 16)
                if not (isinstance(t, int) and t < 2):
                    dve.wait_ge(stored[q], half * 16)
                w = cw[:, ds(t, 1), :].rearrange("p a k -> p (a k)")
                nc.vector.tensor_scalar(y[:, q], u[:, q, 0:N], w[:, 0:1], cb[:, ds(t, 1)], ALU.mult, ALU.add).then_inc(tapped, 1)
                for k in range(1, TAPS):
                    dve.wait_ge(tapped, t * (TAPS - 1) + k)
                    nc.vector.scalar_tensor_tensor(y[:, q], u[:, q, k:k + N], w[:, k:k + 1], y[:, q], ALU.mult,
                                                   ALU.add).then_inc(tapped if k < TAPS - 1 else conv, 1)
            steps(dve, NT, conv4)

        @block.scalar
        def _(act):
            def silu(t, q):
                act.wait_ge(conv, t + 1)
                nc.scalar.activation(y[:, q], y[:, q], ACT.Silu).then_inc(silued, 1)
            steps(act, NT, silu)

        @block.gpsimd
        def _(pool):
            def store(t, q):
                pool.wait_ge(silued, t + 1)
                pool.dma_start(out_d[t], y[:, q]).then_inc(stored[q], 16)
            steps(pool, NT, store)
            for q in range(2):
                pool.wait_ge(stored[q], 16 * (NT // 2))



def lru(nc, name, x_d, cw_d, cb_d, wa_d, ba_d, wx_d, bx_d, lam_d, gate_d, out_d):
    N, NT = SEQ, LW // P
    NCH = N // CH
    with Stage(nc, name) as s:
        u = s.sb("u", [P, 2, N + TAPS - 1])
        x, r, iv, a, t, m = (s.sb(n, [P, N]) for n in ("x", "r", "i", "a", "t", "m"))
        gate, ob = s.sb("gate", [P, 2, N]), s.sb("ob", [P, 2, N])
        cw, cb = s.sb("cw", [P, NT, TAPS]), s.sb("cb", [P, NT])
        wa, wx, par = s.sb("wa", [P, NT, P]), s.sb("wx", [P, NT, P]), s.sb("par", [P, 3, NT])
        dec, z = s.sb("dec", [P, 2, NT]), s.sb("z", [P, 6, NT])
        ps = s.ps("ps", [P, 2, SEQ])
        const_in, zeroed, chain, small = s.sem("const_in"), s.sem("zeroed"), s.sem("chain"), s.sem("small")
        u_in, g_in, stored = s.sems("u_in", 2), s.sems("g_in", 2), s.sems("stored", 2)
        conv, gates, sig, expd, squared, summed, rooted, scanned = (
            s.sem(n) for n in ("conv", "gates", "sig", "expd", "squared", "summed", "rooted", "scanned"))
        block = s.block()

        @block.sync
        def _(sp):
            for dst, src in ((cw, cw_d), (cb, cb_d), (wa, wa_d), (wx, wx_d)):
                sp.dma_start(dst[:], src).then_inc(const_in, 16)
            for i, v in enumerate((ba_d, bx_d, lam_d)):
                sp.dma_start(par[:, i], v).then_inc(const_in, 16)
            for k in range(NT):
                if k >= 2:
                    sp.wait_ge(scanned, k - 1)
                sp.dma_start(u[:, k % 2, TAPS - 1:], x_d[k]).then_inc(u_in[k % 2], 16)
                sp.dma_start(gate[:, k % 2], gate_d[k]).then_inc(g_in[k % 2], 16)
                if k >= 1:
                    sp.wait_ge(scanned, k)
                    sp.dma_start(out_d[k - 1], ob[:, (k - 1) % 2]).then_inc(stored[(k - 1) % 2], 16)
            sp.wait_ge(scanned, NT)
            sp.dma_start(out_d[NT - 1], ob[:, (NT - 1) % 2]).then_inc(stored[(NT - 1) % 2], 16)
            for q in range(2):
                sp.wait_ge(stored[q], 16 * (NT // 2))

        @block.vector
        def _(dve):
            n = [0]

            def step(ins):
                n[0] += 1
                ins.then_inc(chain, 1)
                dve.wait_ge(chain, n[0])

            ts, tt, stt = nc.vector.tensor_scalar, nc.vector.tensor_tensor, nc.vector.scalar_tensor_tensor
            step(nc.vector.memset(u[:, :, 0:TAPS - 1], 0.0))
            dve.wait_ge(const_in, 16 * 7)
            dve.wait_ge(small, 1)
            e, zz, z2, acc = z[:, 0], z[:, 1], z[:, 2], z[:, 3]
            step(ts(zz, e, 2.0, None, ALU.add))
            step(nc.vector.reciprocal(z2, zz))
            step(tt(zz, z2, e, ALU.mult))
            step(tt(z2, zz, zz, ALU.mult))
            step(nc.vector.memset(acc, 1.0 / 17))
            for odd in range(15, 0, -2):
                step(tt(acc, acc, z2, ALU.mult))
                step(ts(acc, acc, 1.0 / odd, None, ALU.add))
            step(tt(acc, acc, zz, ALU.mult))
            step(ts(z[:, 4], par[:, 2], -1.0, 0.0, ALU.mult, ALU.max))
            step(stt(z[:, 5], acc, 2.0, z[:, 4], ALU.mult, ALU.add))
            step(ts(dec[:, 0], z[:, 5], -LRU_C, None, ALU.mult))
            ts(dec[:, 1], z[:, 5], LRU_C, None, ALU.mult).then_inc(zeroed, 1)
            for k in range(NT):
                q = k % 2
                dve.wait_ge(u_in[q], 16 * (k // 2 + 1))
                if k >= 1:
                    dve.wait_ge(gates, k)
                step(ts(x[:], u[:, q, 0:N], cw[:, k, 0:1], cb[:, k:k + 1], ALU.mult, ALU.add))
                for tap in range(1, TAPS):
                    ins = stt(x[:], u[:, q, tap:tap + N], cw[:, k, tap:tap + 1], x[:], ALU.mult, ALU.add)
                    if tap < TAPS - 1:
                        step(ins)
                ins.then_inc(conv, 1)
                dve.wait_ge(squared, k + 1)
                stt(m[:], m[:], 1.0, t[:], ALU.add, ALU.mult).then_inc(summed, 1)
                dve.wait_ge(conv, k + 1)
                step(tt(iv[:], iv[:], x[:], ALU.mult))
                dve.wait_ge(rooted, k + 1)
                step(tt(m[:], m[:], iv[:], ALU.mult))
                step(nc.vector.tensor_tensor_scan(t[:], a[:], m[:], 0.0, ALU.mult, ALU.add))
                dve.wait_ge(g_in[q], 16 * (k // 2 + 1))
                if k >= 2:
                    dve.wait_ge(stored[q], 16 * (k // 2))
                tt(ob[:, q], t[:], gate[:, q], ALU.mult).then_inc(scanned, 1)

        @block.tensor
        def _(pe):
            pe.wait_ge(const_in, 16 * 7)
            for k in range(NT):
                pe.wait_ge(conv, k + 1)
                if k >= 1:
                    pe.wait_ge(sig, 2 * k)
                for half, w in enumerate((wa, wx)):
                    for c in range(NCH):
                        mm = nc.tensor.matmul(ps[:, half, c * CH:(c + 1) * CH], w[:, k], x[:, c * CH:(c + 1) * CH],
                                              start=True, stop=True)
                mm.then_inc(gates, 1)

        @block.scalar
        def _(act):
            act.wait_ge(const_in, 16 * 7)
            nc.scalar.activation(z[:, 1], par[:, 2], ACT.Abs).then_inc(expd, 1)
            act.wait_ge(expd, 1)
            nc.scalar.activation(z[:, 0], z[:, 1], ACT.Exp, scale=-1.0).then_inc(small, 1)
            act.wait_ge(zeroed, 1)
            for k in range(NT):
                act.wait_ge(gates, k + 1)
                if k >= 1:
                    act.wait_ge(scanned, k)
                nc.scalar.activation(r[:], ps[:, 0], ACT.Sigmoid, bias=par[:, 0, k:k + 1]).then_inc(sig, 1)
                nc.scalar.activation(iv[:], ps[:, 1], ACT.Sigmoid, bias=par[:, 1, k:k + 1]).then_inc(sig, 1)
                act.wait_ge(sig, 2 * k + 1)
                nc.scalar.activation(t[:], r[:], ACT.Tanh, scale=dec[:, 1, k:k + 1])
                nc.scalar.activation(a[:], r[:], ACT.Exp, scale=dec[:, 0, k:k + 1]).then_inc(expd, 1)
                act.wait_ge(expd, k + 2)
                nc.scalar.activation(m[:], a[:], ACT.Square).then_inc(squared, 1)
                act.wait_ge(summed, k + 1)
                nc.scalar.activation(m[:], m[:], ACT.Sqrt).then_inc(rooted, 1)


def shifted(eng, pairs, ahead, behind):
    ahead(0, 0)

    def pair(i, last):
        ahead(i, 1)
        behind(i, 0)
        if not last:
            ahead(i + 1, 0)
        behind(i, 1)
    pair(0, pairs == 1)
    if pairs > 2:
        with eng.Fori(1, pairs - 1, 1) as i:
            pair(i, False)
    if pairs > 1:
        pair(pairs - 1, True)



LEVELS = 7


def hgrn(nc, name, q_d, f_d, v_d, mask_d, out_d):
    N, H = SEQ, HGH
    C = N // P
    NX = LEVELS + 2
    NA = NX + 2
    with Stage(nc, name) as s:
        qs, ks, cum = s.sb("q", [P, H, N]), s.sb("k", [P, H, N]), s.sb("cum", [P, H, N])
        e1, reset = s.sb("e1", [P, N]), s.sb("reset", [P, N])
        X = s.sb("X", [P, 2, NX, H, P])
        S, kd = s.sb("S", [P, 2, H, P]), s.sb("kd", [P, 2, H, P])
        state, last = s.sb("state", [P, 2, H, P]), s.sb("last", [P, 2, H])
        v, ktok, ob = s.sb("v", [P, 2, H * P]), s.sb("ktok", [P, 2, H * P]), s.sb("o", [P, 2, H, P])
        mask, ident = s.sb("mask", [P, LEVELS + 1, P], I32), s.sb("ident", [P, P])
        psL, psO, psK, psU = (s.ps(n, [P, 2, H * P]) for n in ("L", "O", "K", "U"))
        const_in, const, eye, q_in, f_in = s.sem("const_in"), s.sem("const"), s.sem("eye"), s.sem("q_in"), s.sems("f_in", H)
        absd, pre, logf, cummed = s.sem("absd"), s.sem("pre"), s.sem("logf"), s.sem("cummed")
        dve_passed, pool_passed = s.sem("dve_passed"), s.sem("pool_passed")
        v_in, stored = s.sems("v_in", 2), s.sems("stored", 2)
        differed, expd, mult, levelled, picked = (s.sem(n) for n in ("differed", "expd", "mult", "levelled", "picked"))
        turned, kmoved, updated, stated, outed, omoved = (s.sem(n) for n in ("turned", "kmoved", "updated", "stated", "outed", "omoved"))
        block = s.block()

        @block.sync
        def _(sp):
            for h in range(H):
                sp.dma_start(cum[:, h], f_d[h]).then_inc(f_in[h], 16)
            sp.dma_start(qs[:], q_d.rearrange("h p t -> p h t")).then_inc(q_in, 16)
            sp.dma_start(mask[:], mask_d).then_inc(const_in, 16)

            def load(c, q):
                wait(sp, outed, c - 1)
                wait(sp, updated, c - 1)
                sp.dma_start(v[:, q], v_d[c]).then_inc(v_in[q], 16)
            steps(sp, C, load)

        @block.scalar
        def _(act):
            for h in range(H):
                act.wait_ge(f_in[h], 16)
                nc.scalar.activation(ks[:, h], cum[:, h], ACT.Sigmoid, scale=-1.0)
                if h >= 1:
                    act.wait_ge(logf, h)
                nc.scalar.activation(e1[:], cum[:, h], ACT.Abs).then_inc(absd, 1)
                act.wait_ge(absd, 3 * h + 1)
                nc.scalar.activation(e1[:], e1[:], ACT.Exp, scale=-1.0).then_inc(absd, 1)
                act.wait_ge(absd, 3 * h + 2)
                nc.scalar.activation(e1[:], e1[:], ACT.Ln, bias=1.0).then_inc(absd, 1)
            act.wait_ge(cummed, H)

            def exps(i, q):
                at = ds((i * 2 + q) * P, P)
                c = i * 2 + q
                for n in range(NX):
                    if n == LEVELS:
                        nc.scalar.activation(X[:, q, n], cum[:, :, at], ACT.Exp).then_inc(expd, 1)
                    else:
                        k = n if n < LEVELS else LEVELS
                        act.wait_ge(differed, c * (LEVELS + 1) + (k + 1))
                        nc.scalar.activation(X[:, q, n], X[:, q, n], ACT.Exp).then_inc(expd, 1)
                nc.scalar.activation(last[:, q], cum[:, :, ds(c * P + (P - 1), 1)].rearrange("p h o -> p (h o)"), ACT.Exp).then_inc(expd, 1)
                nc.scalar.copy(kd[:, q], ks[:, :, at]).then_inc(expd, 1)

            def moves(i, q):
                c = i * 2 + q
                act.wait_ge(turned, c + 1)
                wait(act, updated, c - 1)
                nc.scalar.copy(ktok[:, q], psK[:, q]).then_inc(kmoved, 1)
                act.wait_ge(outed, c + 1)
                if not (isinstance(i, int) and i == 0):
                    act.wait_ge(stored[q], i * 16)
                nc.scalar.copy(ob[:, q].rearrange("p h t -> p (h t)"), psO[:, q]).then_inc(omoved, 1)
            shifted(act, C // 2, exps, moves)

        @block.vector
        def _(dve):
            nc.vector.memset(reset[:], 1.0).then_inc(const, 1)
            nc.vector.memset(S[:], 0.0).then_inc(const, 1)
            nc.vector.memset(state[:], 0.0).then_inc(const, 1)
            dve.wait_ge(const, 3)
            nc.vector.memset(reset[:].rearrange("p (c t) -> p c t", t=P)[:, :, 0:1], 0.0).then_inc(pre, 1)
            for h in range(H):
                dve.wait_ge(absd, 3 * h + 3)
                nc.vector.scalar_tensor_tensor(cum[:, h], cum[:, h], 0.0, e1[:], ALU.min, ALU.subtract).then_inc(logf, 1)
                dve.wait_ge(logf, h + 1)
                dve.wait_ge(pre, 1)
                nc.vector.tensor_tensor_scan(cum[:, h], reset[:], cum[:, h], 0.0, ALU.mult, ALU.add).then_inc(cummed, 1)
            dve.wait_ge(cummed, H)
            dve.wait_ge(const_in, 16)

            def differences(i, q, n):
                c = i * 2 + q
                if n == 0:
                    wait(dve, outed, c - 1)
                cc = cum[:, :, ds(c * P, P)]
                if n == LEVELS:
                    nc.vector.tensor_tensor(X[:, q, n + 1], cc[:, :, P - 1:P].broadcast_to([P, H, P]), cc, ALU.subtract).then_inc(differed, 1)
                    return
                m = P >> (n + 1)
                pair = cc.rearrange("p h (g b m) -> p h g b m", b=2, m=m)
                x = X[:, q, n].rearrange("p h (g b m) -> p h g b m", b=2, m=m)
                if m == 1:
                    nc.vector.tensor_tensor(x[:, :, :, 1, 0], pair[:, :, :, 1, 0], pair[:, :, :, 0, 0], ALU.subtract)
                    nc.vector.memset(x[:, :, :, 0, 0], 0.0).then_inc(differed, 1)
                elif m == P // 2:
                    edge = pair[:, :, 0, 0, m - 1:m].broadcast_to([P, H, m])
                    nc.vector.tensor_tensor(x[:, :, 0, 1], pair[:, :, 0, 1], edge, ALU.subtract)
                    nc.vector.tensor_tensor(x[:, :, 0, 0], edge, pair[:, :, 0, 0], ALU.subtract).then_inc(differed, 1)
                else:
                    edge = pair[:, :, :, 0, m - 1:m].broadcast_to([P, H, P // (2 * m), m])
                    nc.vector.tensor_tensor(x[:, :, :, 1], pair[:, :, :, 1], edge, ALU.subtract)
                    nc.vector.tensor_tensor(x[:, :, :, 0], edge, pair[:, :, :, 0], ALU.subtract).then_inc(differed, 1)

            def pick(i, q, n):
                c = i * 2 + q
                dve.wait_ge(levelled, c * (LEVELS + 1) + (n + 1))
                wait(dve, outed, c - 1)
                wait_apart(dve, picked, c * (LEVELS + 1) + n, dve_passed)
                nc.vector.copy_predicated(S[:, q], bcast(mask[:, n], H), psL[:, n % 2].rearrange("p (h t) -> p h t", h=H)).then_inc(picked, 1)

            def update(i, q):
                c = i * 2 + q
                dve.wait_ge(updated, c + 1)
                dve.wait_ge(expd, c * NA + (NX + 1))
                wait(dve, stated, c)
                for h in range(H):
                    ins = nc.vector.scalar_tensor_tensor(state[:, q, h], state[:, 1 - q, h], last[:, q, h:h + 1],
                                                         psU[:, q, h * P:(h + 1) * P], ALU.mult, ALU.add)
                ins.then_inc(stated, 1)

            def pair(i, last_pair):
                for q in range(2):
                    for n in range(LEVELS + 1):
                        if q == 0:
                            differences(i, 1, n)
                        elif not last_pair:
                            differences(i + 1, 0, n)
                        pick(i, q, n)
                    update(i, q)
            for n in range(LEVELS + 1):
                differences(0, 0, n)
            pair(0, False)
            with dve.Fori(1, C // 2 - 1, 1) as i:
                pair(i, False)
            pair(C // 2 - 1, True)

        @block.gpsimd
        def _(pool):
            pool.memset(ident[:], 0.0).then_inc(eye, 1)
            pool.wait_ge(eye, 1)
            pool.affine_select(out=ident[:], in_=ident[:], compare_op=ALU.not_equal, fill=1.0, base=0,
                               pattern=[[-1, P]], channel_multiplier=1).then_inc(eye, 1)
            pool.wait_ge(q_in, 16)
            pool.wait_ge(cummed, H)

            def products(i, q):
                c = i * 2 + q
                at = ds(c * P, P)
                for n in range(NX):
                    wait_apart(pool, expd, c * NA + (n + 1), pool_passed)
                    if n >= LEVELS:
                        pool.tensor_tensor(X[:, q, n], X[:, q, n], (qs, ks)[n - LEVELS][:, :, at], ALU.mult).then_inc(mult, 1)
                        continue
                    m = P >> (n + 1)
                    x = X[:, q, n].rearrange("p h (g b m) -> p h g b m", b=2, m=m)
                    for b, src in ((1, qs), (0, ks)):
                        part = src[:, :, at].rearrange("p h (g b m) -> p h g b m", b=2, m=m)
                        if m == 1:
                            o, w = x[:, :, :, b, 0], part[:, :, :, b, 0]
                        elif m == P // 2:
                            o, w = x[:, :, 0, b], part[:, :, 0, b]
                        else:
                            o, w = x[:, :, :, b], part[:, :, :, b]
                        ins = pool.tensor_tensor(o, o, w, ALU.mult)
                    ins.then_inc(mult, 1)

            def store(i, q):
                c = i * 2 + q
                wait_apart(pool, omoved, c + 1, pool_passed)
                pool.dma_start(out_d[:, :, ds(c * P, P)].rearrange("h p t -> p h t"), ob[:, q]).then_inc(stored[q], 16)
            shifted(pool, C // 2, products, store)
            for q in range(2):
                pool.wait_ge(stored[q], 16 * (C // 2))

        @block.tensor
        def _(pe):
            pe.wait_ge(eye, 2)
            pe.wait_ge(const, 3)
            pe.wait_ge(q_in, 16)

            def chunk(c, q):
                at = ds(c * P, P)
                half = c // 2 if isinstance(c, int) else (c - q) // 2
                for n in range(LEVELS + 1):
                    if n < LEVELS:
                        pe.wait_ge(mult, c * NX + (n + 1))
                    wait(pe, picked, c * (LEVELS + 1) + (n - 1))
                    for h in range(H):
                        o = psL[:, n % 2, h * P:(h + 1) * P]
                        if n < LEVELS:
                            mm = nc.tensor.matmul(o, X[:, q, n, h], X[:, q, n, h], start=True, stop=True)
                        else:
                            if h == 0:
                                pe.wait_ge(expd, c * NA + NA)
                            mm = nc.tensor.matmul(o, kd[:, q, h], qs[:, h, at], start=True, stop=True)
                    mm.then_inc(levelled, 1)
                pe.wait_ge(mult, c * NX + NX)
                wait(pe, kmoved, c - 1)
                for h in range(H):
                    tr = nc.tensor.transpose(psK[:, q, h * P:(h + 1) * P], X[:, q, NX - 1, h], ident[:])
                tr.then_inc(turned, 1)
                pe.wait_ge(v_in[q], half * 16 + 16)
                wait(pe, omoved, c - 1)
                wait(pe, stated, c)
                pe.wait_ge(picked, (c + 1) * (LEVELS + 1))
                for h in range(H):
                    o = psO[:, q, h * P:(h + 1) * P]
                    nc.tensor.matmul(o, v[:, q, h * P:(h + 1) * P], S[:, q, h], start=True, stop=False)
                    mm = nc.tensor.matmul(o, state[:, 1 - q, h], X[:, q, LEVELS, h], start=False, stop=True)
                mm.then_inc(outed, 1)
                pe.wait_ge(kmoved, c + 1)
                wait(pe, stated, c - 1)
                for h in range(H):
                    mm = nc.tensor.matmul(psU[:, q, h * P:(h + 1) * P], ktok[:, q, h * P:(h + 1) * P],
                                          v[:, q, h * P:(h + 1) * P], start=True, stop=True)
                mm.then_inc(updated, 1)
            steps(pe, C, chunk)



def ssd(nc, name, x_d, z_d, dt_d, bias_d, alog_d, skip_d, tri_d, out_d):
    N = SEQ
    C = N // P
    H = SH // SG
    HP = SW // SH
    GT = SW // SG // P
    NI = 4
    with Stage(nc, name) as s:
        xs, Bt, Ct, zb = s.sb("x", [P, 2, GT, P]), s.sb("B", [P, 2, P]), s.sb("C", [P, 2, P]), s.sb("z", [P, 2, GT, P])
        dt, dA, ncum = s.sb("dt", [P, C, SH]), s.sb("dA", [P, C, SH]), s.sb("ncum", [P, C, SH])
        tmp, bias, alog = s.sb("tmp", [P, C, SH]), s.sb("bias", [P, SH]), s.sb("alog", [P, SH])
        skip, tri, ident = s.sb("skip", [P, SW // P]), s.sb("tri", [P, P]), s.sb("ident", [P, P])
        dAu, wl = s.sb("dAu", [P, 2, H]), s.sb("wl", [P, 2, H])
        dec = s.sb("dec", [P, 2, H])
        CB, Btok = s.sb("CB", [P, 2, P]), s.sb("Btok", [P, 2, P])
        xdt, xw = s.sb("xdt", [P, 2, H, HP]), s.sb("xw", [P, 2, H, HP])
        L, EC = s.sb("L", [P, 2, H, P]), s.sb("EC", [P, 2, H, P])
        state, ob = s.sb("state", [P, 2, H, HP]), s.sb("o", [P, 2, GT, P])
        psB = s.ps("cumB", [P, 2, H, P])
        psM, psX = s.ps("psM", [P, CH]), s.ps("psX", [P, CH])
        psY, psU = s.ps("psY", [P, CH]), s.ps("psU", [P, CH])
        const_in, dt_in, eye, zero, small, dts, cums = (s.sem(n) for n in ("const_in", "dt_in", "eye", "zero", "small", "dts", "cums"))
        pool_passed = s.sem("pool_passed")
        unit_in, stored = s.sems("unit_in", 2), s.sems("stored", 2)
        copied, products, spread, clipped, expd, masked, widened = (
            s.sem(n) for n in ("copied", "products", "spread", "clipped", "expd", "masked", "widened"))
        bmoved, xtimed, wlog, wexp, weighted, ends = (s.sem(n) for n in ("bmoved", "xtimed", "wlog", "wexp", "weighted", "ends"))
        yed, updated, decayed, stated, skipped, gated = (s.sem(n) for n in ("yed", "updated", "decayed", "stated", "skipped", "gated"))
        block = s.block()

        @block.sync
        def _(sp):
            sp.dma_start(dt[:], dt_d.rearrange("c p h -> p c h")).then_inc(dt_in, 16)
            for dst, src in ((bias, bias_d), (alog, alog_d), (skip, skip_d), (tri, tri_d)):
                sp.dma_start(dst[:], src).then_inc(const_in, 16)

            def load(i, q):
                u = i * 2 + q
                wait(sp, gated, u - 1)
                wait(sp, updated, u - 1)
                at = ds(i * P, P)
                sp.dma_start(xs[:, q], x_d[q * GT:(q + 1) * GT, :, at].rearrange("a p t -> p a t")).then_inc(unit_in[q], 16)
                sp.dma_start(Bt[:, q], x_d[SG * GT + q, :, at]).then_inc(unit_in[q], 16)
                sp.dma_start(Ct[:, q], x_d[SG * GT + SG + q, :, at]).then_inc(unit_in[q], 16)
                sp.dma_start(zb[:, q], z_d[q * GT:(q + 1) * GT, :, at].rearrange("a p t -> p a t")).then_inc(unit_in[q], 16)
            for q in range(2):
                load(0, q)
            with sp.Fori(1, C, 1) as i:
                for q in range(2):
                    load(i, q)

        @block.gpsimd
        def _(pool):
            pool.memset(ident[:], 0.0).then_inc(eye, 1)
            pool.wait_ge(eye, 1)
            pool.affine_select(out=ident[:], in_=ident[:], compare_op=ALU.not_equal, fill=1.0, base=0,
                               pattern=[[-1, P]], channel_multiplier=1).then_inc(eye, 1)

            def weights(i, q):
                u = i * 2 + q
                pool.wait_ge(masked, u + 1)
                wait_apart(pool, expd, 2 * u + 2, pool_passed)
                pool.tensor_tensor(L[:, q], L[:, q], bcast(CB[:, q], H), ALU.mult).then_inc(widened, 1)
                wait_apart(pool, ends, u + 1, pool_passed)
                pool.tensor_tensor(EC[:, q], EC[:, q], bcast(Ct[:, q], H), ALU.mult).then_inc(widened, 1)

            def store(i, q):
                wait_apart(pool, gated, i * 2 + (q + 1), pool_passed)
                pool.dma_start(out_d[q * GT:(q + 1) * GT, :, ds(i * P, P)].rearrange("a p t -> p a t"), ob[:, q]).then_inc(stored[q], 16)
            shifted(pool, C, weights, store)
            for q in range(2):
                pool.wait_ge(stored[q], 16 * C)

        @block.scalar
        def _(act):
            act.wait_ge(const_in, 64)
            nc.scalar.activation(alog[:], alog[:], ACT.Exp).then_inc(small, 1)
            act.wait_ge(dts, 1)
            nc.scalar.activation(tmp[:], dt[:], ACT.Abs).then_inc(small, 1)
            act.wait_ge(small, 2)
            nc.scalar.activation(tmp[:], tmp[:], ACT.Exp, scale=-1.0).then_inc(small, 1)
            act.wait_ge(small, 3)
            nc.scalar.activation(tmp[:], tmp[:], ACT.Ln, bias=1.0).then_inc(small, 1)

            def front(i, q):
                u = i * 2 + q
                act.wait_ge(spread, u + 1)
                wait(act, yed, u - 1)
                nc.scalar.activation(EC[:, q], psB[:, q], ACT.Exp).then_inc(expd, 1)
                act.wait_ge(clipped, u + 1)
                nc.scalar.activation(L[:, q], L[:, q], ACT.Exp).then_inc(expd, 1)
                act.wait_ge(masked, u + 1)
                wait(act, updated, u - 1)
                nc.scalar.copy(Btok[:, q], psM[:, P:2 * P]).then_inc(bmoved, 1)
                act.wait_ge(wlog, u + 1)
                nc.scalar.activation(wl[:, q], wl[:, q], ACT.Exp).then_inc(wexp, 1)
            shifted(act, C, front, lambda i, q: None)

        @block.vector
        def _(dve):
            ts, tt, stt = nc.vector.tensor_scalar, nc.vector.tensor_tensor, nc.vector.scalar_tensor_tensor
            nc.vector.memset(state[:], 0.0).then_inc(zero, 1)
            dve.wait_ge(dt_in, 16)
            dve.wait_ge(const_in, 64)
            tt(dt[:], dt[:], bcast(bias[:], C), ALU.add).then_inc(dts, 1)
            dve.wait_ge(dts, 1)
            dve.wait_ge(small, 4)
            stt(dt[:], dt[:], 0.0, tmp[:], ALU.max, ALU.add).then_inc(dts, 1)
            dve.wait_ge(dts, 2)
            ts(alog[:], alog[:], -1.0, None, ALU.mult).then_inc(dts, 1)
            dve.wait_ge(dts, 3)
            tt(dA[:], dt[:], bcast(alog[:], C), ALU.mult).then_inc(dts, 1)
            dve.wait_ge(cums, 1)
            ts(ncum[:].rearrange("p c h -> p (c h)"), psX[:, 0:C * SH], -1.0, None, ALU.mult).then_inc(dts, 1)
            dve.wait_ge(dts, 5)

            def heads(t, i, q):
                return t[:, ds(i, 1), q * H:(q + 1) * H].rearrange("p a h -> p (a h)")

            def front(i, q):
                u = i * 2 + q
                wait(dve, spread, u - 1)
                nc.vector.tensor_copy(dAu[:, q], heads(dA, i, q)).then_inc(copied, 1)
                dve.wait_ge(products, u + 1)
                wait(dve, updated, u - 1)
                tt(CB[:, q], psM[:, 0:P], tri[:], ALU.mult).then_inc(masked, 1)
                tt(xdt[:, q], psX[:].rearrange("p (h e) -> p h e", h=H), bcast(heads(dt, i, q), HP, 2), ALU.mult).then_inc(xtimed, 1)
                dve.wait_ge(expd, 2 * u + 1)
                for h in range(H):
                    ins = ts(L[:, q, h], psB[:, q, h], heads(ncum, i, q)[:, h:h + 1], 0.0, ALU.add, ALU.min)
                ins.then_inc(clipped, 1)
                tt(wl[:, q], psB[:, q, :, P - 1], heads(ncum, i, q), ALU.add).then_inc(wlog, 1)
                dve.wait_ge(expd, 2 * u + 1)
                nc.vector.tensor_copy(dec[:, q], EC[:, q, :, P - 1]).then_inc(ends, 1)
                dve.wait_ge(wexp, u + 1)
                dve.wait_ge(xtimed, u + 1)
                tt(xw[:, q], xdt[:, q], bcast(wl[:, q], HP, 2), ALU.mult).then_inc(weighted, 1)

            def back(i, q):
                u = i * 2 + q
                dve.wait_ge(yed, u + 1)
                tt(state[:, q], state[:, q], bcast(dec[:, q], HP, 2), ALU.mult).then_inc(decayed, 1)
                dve.wait_ge(updated, u + 1)
                dve.wait_ge(decayed, u + 1)
                tt(state[:, q], state[:, q], psU[:].rearrange("p (h e) -> p h e", h=H), ALU.add).then_inc(stated, 1)
                if not (isinstance(i, int) and i == 0):
                    dve.wait_ge(stored[q], i * 16)
                for a in range(GT):
                    ins = stt(ob[:, q, a], xs[:, q, a], skip[:, q * GT + a:q * GT + a + 1], psY[:, a * P:(a + 1) * P], ALU.mult, ALU.add)
                ins.then_inc(skipped, 1)
                dve.wait_ge(skipped, u + 1)
                tt(ob[:, q], ob[:, q], zb[:, q], ALU.mult).then_inc(gated, 1)
            shifted(dve, C, front, back)

        @block.tensor
        def _(pe):
            pe.wait_ge(eye, 2)
            pe.wait_ge(const_in, 64)
            pe.wait_ge(zero, 1)
            pe.wait_ge(dts, 4)
            nc.tensor.matmul(psX[:, 0:C * SH], tri[:], dA[:].rearrange("p c h -> p (c h)"), start=True, stop=True).then_inc(cums, 1)
            pe.wait_ge(dts, 5)

            def front(i, q):
                u = i * 2 + q
                pe.wait_ge(unit_in[q], i * (16 * NI) + 16 * NI)
                wait(pe, masked, u)
                wait(pe, bmoved, u)
                wait(pe, xtimed, u)
                nc.tensor.matmul(psM[:, 0:P], Bt[:, q], Ct[:, q], start=True, stop=True)
                nc.tensor.transpose(psM[:, P:2 * P], Bt[:, q], ident[:])
                for a in range(GT):
                    mm = nc.tensor.transpose(psX[:, a * P:(a + 1) * P], xs[:, q, a], ident[:])
                mm.then_inc(products, 1)
                pe.wait_ge(copied, u + 1)
                wait(pe, expd, 2 * u - 2)
                wait(pe, wlog, u - 1)
                for h in range(H):
                    mm = nc.tensor.matmul(psB[:, q, h], dAu[:, q, h:h + 1].broadcast_to([P, P]), tri[:], start=True, stop=True)
                mm.then_inc(spread, 1)

            def back(i, q):
                u = i * 2 + q
                pe.wait_ge(widened, 2 * u + 2)
                if not (isinstance(i, int) and i == 0):
                    pe.wait_ge(stated, u - 1)
                wait(pe, skipped, u)
                for h in range(H):
                    rows = slice(h % 2 * HP, h % 2 * HP + HP)
                    o = psY[rows, h // 2 * P:(h // 2 + 1) * P]
                    nc.tensor.matmul(o, xdt[:, q, h], L[:, q, h], start=True, stop=False)
                    mm = nc.tensor.matmul(o, state[:, q, h], EC[:, q, h], start=False, stop=True)
                mm.then_inc(yed, 1)
                pe.wait_ge(weighted, u + 1)
                wait(pe, stated, u)
                nc.tensor.matmul(psU[:], Btok[:, q], xw[:, q].rearrange("p h e -> p (h e)"), start=True, stop=True).then_inc(updated, 1)
            shifted(pe, C, front, back)



def load_constants(nc, loads, zeros):
    with Stage(nc, "init") as s:
        z = s.sb("z", [P, P])
        loaded, zeroed, padded = s.sem("loaded"), s.sem("zeroed"), s.sem("padded")
        block = s.block()

        @block.vector
        def _(dve):
            nc.vector.memset(z[:], 0.0).then_inc(zeroed, 1)

        @block.sync
        def _(sp):
            for dst, src in loads:
                sp.dma_start(dst, src).then_inc(loaded, 16)
            sp.wait_ge(loaded, 16 * len(loads))
            sp.wait_ge(zeroed, 1)
            for dst in zeros:
                sp.dma_start(dst, z[:]).then_inc(padded, 16)
            sp.wait_ge(padded, 16 * len(zeros))


def program(nc, t, out):
    def dram(name, shape):
        return nc.dram_tensor(name, shape, F32, kind="Internal").ap()

    kpad, vpad = dram("kpad", [P, SEQ + 2 * P]), dram("vpad", [SEQ // P + 2, P, P])
    with ExitStack() as keep:
        def sb(name, shape):
            return keep.enter_context(nc.sbuf_tensor(name, shape, F32))

        mod1, gain1 = sb("mod1", [P, 3 * KT, 2]), sb("gain1", [P, KT, 2])
        mod2, gain2 = sb("mod2", [P, 3 * KT, 1]), sb("gain2", [P, KT, 1])
        final_g, final_g2 = sb("final_g", [P, KT]), sb("final_g2", [P, KT])
        hg_g, ssd_g = sb("hg_g", [P, HW // P]), sb("ssd_g", [P, SW // P])
        load_constants(nc, [(final_g[:], t["final_g"]), (final_g2[:], t["final_norm_w_2"]),
                            (hg_g[:], t["hg_norm_w_2"]), (ssd_g[:], t["ssd_norm_w_2"])],
                       [kpad[:, 0:P], kpad[:, P + SEQ:], vpad[0], vpad[SEQ // P + 1]])

        xT, ctxT = t["x"], t["ctx"]
        for l in range(DEPTH):
            modulation(nc, f"ada{l}", t["cond"], t["w_ada"][l], t["b_ada"][l], t["norm_g"][l], mod1, gain1, 2)
            kcT, vc = dram(f"kcT{l}", [1, P, CTX]), dram(f"vc{l}", [CTX // P, P, P])
            more = l < DEPTH - 1
            for part in ("c", ""):
                n = f"{part}{l}"
                N, src, which = (CTX, ctxT, 1) if part else (SEQ, xT, 0)
                full = not part or more
                with nc.sbuf_tensor(f"h{n}", [P, KT, N], F32) as h:
                    norm(nc, f"norm{n}", src, N, gain1[:, :, which], out_sb=h, shift=mod1[:, 0:KT, which])
                    if full:
                        q, sig, val, u = dram(f"q{n}", [4, P, N]), dram(f"sig{n}", [2, P, N]), dram(f"val{n}", [2, P, N]), dram(f"u{n}", [N // P, P, 2 * P])
                        gates = dram(f"gates{n}", [8, P, N])
                        turn = ACT.Copy if part else "rope"
                        kout = kcT if part else kpad[:, P:P + SEQ].unsqueeze(0)
                        vout = vc if part else vpad[1:SEQ // P + 1]
                        project(nc, f"in{n}", h, N, t["w_in"][l],
                                [(turn, 4, q, SCALE), (ACT.Silu, 8, gates, 1.0), (ACT.Sigmoid, 2, sig, 1.0),
                                 (ACT.Copy, 2, val, 1.0), (turn, 1, kout, 1.0)], tables=None if part else t["rope"])
                        project_tokens(nc, f"tok{n}", h, N, t["w_vu"][l], 3 * P, [(vout, 0, P), (u, P, 2 * P)])
                    else:
                        project(nc, f"in{n}", h, N, t["w_in"][l][16:17], [(ACT.Copy, 1, kcT, 1.0)])
                        project_tokens(nc, f"tok{n}", h, N, t["w_vu"][l][:, :, 0:P], P, [(vc, 0, P)])
                if not full:
                    continue
                y = dram(f"y{n}", [8, P, N])
                if part:
                    attention(nc, f"att{n}", N, q, kcT[0], vc, t["attn_sink"][l], gates[0:4], y[0:4])
                else:
                    attention(nc, f"att{n}", N, q, kcT[0], vc, t["attn_sink"][l], gates[0:4], y[0:4],
                              kpad, vpad, t["window"])
                conformer(nc, f"conf{n}", N, val, sig, t["conv_w"][l], t["conv_b"][l], t["conv_ln_g"][l],
                          t["conv_ln_b"][l], gates[4:6], y[4:6])
                fourier(nc, f"four{n}", N, u, t[f"fourier{N}"], t["heads"], t["w_four"][l], t["b_four"][l], gates[6:8], y[6:8])
                new = dram(f"x{n}", [KT, P, N])
                project_out(nc, f"out{n}", N, y, t["w_out"][l], mod1[:, 2 * KT:, which], src, new, KT)
                if part:
                    ctxT = new
                else:
                    xT = new

        x2, x3 = dram("x2", [KT, P, SEQ]), dram("x3", [KT, P, SEQ])
        norm(nc, "mid", xT, SEQ, final_g, out_dram=x2)
        modulation(nc, "ada_2", t["cond_2"], t["w_ada_2"], t["b_ada_2"], t["norm_w_2"], mod2, gain2, 1)
        ax, hf, xbc = dram("ax", [4, P, SEQ]), dram("hf", [4, P, SEQ]), dram("xbc", [12, P, SEQ])
        gates = dram("gates_2", [20, P, SEQ])
        hi, dt = dram("hi", [SEQ // P, P, HW]), dram("dt", [SEQ // P, P, SH])
        with nc.sbuf_tensor("h_2", [P, KT, SEQ], F32) as h:
            norm(nc, "norm_2", x2, SEQ, gain2[:, :, 0], out_sb=h, shift=mod2[:, 0:KT, 0])
            project(nc, "in_2", h, SEQ, t["w_in_2"], [(ACT.Copy, 4, ax, 1.0), (ACT.Copy, 4, hf, 1.0), (ACT.Copy, 12, xbc, 1.0),
                                                      (ACT.Silu, 20, gates, 1.0)])
            project_tokens(nc, "hi_2", h, SEQ, t["w_hi_2"], HW, [(hi, 0, HW)])
            project_tokens(nc, "dt_2", h, SEQ, t["w_dt_2"], SH, [(dt, 0, SH)])
        y = dram("y_2", [16, P, SEQ])
        lru(nc, "lru", ax, t["lru_conv_w_2"], t["lru_conv_b_2"], t["lru_wa_2"], t["lru_ba_2"], t["lru_wx_2"], t["lru_bx_2"],
            t["lru_lambda_2"], gates[0:4], y[0:4])
        o_hg, o_ssd, xbcs = dram("o_hg", [4, P, SEQ]), dram("o_ssd", [8, P, SEQ]), dram("xbcs", [12, P, SEQ])
        hgrn(nc, "hgrn", gates[4:8], hf, hi, t["levels"], o_hg)
        norm(nc, "hgnorm", o_hg, SEQ, hg_g, out_dram=y[4:8], gate_d=gates[8:12], K=HW // P)
        causal_conv(nc, "conv_2", 12, xbc, t["ssd_conv_w_2"], t["ssd_conv_b_2"], xbcs)
        ssd(nc, "ssd", xbcs, gates[12:20], dt, t["ssd_dt_bias_2"], t["ssd_a_log_2"], t["ssd_d_2"], t["causal"], o_ssd)
        for g in range(SG):
            norm(nc, f"ssdnorm{g}", o_ssd[4 * g:4 * g + 4], SEQ, ssd_g[:, 4 * g:4 * g + 4], out_dram=y[8 + 4 * g:12 + 4 * g], K=4)
        project_out(nc, "out_2", SEQ, y, t["w_out_2"], mod2[:, 2 * KT:, 0], x2, x3, 16)
        norm(nc, "final", x3, SEQ, final_g2, out_dram=out)



def rope_tables():
    pos = np.arange(SEQ)
    f = 10000.0 ** (-np.arange(16, dtype=np.float32) / 16)
    row = (pos // 64).astype(np.float32)[None] * f[:, None].astype(np.float32)
    col = (pos % 64).astype(np.float32)[None] * f[:, None].astype(np.float32)
    c = np.concatenate([np.cos(row), np.cos(row), np.cos(col), np.cos(col)])
    s = np.concatenate([-np.sin(row), np.sin(row), -np.sin(col), np.sin(col)])
    return np.stack([np.tile(c, (2, 1)), np.tile(s, (2, 1))]).astype(np.float32)


def window_masks():
    q, r = np.arange(P)[:, None], np.arange(P)[None, :]
    m = [np.where(r >= q, 0.0, NEG), np.where(r <= q, 0.0, NEG), np.full((P, P), NEG)]
    return np.stack(m, axis=1).astype(np.float32)


def fourier_table(N):
    R = N // 128
    n1, k2, k1 = np.arange(128)[None, :, None], np.arange(R)[:, None, None], np.arange(128)[None, None, :]
    ang = 2 * np.pi * ((n1 * (R * k1 + k2)) % N) / N
    c, s = np.cos(ang), np.sin(ang)
    sign = np.where(k2 <= R // 2, 1.0, -1.0)
    return np.concatenate([c, s, sign * s, -sign * c], axis=2).astype(np.float32)


def head_table():
    d = np.arange(64)
    ang = 2 * np.pi * ((d[:, None] * d[None, :]) % 64) / 64
    eye = np.eye(2)
    return np.stack([np.kron(eye, np.cos(ang)), np.kron(eye, np.sin(ang))], axis=1).astype(np.float32)


def hgrn_masks():
    s, t = np.arange(P)[:, None], np.arange(P)[None, :]
    out = []
    for n in range(LEVELS):
        m = P >> (n + 1)
        out.append((s // (2 * m) == t // (2 * m)) & (s // m % 2 == 0) & (t // m % 2 == 1))
    return np.ascontiguousarray(np.stack(out + [s == t], axis=1).astype(np.int32))


def blockdiag(w):
    out = np.zeros((P, 4, P), w.dtype)
    for h in range(8):
        r = slice(h % 2 * 64, h % 2 * 64 + 64)
        out[r, h // 2, r] = w[h]
    return out



def tiles(w):
    return np.ascontiguousarray(w.reshape(w.shape[0] // P, P, -1, P).transpose(2, 1, 0, 3))


def columns(v):
    return np.ascontiguousarray(v.reshape(-1, P).T)


def transposed(x):
    return np.ascontiguousarray(x.T.reshape(-1, P, x.shape[0]))


def taps(w):
    return np.ascontiguousarray(w.T.reshape(-1, P, w.shape[0]).transpose(1, 0, 2))


def everywhere(v):
    return np.ascontiguousarray(np.broadcast_to(v.reshape(1, -1), (P, v.size)))


def head_order():
    heads = [g * GQ + j for j in range(GQ) for g in range(NKV)]
    return np.concatenate([np.arange(h * HD, (h + 1) * HD) for h in heads])


def layout(a):
    order = head_order()
    edge = np.cumsum([0, 512, 128, 128, 512, 256, 256, 256, 256, 256])
    q, k, v, g_att, c_a, c_b, g_conv, f_u, g_four = (np.arange(edge[i], edge[i + 1]) for i in range(9))
    cols = np.concatenate([q[order], g_att[order], g_conv, g_four, c_b, c_a, k])
    vu = np.concatenate([v, f_u])
    kmajor = lambda w: np.ascontiguousarray(w.reshape(KT, P, -1).transpose(1, 0, 2))
    layers = lambda f, name: np.stack([f(a[name][l]) for l in range(DEPTH)])
    t = {
        "x": transposed(a["x"][0]), "ctx": transposed(a["ctx"][0]),
        "cond": np.ascontiguousarray(np.stack([columns(a["c"][0]), columns(a["c_ctx"])], axis=2)),
        "cond_2": columns(a["c_2"][0])[:, :, None].copy(),
        "w_ada": layers(tiles, "w_ada"), "b_ada": layers(columns, "b_ada"), "norm_g": layers(columns, "norm_g"),
        "w_in": np.stack([tiles(a["w_in"][l][:, cols]) for l in range(DEPTH)]),
        "w_vu": np.stack([kmajor(a["w_in"][l][:, vu]) for l in range(DEPTH)]),
        "attn_sink": a["attn_sink"].reshape(DEPTH, 1, NH),
        "conv_w": layers(taps, "conv_w"), "conv_b": layers(columns, "conv_b"),
        "conv_ln_g": layers(columns, "conv_ln_g"), "conv_ln_b": layers(columns, "conv_ln_b"),
        "w_four": a["w_four"], "b_four": layers(columns, "b_four"),
        "w_out": np.stack([tiles(np.concatenate([a["w_out"][l][order], a["w_out"][l][ATT:]])) for l in range(DEPTH)]),
        "final_g": columns(a["final_g"]),
        "rope": rope_tables(), "window": window_masks(), "heads": head_table(),
        "fourier2048": fourier_table(SEQ), "fourier256": fourier_table(CTX),
    }
    edge = np.cumsum([0, 512, 512, 512, 512, 512, 512, 1024, 1536, 16])
    a_x, a_g, hg_q, hg_f, hg_i, hg_g, z, xbc, dt = (np.arange(edge[i], edge[i + 1]) for i in range(9))
    w = a["w_in_2"][0]
    t.update({
        "w_ada_2": tiles(a["w_ada_2"][0]), "b_ada_2": columns(a["b_ada_2"][0]), "norm_w_2": columns(a["norm_w_2"][0]),
        "w_in_2": tiles(w[:, np.concatenate([a_x, hg_f, xbc, a_g, hg_q, hg_g, z])]),
        "w_hi_2": kmajor(w[:, hg_i]), "w_dt_2": kmajor(w[:, dt]),
        "lru_conv_w_2": taps(a["lru_conv_w_2"][0]), "lru_conv_b_2": columns(a["lru_conv_b_2"][0]),
        "lru_wa_2": blockdiag(a["lru_wa_2"][0]), "lru_wx_2": blockdiag(a["lru_wx_2"][0]),
        "lru_ba_2": columns(a["lru_ba_2"][0].reshape(-1)), "lru_bx_2": columns(a["lru_bx_2"][0].reshape(-1)),
        "lru_lambda_2": columns(a["lru_lambda_2"][0]), "hg_norm_w_2": columns(a["hg_norm_w_2"][0]),
        "ssd_conv_w_2": taps(a["ssd_conv_w_2"][0]), "ssd_conv_b_2": columns(a["ssd_conv_b_2"][0]),
        "ssd_dt_bias_2": everywhere(a["ssd_dt_bias_2"][0]), "ssd_a_log_2": everywhere(a["ssd_a_log_2"][0]),
        "ssd_d_2": columns(np.repeat(a["ssd_d_2"][0], SW // SH)), "ssd_norm_w_2": columns(a["ssd_norm_w_2"][0]),
        "w_out_2": tiles(a["w_out_2"][0]), "final_norm_w_2": columns(a["final_norm_w_2"]),
        "levels": hgrn_masks(), "causal": np.triu(np.ones((P, P), np.float32)),
    })
    return t


def kernel(**inputs):
    import concourse.bacc as bacc
    from concourse.bass_utils import run_bass_kernel_spmd

    arrays = {f"in_{n}": v for n, v in layout({n: np.asarray(v) for n, v in inputs.items()}).items()}
    nc = bacc.Bacc("TRN2", target_bir_lowering=False, num_devices=1)
    aps = {n[3:]: nc.dram_tensor(n, v.shape, mybir.dt.from_np(v.dtype), kind="ExternalInput").ap() for n, v in arrays.items()}
    out = nc.dram_tensor("out", (KT, P, SEQ), F32, kind="ExternalOutput").ap()
    program(nc, aps, out)
    r = run_bass_kernel_spmd(nc, [arrays], core_ids=[0])
    return np.ascontiguousarray(r.results[0]["out"].reshape(D, SEQ).T)[None]
```

```python
from contextlib import ExitStack

import numpy as np

import concourse.bass as bass
import concourse.mybir as mybir

F32 = mybir.dt.float32
BF16 = mybir.dt.bfloat16
F32R = mybir.dt.float32r
I32 = mybir.dt.int32
ALU = mybir.AluOpType
ACT = mybir.ActivationFunctionType
AX = mybir.AxisListType
ds = bass.ds

P = 128
D = 1024
KT = D // P
SEQ = 2048
CTX = 256
DEPTH = 2
CH = 512
EPS = 1e-6
NEG = -1e30

HD = 64
NH = 8
ATT = NH * HD
NKV = 2
GQ = NH // NKV
SCALE = HD ** -0.5
CONV_K = 31
FH = 64

LW = 512
HW = 512
HGH = HW // P
SW = 1024
SH = 16
SG = 2
SXBC = SW + 2 * SG * P
TAPS = 4
LRU_C = 8.0


def wait(eng, sem, value):
    if not (isinstance(value, int) and value <= 0):
        eng.wait_ge(sem, value)


def wait_apart(eng, sem, value, passed):
    wait(eng, sem, value)
    eng.sem_inc(passed, 1)


def steps(eng, n, body):
    first = min(n, 2)
    for b in range(first):
        body(b, b % 2)
    pairs = n // 2
    if pairs > 2:
        with eng.Fori(1, pairs - 1, 1) as i:
            for q in range(2):
                body(i * 2 + q, q)
    for b in range(max(first, n - 2), n):
        body(b, b % 2)


class Stage:

    def __init__(self, nc, name):
        self.nc, self.name, self.ctx, self.taken = nc, name, ExitStack(), []

    def __enter__(self):
        self.ctx.__enter__()
        return self

    def __exit__(self, *a):
        self.ctx.__exit__(*a)
        if a[0] is None:
            self.nc.clear_and_free_semaphores(self.taken)
            self.nc.all_engine_barrier()

    def sb(self, name, shape, dt=F32):
        return self.ctx.enter_context(self.nc.sbuf_tensor(f"{self.name}_{name}", shape, dt))

    def ps(self, name, shape, dt=F32):
        return self.ctx.enter_context(self.nc.psum_tensor(f"{self.name}_{name}", shape, dt))

    def sem(self, name):
        self.taken.append(self.nc.alloc_semaphore(f"{self.name}_{name}"))
        return self.taken[-1]

    def sems(self, name, n):
        return [self.sem(f"{name}{i}") for i in range(n)]

    def block(self):
        return self.ctx.enter_context(self.nc.Block())


def bcast(ap, n, axis=1):
    a = ap.unsqueeze(axis)
    shape = list(a.shape)
    shape[axis] = n
    return a.broadcast_to(shape)



def modulations(nc, name, sets):
    NJ, NB, NC = 3 * KT, 3, 3 * D // CH
    NM = 2
    n_sets = len(sets)
    with Stage(nc, name) as s:
        c, sc = s.sb("c", [P, n_sets, KT * NM]), s.sb("sc", [P, n_sets, KT * NM])
        bb, gg = s.sb("b", [P, n_sets, NJ]), s.sb("g", [P, n_sets, KT])
        wt, ident = s.sb("w", [P, NB, KT, CH]), s.sb("ident", [NM, NM])
        row = s.sb("row", [NM, 2, CH])
        ps, psT = s.ps("ps", [P, 2, CH]), s.ps("psT", [P, 2, CH])
        c_in, silu_done, mm_done, moved = s.sem("c_in"), s.sem("silu_done"), s.sem("mm_done"), s.sem("moved")
        turned, eye, done = s.sem("turned"), s.sem("eye"), s.sem("done")
        w_in = s.sems("w_in", NB)
        block = s.block()
        units = [(m, j) for m in range(n_sets) for j in range(NC)]

        @block.sync
        def _(sp):
            for m, (cond, w, b, g, mod, gain, ncond) in enumerate(sets):
                sp.dma_start(c[:, m, 0:KT * ncond], cond.rearrange("p k n -> p (k n)")).then_inc(c_in, 16)
                sp.dma_start(bb[:, m], b).then_inc(c_in, 16)
                sp.dma_start(gg[:, m], g).then_inc(c_in, 16)
            for u, (m, j) in enumerate(units):
                wait(sp, mm_done, u + 1 - NB)
                sp.dma_start(wt[:, u % NB], sets[m][1][j]).then_inc(w_in[u % NB], 16)

        @block.gpsimd
        def _(pool):
            pool.memset(ident[:], 0.0).then_inc(eye, 1)
            pool.wait_ge(eye, 1)
            pool.affine_select(out=ident[:], in_=ident[:], compare_op=ALU.not_equal, fill=1.0, base=0,
                               pattern=[[-1, NM]], channel_multiplier=1).then_inc(eye, 1)

        @block.scalar
        def _(act):
            act.wait_ge(c_in, 48 * n_sets)
            for m, one in enumerate(sets):
                nc.scalar.activation(sc[:, m, 0:KT * one[-1]], c[:, m, 0:KT * one[-1]], ACT.Silu).then_inc(silu_done, 1)
            for u, (m, j) in enumerate(units):
                n = sets[m][-1]
                act.wait_ge(mm_done, u + 1)
                wait(act, turned, u - 1)
                nc.scalar.copy(row[0:n, u % 2], ps[0:n, u % 2]).then_inc(moved, 1)

        @block.tensor
        def _(pe):
            pe.wait_ge(silu_done, n_sets)
            pe.wait_ge(eye, 2)

            def turn(u):
                m, j = units[u]
                n = sets[m][-1]
                pe.wait_ge(moved, u + 1)
                if j == 0:
                    wait(pe, done, 2 * (m - 1))
                for a in range(CH // P):
                    at = (j * (CH // P) + a) * n
                    tr = nc.tensor.transpose(psT[:, m % 2, at:at + n], row[0:n, u % 2, a * P:(a + 1) * P], ident[0:n, 0:n])
                tr.then_inc(turned, 1)

            for u, (m, j) in enumerate(units):
                n = sets[m][-1]
                pe.wait_ge(w_in[u % NB], (u // NB + 1) * 16)
                wait(pe, moved, u - 1)
                for k in range(KT):
                    mm = nc.tensor.matmul(ps[0:n, u % 2], sc[:, m, k * n:(k + 1) * n], wt[:, u % NB, k], start=(k == 0), stop=(k == KT - 1))
                mm.then_inc(mm_done, 1)
                if u >= 1:
                    turn(u - 1)
            turn(len(units) - 1)

        @block.vector
        def _(dve):
            dve.wait_ge(c_in, 48 * n_sets)
            for m, (cond, w, b, g, mod, gain, ncond) in enumerate(sets):
                dve.wait_ge(turned, (m + 1) * NC)
                for n in range(ncond):
                    last = nc.vector.tensor_tensor(mod[:, :, n], psT[:, m % 2, 0:NJ * ncond].rearrange("p (j n) -> p j n", n=ncond)[:, :, n],
                                                   bb[:, m], ALU.add)
                last.then_inc(done, 1)
                dve.wait_ge(done, 2 * m + 1)
                for n in range(ncond):
                    last = nc.vector.scalar_tensor_tensor(gain[:, :, n], mod[:, KT:2 * KT, n], 1.0, gg[:, m], ALU.add, ALU.mult)
                last.then_inc(done, 1)



def norm(nc, name, xT, N, gain, out_sb=None, out_dram=None, shift=None, gate_d=None, K=KT, groups=1):
    W = min(CH if out_sb is None else CH // 2, N)
    NG = N // W
    NCH = NG * groups
    NX = 4 if out_sb is None else 3
    with Stage(nc, name) as s:
        x = s.sb("x", [P, NX, K, W])
        sq = s.sb("sq", [P, 2, K, W])
        ones = s.sb("ones", [P, P])
        eps = s.sb("eps", [P, 1])
        root = s.sb("root", [P, 2, W])
        rstd = s.sb("rstd", [P, 2, W])
        o = s.sb("o", [P, 2, K, W])
        gb = None if gate_d is None else s.sb("g", [P, NX, K, W])
        ps = s.ps("ps", [P, 2, CH])
        x_in, g_in, o_out = s.sems("x_in", NX), s.sems("g_in", NX), s.sems("o_out", 2)
        const, sq_done, sum_done, root_done = s.sem("const"), s.sem("sq_done"), s.sem("sum_done"), s.sem("root_done")
        rstd_done, scaled, done, parted = s.sem("rstd_done"), s.sem("scaled"), s.sem("done"), s.sem("parted")
        block = s.block()

        def rows(c):
            return slice(c // NG * K, c // NG * K + K)

        def dst(c, k):
            return o[:, c % 2, k]

        def part(i, c, k):
            return out_sb[:, i, k, c * W:(c + 1) * W]

        @block.sync
        def _(sp):
            for c in range(NCH):
                kk, cc = rows(c), slice(c % NG * W, c % NG * W + W)
                if c >= NX:
                    sp.wait_ge(scaled, c + 1 - NX)
                sp.dma_start(x[:, c % NX], xT[kk, :, cc].rearrange("k p t -> p k t")).then_inc(x_in[c % NX], 16)
                if gb is not None:
                    if c >= NX:
                        sp.wait_ge(done, c + 1 - NX)
                    sp.dma_start(gb[:, c % NX], gate_d[kk, :, cc].rearrange("k p t -> p k t")).then_inc(g_in[c % NX], 16)

        if out_sb is None:
            @block.gpsimd
            def _(pool):
                for c in range(NCH):
                    pool.wait_ge(done, c + 1)
                    pool.dma_start(out_dram[rows(c), :, c % NG * W:c % NG * W + W].rearrange("k p t -> p k t"), o[:, c % 2]).then_inc(o_out[c % 2], 16)
                for q in range(2):
                    n = (NCH + 1 - q) // 2
                    if n:
                        pool.wait_ge(o_out[q], 16 * n)

        @block.tensor
        def _(pe):
            pe.wait_ge(const, 2)
            for c in range(NCH):
                pe.wait_ge(sq_done, c + 1)
                if c >= 2:
                    pe.wait_ge(root_done, c - 1)
                for k in range(K):
                    mm = nc.tensor.matmul(ps[:, c % 2, :W], ones[:], sq[:, c % 2, k], start=(k == 0), stop=(k == K - 1))
                mm.then_inc(sum_done, 1)

        @block.scalar
        def _(act):
            act.wait_ge(const, 2)

            def finish(c):
                act.wait_ge(scaled, c + 1)
                for k in range(K):
                    last = nc.scalar.activation(part(0, c, k), dst(c, k), ACT.Identity, bias=shift[:, k:k + 1])
                last.then_inc(done, 1)

            def square(c):
                act.wait_ge(x_in[c % NX], 16 * (c // NX + 1))
                wait(act, sum_done, c - 1)
                nc.scalar.activation(sq[:, c % 2], x[:, c % NX], ACT.Square).then_inc(sq_done, 1)

            square(0)
            for c in range(NCH):
                if c + 1 < NCH:
                    square(c + 1)
                act.wait_ge(sum_done, c + 1)
                if c >= 2:
                    act.wait_ge(rstd_done, c - 1)
                nc.scalar.activation(root[:, c % 2], ps[:, c % 2, :W], ACT.Sqrt, bias=eps[:, 0:1]).then_inc(root_done, 1)
                if shift is not None and c >= 1:
                    finish(c - 1)
            if shift is not None:
                finish(NCH - 1)

        @block.vector
        def _(dve):
            nc.vector.memset(ones[:], 1.0 / (K * P)).then_inc(const, 1)
            nc.vector.memset(eps[:], EPS).then_inc(const, 1)

            def rest(c):
                dve.wait_ge(done, c + 1)
                for k in range(K):
                    last = nc.vector.scalar_tensor_tensor(part(1, c, k), dst(c, k), shift[:, k:k + 1], part(0, c, k).bitcast(F32),
                                                          ALU.add, ALU.subtract)
                last.then_inc(parted, 1)

            for c in range(NCH):
                dve.wait_ge(root_done, c + 1)
                nc.vector.reciprocal(rstd[:, c % 2], root[:, c % 2]).then_inc(rstd_done, 1)
                dve.wait_ge(rstd_done, c + 1)
                if out_sb is None and c >= 2:
                    dve.wait_ge(o_out[c % 2], 16 * (c // 2))
                if out_sb is not None and c >= 1:
                    rest(c - 1)
                if out_sb is not None and c >= 2:
                    dve.wait_ge(parted, c - 1)
                for k in range(K):
                    last = nc.vector.scalar_tensor_tensor(dst(c, k), x[:, c % NX, k], gain[:, c // NG * K + k:c // NG * K + k + 1], rstd[:, c % 2],
                                                          ALU.mult, ALU.mult)
                    if k == K - 1:
                        last.then_inc(scaled, 1)
                if gb is not None:
                    dve.wait_ge(scaled, c + 1)
                    dve.wait_ge(g_in[c % NX], 16 * (c // NX + 1))
                    nc.vector.tensor_tensor(o[:, c % 2], o[:, c % 2], gb[:, c % NX], ALU.mult).then_inc(done, 1)
                elif shift is None:
                    dve.wait_ge(scaled, c + 1)
                    dve.engine_nop().then_inc(done, 1)
            if out_sb is not None:
                rest(NCH - 1)



PARTS = ((0, 0), (0, 1), (1, 0))


def project(nc, name, h, N, w, runs, tables=None, taps4=None, glu=None, taps31=None):
    W = min(CH, N)
    NCH = N // W
    rope = any(r[0] == "rope" for r in runs)
    total = sum(r[1] for r in runs)
    convs = any(r[0] in ("conv", "conv_silu") for r in runs)
    kept = 2 if glu else 0
    decays = any(r[0] == "decay" for r in runs)
    on_dve = ("rope", "glu")
    H = CONV_K // 2
    with Stage(nc, name) as s:
        wt, wp = s.sb("w", [P, 2, KT, P]), s.sb("wp", [P, 2, 2, KT, P], F32R)
        ob = s.sb("ob", [P, 2, N])
        if rope:
            cs = glu[0].rearrange("p a t -> p (a t)")[:, 0:2 * N].rearrange("p (a t) -> p a t", a=2)
            rot = s.sb("rot", [P, 2, W])
        if convs:
            nconv = sum(r[1] for r in runs if r[0] in ("conv", "conv_silu"))
            ub = s.sb("ub", [P, 2, N + TAPS - 1])
            cw, cb = s.sb("cw", [P, nconv, TAPS]), s.sb("cb", [P, nconv])
        if decays:
            reset = s.sb("reset", [P, N])
            ustored, absd, logf, cummed = s.sems("ustored", 2), s.sem("absd"), s.sem("logf"), s.sem("cummed")
        if glu:
            u, y = glu
            cw31, cb31 = s.sb("cw31", [P, 2, CONV_K]), s.sb("cb31", [P, 2])
        ps = s.ps("ps", [P, 2, SEQ])
        w_in, stored = s.sems("w_in", 2), s.sems("stored", 2)
        tab_in, mm_done, emptied, roped = s.sem("tab_in"), s.sem("mm_done"), s.sem("emptied"), s.sem("roped")
        swapped, turned, led, parted = s.sem("swapped"), s.sem("turned"), s.sem("led"), s.sem("parted")
        passed, ready, const_in, zeroed = s.sem("passed"), s.sem("ready"), s.sem("const_in"), s.sem("zeroed")
        conv, tapped, multiplied = s.sem("conv"), s.sem("tapped"), s.sem("multiplied")
        block = s.block()

        def tiles(eng, body, ahead=None, only=None):
            def tile(it, q, *rest, last=False):
                if ahead is not None and not last:
                    ahead(it + q, 1 - q)
                body(rest[0], it, q, *rest[1:])
            if ahead is not None:
                ahead(0, 0)
            at, nth = 0, {}
            for r, (kind, count, out, scale) in enumerate(runs):
                pairs = count // 2
                final = r == len(runs) - 1
                group = "conv" if kind == "conv_silu" else kind
                n0 = nth.get(group, 0)
                if only is None or group == only:
                    start = 0
                    if pairs or at == 0:
                        for q in range(min(2, count)):
                            tile(at, q, kind, q, out, n0 + q, scale, last=final and count == q + 1)
                        start = 1
                    end = pairs - (1 if final and count % 2 == 0 else 0)
                    if end > start:
                        with eng.Fori(start, end, 1) as i:
                            for q in range(2):
                                tile(i + at, q, kind, i * 2 + q, out, i * 2 + (n0 + q), scale)
                    if end < pairs and pairs > 1:
                        for q in range(2):
                            n = (pairs - 1) * 2 + q
                            tile(at + pairs - 1, q, kind, n, out, n0 + n, scale, last=q == 1)
                    if count % 2 and (at or count > 1):
                        tile(at + pairs, 0, kind, count - 1, out, n0 + count - 1, scale, last=True)
                at += pairs
                nth[group] = n0 + count

        @block.sync
        def _(sp):
            if convs:
                sp.dma_start(cw[:], taps4[0]).then_inc(const_in, 16)
                sp.dma_start(cb[:], taps4[1]).then_inc(const_in, 16)
            if glu:
                sp.dma_start(cw31[:], taps31[0]).then_inc(const_in, 16)
                sp.dma_start(cb31[:], taps31[1]).then_inc(const_in, 16)

            def load(kind, it, q, n, out, nth, scale):
                wait(sp, parted, it * 2 + (q - 1))
                sp.dma_start(wt[:, q], w[it * 2 + q]).then_inc(w_in[q], 16)
            tiles(sp, load)

        @block.tensor
        def _(pe):
            def products(kind, it, q, n, out, nth, scale):
                pe.wait_ge(parted, it * 2 + (q + 1))
                wait(pe, emptied, it * 2 + (q - 1))
                for c in range(NCH):
                    for n, (i, j) in enumerate(PARTS):
                        for k in range(KT):
                            mm = nc.tensor.matmul(ps[:, q, c * W:(c + 1) * W], wp[:, q, i, k], h[:, j, k, c * W:(c + 1) * W],
                                                  start=(n + k == 0), stop=(n == 2 and k == KT - 1))
                mm.then_inc(mm_done, 1)
            tiles(pe, products)

        @block.scalar
        def _(act):
            def lead(it, q):
                act.wait_ge(w_in[q], it * 16 + 16)
                wait(act, mm_done, it * 2 + (q - 1))
                nc.scalar.activation(wp[:, q, 0], wt[:, q], ACT.Copy).then_inc(led, 1)

            def empty(kind, it, q, n, out, nth, scale):
                t = it * 2 + q
                if kind in on_dve:
                    act.wait_ge(roped if kind == "rope" else multiplied, nth + 1)
                    wait(act, emptied, t)
                    act.sem_inc(emptied, 1)
                    wait(act, ready, t)
                    act.sem_inc(ready, 1)
                    return
                act.wait_ge(mm_done, t + 1)
                if kind == "decay":
                    act.wait_ge(stored[q], it * 16)
                    if not (isinstance(nth, int) and nth < 2):
                        act.wait_ge(ustored[q], (nth - q) // 2 * 16)
                    nc.scalar.activation(ob[:, q], ps[:, q, :N], ACT.Sigmoid, scale=-1.0)
                    e1 = ub[:, q, 0:N]
                    nc.scalar.activation(e1, ps[:, q, :N], ACT.Abs).then_inc(absd, 1)
                    for n, (fn, scale, bias) in enumerate(((ACT.Exp, -1.0, 0.0), (ACT.Ln, 1.0, 1.0))):
                        act.wait_ge(absd, nth * 3 + (n + 1))
                        nc.scalar.activation(e1, e1, fn, scale=scale, bias=bias).then_inc(absd, 1)
                    act.wait_ge(cummed, nth + 1)
                    wait(act, emptied, t)
                    act.sem_inc(emptied, 1)
                    wait(act, ready, t)
                    act.sem_inc(ready, 1)
                    return
                if kind == "sigmoid":
                    nc.scalar.activation(y[:, n], ps[:, q, :N], ACT.Sigmoid).then_inc(emptied, 1)
                elif kind in ("conv", "conv_silu"):
                    nc.scalar.activation(ub[:, q, TAPS - 1:], ps[:, q, :N], ACT.Copy).then_inc(emptied, 1)
                    act.wait_ge(conv, nth + 1)
                    if kind == "conv_silu":
                        nc.scalar.activation(ob[:, q], ob[:, q], ACT.Silu).then_inc(ready, 1)
                        return
                else:
                    if not (isinstance(it, int) and it <= kept):
                        act.wait_ge(stored[q], it * 16 - kept * 16)
                    nc.scalar.activation(ob[:, q], ps[:, q, :N], kind, scale=scale).then_inc(emptied, 1)
                act.wait_ge(emptied, t + 1)
                wait(act, ready, t)
                act.sem_inc(ready, 1)
            tiles(act, empty, lead)

        @block.vector
        def _(dve):
            ts, stt = nc.vector.tensor_scalar, nc.vector.scalar_tensor_tensor
            if convs:
                nc.vector.memset(ub[:, :, 0:TAPS - 1], 0.0).then_inc(zeroed, 1)
                dve.wait_ge(zeroed, 1)
                dve.wait_ge(const_in, 32)
            if glu:
                nc.vector.memset(u[:, :, 0:H], 0.0)
                nc.vector.memset(u[:, :, H + N:], 0.0).then_inc(zeroed, 1)

            def conv4(kind, it, q, n, out, nth, scale):
                dve.wait_ge(emptied, it * 2 + (q + 1))
                if not (isinstance(it, int) and it == 0):
                    dve.wait_ge(stored[q], it * 16)
                c = cw[:, ds(nth, 1), :].rearrange("p a k -> p (a k)")
                ts(ob[:, q], ub[:, q, 0:N], c[:, 0:1], cb[:, ds(nth, 1)], ALU.mult, ALU.add).then_inc(tapped, 1)
                for k in range(1, TAPS):
                    dve.wait_ge(tapped, nth * (TAPS - 1) + k)
                    stt(ob[:, q], ub[:, q, k:k + N], c[:, k:k + 1], ob[:, q], ALU.mult, ALU.add).then_inc(tapped if k < TAPS - 1 else conv, 1)
            if convs:
                tiles(dve, conv4, only="conv")

            def decay(kind, it, q, n, out, nth, scale):
                dve.wait_ge(absd, nth * 3 + 3)
                e1 = ub[:, q, 0:N]
                stt(e1, ps[:, q, :N], 0.0, e1, ALU.min, ALU.subtract).then_inc(logf, 1)
                dve.wait_ge(logf, nth + 1)
                nc.vector.tensor_tensor_scan(e1, reset[:], e1, 0.0, ALU.mult, ALU.add).then_inc(cummed, 1)
            if decays:
                nc.vector.memset(reset[:], 1.0).then_inc(zeroed, 1)
                dve.wait_ge(zeroed, 2)
                nc.vector.memset(reset[:].rearrange("p (c t) -> p c t", t=P)[:, :, 0:1], 0.0).then_inc(zeroed, 1)
                dve.wait_ge(zeroed, 3)
                tiles(dve, decay, only="decay")

            def multiply(kind, it, q, n, out, nth, scale):
                dve.wait_ge(mm_done, it * 2 + (q + 1))
                dve.wait_ge(emptied, nth + 1)
                nc.vector.tensor_tensor(u[:, nth, H:H + N], ps[:, q, :N], y[:, nth], ALU.mult).then_inc(multiplied, 1)
            if glu:
                tiles(dve, multiply, only="glu")
                dve.wait_ge(multiplied, 2)
                dve.wait_ge(zeroed, 1)
                dve.wait_ge(const_in, 32)
                for t in range(2):
                    ts(y[:, t], u[:, t, 0:N], cw31[:, t, 0:1], cb31[:, t:t + 1], ALU.mult, ALU.add).then_inc(tapped, 1)
                    for k in range(1, CONV_K):
                        dve.wait_ge(tapped, t * CONV_K + k)
                        stt(y[:, t], u[:, t, k:k + N], cw31[:, t, k:k + 1], y[:, t], ALU.mult, ALU.add).then_inc(tapped, 1)

            swap = [(i + 16) % 32 for i in range(32)]

            def turn(kind, it, q, n, out, nth, scale):
                dve.wait_ge(mm_done, it * 2 + (q + 1))
                if not (isinstance(it, int) and it <= kept):
                    dve.wait_ge(stored[q], it * 16 - kept * 16)
                for c in range(NCH):
                    cc = slice(c * W, (c + 1) * W)
                    m = nth * NCH + c
                    wait(dve, turned, m * 3 - 3)
                    nc.vector.stream_shuffle(rot[:, c % 2], ps[:, q, cc], swap).then_inc(swapped, 1)
                    stt(ob[:, q, cc], ps[:, q, cc], scale, cs[:, 0, cc], ALU.mult, ALU.mult).then_inc(turned, 1)
                    dve.wait_ge(swapped, m + 1)
                    stt(rot[:, c % 2], rot[:, c % 2], scale, cs[:, 1, cc], ALU.mult, ALU.mult).then_inc(turned, 1)
                    dve.wait_ge(turned, m * 3 + 2)
                    nc.vector.tensor_tensor(ob[:, q, cc], ob[:, q, cc], rot[:, c % 2], ALU.add).then_inc(turned, 1)
                dve.wait_ge(turned, nth * 3 * NCH + 3 * NCH)
                dve.sem_inc(roped, 1)
            if rope:
                dve.wait_ge(tab_in, 16)
                tiles(dve, turn, only="rope")

        @block.gpsimd
        def _(pool):
            def rest(it, q):
                wait_apart(pool, led, it * 2 + (q + 1), passed)
                pool.tensor_tensor(wp[:, q, 1], wt[:, q], wp[:, q, 0].bitcast(F32), ALU.subtract).then_inc(parted, 1)

            def store(kind, it, q, n, out, nth, scale):
                if kind == "rope" and isinstance(nth, int) and nth == 0:
                    pool.wait_ge(tapped, 2 * CONV_K)
                    pool.dma_start(cs, tables.rearrange("a p t -> p a t")).then_inc(tab_in, 16)
                if out is None:
                    return
                wait_apart(pool, ready, it * 2 + (q + 1), passed)
                if kind == "decay":
                    pool.dma_start(out[0][n], ob[:, q]).then_inc(stored[q], 16)
                    pool.dma_start(out[1][n], ub[:, q, 0:N]).then_inc(ustored[q], 16)
                    return
                pool.dma_start(out[n], ob[:, q]).then_inc(stored[q], 16)
            tiles(pool, store, rest)
            for q in range(2):
                if decays:
                    pool.wait_ge(ustored[q], 16 * (sum(r[1] for r in runs if r[0] == "decay") // 2))
                if (total + 1 - q) // 2 > kept:
                    pool.wait_ge(stored[q], 16 * ((total + 1 - q) // 2 - kept))


def project_tokens(nc, name, h, N, w, NW, outs):
    NT = N // P
    with Stage(nc, name) as s:
        wt, wp = s.sb("w", [P, KT, NW]), s.sb("wp", [P, 2, KT, NW], F32R)
        ob = s.sb("ob", [P, 4, NW])
        ps = s.ps("ps", [P, 4, CH])
        w_in, led, parted, mm_done, emptied = (s.sem(x) for x in ("w_in", "led", "parted", "mm_done", "emptied"))
        stored = s.sems("stored", 4)
        block = s.block()

        @block.sync
        def _(sp):
            sp.dma_start(wt[:], w).then_inc(w_in, 16)
            for t in range(NT):
                sp.wait_ge(emptied, t + 1)
                for out, c0, n in outs:
                    sp.dma_start(out[t], ob[:, t % 4, c0:c0 + n]).then_inc(stored[t % 4], 16)
            for q in range(min(4, NT)):
                sp.wait_ge(stored[q], 16 * len(outs) * ((NT + 3 - q) // 4))

        @block.vector
        def _(dve):
            for k in range(KT):
                dve.wait_ge(led, k + 1)
                nc.vector.tensor_tensor(wp[:, 1, k], wt[:, k], wp[:, 0, k].bitcast(F32), ALU.subtract).then_inc(parted, 1)

        @block.tensor
        def _(pe):
            for t in range(NT):
                if t >= 4:
                    pe.wait_ge(emptied, t - 3)
                for n, (i, j) in enumerate(PARTS):
                    for k in range(KT):
                        if t == 0 and n == 0:
                            pe.wait_ge(parted, k + 1)
                        mm = nc.tensor.matmul(ps[:, t % 4, :NW], h[:, j, k, t * P:(t + 1) * P], wp[:, i, k],
                                              start=(n + k == 0), stop=(n == 2 and k == KT - 1))
                mm.then_inc(mm_done, 1)

        @block.scalar
        def _(act):
            act.wait_ge(w_in, 16)
            for k in range(KT):
                nc.scalar.activation(wp[:, 0, k], wt[:, k], ACT.Copy).then_inc(led, 1)
            for t in range(NT):
                act.wait_ge(mm_done, t + 1)
                if t >= 4:
                    act.wait_ge(stored[t % 4], 16 * len(outs) * (t // 4))
                nc.scalar.activation(ob[:, t % 4], ps[:, t % 4, :NW], ACT.Copy).then_inc(emptied, 1)



def attention(nc, name, N, q_d, kc_d, vc_d, sink_d, gate_d, out_d, k_d=None, v_d=None, mask_d=None):
    NB = N // P
    win = k_d is not None
    NW = 3 if win else 0
    NT = NW + 2
    NK = NT * P
    U = 2 * NT
    with Stage(nc, name) as s:
        qb, gb, ob = s.sb("q", [P, 2, 4, P]), s.sb("g", [P, 2, 4, P]), s.sb("o", [P, 2, 4, P])
        kc, vc = s.sb("kc", [P, CTX]), s.sb("vc", [P, 2, P])
        if win:
            kw, vw = s.sb("kw", [P, 2, 3 * P]), s.sb("vw", [P, 2, 3, P])
            idb, mk, mkf = s.sb("idb", [P, P], BF16), s.sb("mk", [P, 3, P], BF16), s.sb("mkf", [P, 3, P])
            masks_in = s.sem("masks_in")
        ident, ones, sink = s.sb("ident", [P, P]), s.sb("ones", [1, P]), s.sb("sink", [1, NH])
        prob = s.sb("prob", [P, 2, NH, NK + 1])
        pT = s.sb("pT", [P, 4, 4 * P])
        nmax, den, rden = s.sb("nmax", [P, 2, NH]), s.sb("den", [P, 2, NH]), s.sb("rden", [P, 2, NH])
        psS = s.ps("S", [P, 2, 2 * CH])
        psT = s.ps("T", [P, 2, CH])
        psO = s.ps("O", [P, 2, CH])
        const_in, const = s.sem("const_in"), s.sem("const")
        qk_in, vg_in, stored = s.sems("qk_in", 2), s.sems("vg_in", 2), s.sems("stored", 2)
        scored, maxed, expd, inverted, normed = (s.sem(x) for x in ("scored", "maxed", "expd", "inverted", "normed"))
        turned, movedD, movedA, summed, gated = (s.sem(x) for x in ("turned", "movedD", "movedA", "summed", "gated"))
        block = s.block()
        NQK, NVG = (2, 2) if win else (1, 1)

        def pipeline(eng, first, body):
            for hh in range(NH):
                first(hh)
            body(0, 0, NB == 1)
            body(1, 1, NB == 2)
            if NB > 4:
                with eng.Fori(1, NB // 2 - 1, 1) as i:
                    for q in range(2):
                        body(i * 2 + q, q, False)
            if NB > 2:
                body(NB - 2, 0, False)
                body(NB - 1, 1, True)

        def rounds(b, q, last, head, unit):
            for u in range(max(NH, U + 1)):
                if u < NH and not last:
                    head(b + 1, 1 - q, u)
                if u <= U:
                    unit(b, q, u)

        def half(b, q):
            return b // 2 if isinstance(b, int) else (b - q) // 2

        @block.sync
        def _(sp):
            sp.dma_start(kc[:], kc_d).then_inc(const_in, 16)
            sp.dma_start(vc[:], vc_d.rearrange("t p d -> p t d")).then_inc(const_in, 16)
            sp.dma_start(sink[:], sink_d).then_inc(const_in, 16)
            if win:
                sp.dma_start(mkf[:], mask_d).then_inc(masks_in, 16)

            def load(b, q):
                at = ds(b * P, P)
                wait(sp, scored, (b - 1) * NH)
                sp.dma_start(qb[:, q], q_d[:, :, at].rearrange("j p t -> p j t")).then_inc(qk_in[q], 16)
                if win:
                    sp.dma_start(kw[:, q], k_d[:, ds(b * P, 3 * P)]).then_inc(qk_in[q], 16)
                wait(sp, gated, b - 1)
                if win:
                    sp.dma_start(vw[:, q], v_d[ds(b, 3)].rearrange("t p d -> p t d")).then_inc(vg_in[q], 16)
                sp.dma_start(gb[:, q], gate_d[:, :, at].rearrange("j p t -> p j t")).then_inc(vg_in[q], 16)
            steps(sp, NB, load)

        @block.gpsimd
        def _(pool):
            pool.memset(ident[:], 0.0).then_inc(const, 1)
            pool.wait_ge(const, 1)
            pool.affine_select(out=ident[:], in_=ident[:], compare_op=ALU.not_equal, fill=1.0, base=0,
                               pattern=[[-1, P]], channel_multiplier=1).then_inc(const, 1)
            pool.memset(ones[:], 1.0).then_inc(const, 1)
            if win:
                pool.wait_ge(const, 3)
                pool.tensor_copy(idb[:], ident[:]).then_inc(const, 1)
                pool.wait_ge(masks_in, 16)
                pool.tensor_copy(mk[:], mkf[:]).then_inc(const, 1)

            def store(b, q):
                pool.wait_ge(gated, b + 1)
                pool.dma_start(out_d[:, :, ds(b * P, P)].rearrange("j p t -> p j t"), ob[:, q]).then_inc(stored[q], 16)
            steps(pool, NB, store)
            for q in range(2):
                pool.wait_ge(stored[q], 16 * (NB // 2))

        @block.tensor
        def _(pe):
            pe.wait_ge(const, 5 if win else 3)
            pe.wait_ge(const_in, 48)

            def scores(b, q, hh):
                if hh == 0:
                    pe.wait_ge(qk_in[q], half(b, q) * 16 * NQK + 16 * NQK)
                j, g = hh // 2, hh % 2
                rows = slice(g * HD, g * HD + HD)
                S = psS[:, hh % 2]
                wait(pe, expd, b * NH + (hh - 1))
                lhs = qb[rows, q, j]
                c = 0
                nc.tensor.matmul(S[:, 0:CTX], lhs, kc[rows, :], start=True, stop=True)
                c = CTX
                if win:
                    nc.tensor.matmul(S[:, c:c + 2 * P], lhs, kw[rows, q, 0:2 * P], start=True, stop=False)
                    nc.tensor.matmul(S[:, c:c + P], idb[:], mk[:, 2 if isinstance(b, int) and b == 0 else 0], start=False, stop=True)
                    c = CH
                    nc.tensor.matmul(S[:, c:c + P], lhs, kw[rows, q, 2 * P:3 * P], start=True, stop=False)
                    nc.tensor.matmul(S[:, c:c + P], idb[:], mk[:, 2 if isinstance(b, int) and b == NB - 1 else 1], start=False, stop=True)
                    c = CH + P
                h = g * GQ + j
                nc.tensor.matmul(S[:, c:c + 1], ones[:], sink[:, h:h + 1], start=True, stop=True).then_inc(scored, 1)

            def values(b, q, u):
                if u == 0:
                    pe.wait_ge(normed, b * NH + NH)
                if u < U:
                    kt, g = u // 2, u % 2
                    wait(pe, (movedD, movedA)[g], b * NT + kt)
                    for j in range(4):
                        tr = nc.tensor.transpose(psT[:, g, j * P:(j + 1) * P], prob[:, q, 2 * j + g, kt * P:(kt + 1) * P], ident[:])
                    tr.then_inc(turned, 1)
                if u == 1:
                    pe.wait_ge(vg_in[q], half(b, q) * 16 * NVG + 16 * NVG)
                    wait(pe, gated, b - 1)
                if u >= 1:
                    kt, g = (u - 1) // 2, (u - 1) % 2
                    cols = slice(g * HD, g * HD + HD)
                    val = vc[:, kt, cols] if kt < 2 else vw[:, q, kt - 2, cols]
                    pe.wait_ge((movedD, movedA)[g], b * NT + (kt + 1))
                    nc.tensor.matmul(psO[cols, q], val, pT[:, (U * q + u - 1) % 4], start=(kt == 0),
                                     stop=(kt == NT - 1)).then_inc(summed, 1)
            pipeline(pe, lambda hh: scores(0, 0, hh), lambda b, q, last: rounds(b, q, last, scores, values))

        def move(eng, b, q, u, op, moved):
            eng.wait_ge(turned, b * U + (u + 1))
            wait(eng, summed, b * U + (u - 3))
            op(pT[:, (U * q + u) % 4], psT[:, u % 2]).then_inc(moved, 1)

        @block.scalar
        def _(act):
            def exps(b, q, hh):
                if hh == 0:
                    wait(act, turned, (b - 1) * U)
                act.wait_ge(maxed, b * NH + (hh + 1))
                nc.scalar.activation(prob[:, q, hh], psS[:, hh % 2, 0:NK + 1], ACT.Exp, bias=nmax[:, q, hh:hh + 1],
                                     accum_out=den[:, q, hh:hh + 1]).then_inc(expd, 1)

            def moves(b, q, u):
                if u % 2 and u < U:
                    move(act, b, q, u, nc.scalar.copy, movedA)
            pipeline(act, lambda hh: exps(0, 0, hh), lambda b, q, last: rounds(b, q, last, exps, moves))

        @block.vector
        def _(dve):
            def norms(b, q, hh):
                dve.wait_ge(expd, b * NH + (hh + 1))
                nc.vector.reciprocal(rden[:, q, hh:hh + 1], den[:, q, hh:hh + 1]).then_inc(inverted, 1)
                dve.wait_ge(inverted, b * NH + (hh + 1))
                nc.vector.tensor_scalar(prob[:, q, hh, 0:NK], prob[:, q, hh, 0:NK], rden[:, q, hh:hh + 1], None,
                                        ALU.mult).then_inc(normed, 1)

            def heads(b, q, hh):
                dve.wait_ge(scored, b * NH + (hh + 1))
                nc.vector.tensor_reduce(nmax[:, q, hh:hh + 1], psS[:, hh % 2, 0:NK + 1], AX.X, ALU.max,
                                        negate=True).then_inc(maxed, 1)
                if hh >= 1:
                    norms(b, q, hh - 1)
                if hh == NH - 1:
                    norms(b, q, hh)

            def gates(b, q):
                dve.wait_ge(summed, b * U + U)
                if not (isinstance(b, int) and b < 2):
                    dve.wait_ge(stored[q], half(b, q) * 16)
                nc.vector.tensor_tensor(ob[:, q].rearrange("p j t -> p (j t)"), psO[:, q],
                                        gb[:, q].rearrange("p j t -> p (j t)"), ALU.mult).then_inc(gated, 1)

            def moves(b, q, u):
                if u % 2 == 0 and u < U:
                    move(dve, b, q, u, nc.vector.tensor_copy, movedD)
                if u == 0 and not (isinstance(b, int) and b == 0):
                    gates(b - 1, 1 - q)

            def body(b, q, last):
                rounds(b, q, last, heads, moves)
                if last:
                    gates(b, q)
            pipeline(dve, lambda hh: heads(0, 0, hh), body)



def fourier(nc, name, N, u_d, tab_d, headtab_d, wf_d, bf_d, gate_d, out_d):
    R = N // P
    W = min(CH, N)
    NCH = N // W
    C2 = 2 * P
    half = R // 2
    with Stage(nc, name) as s:
        u = s.sb("u", [P, R, C2])
        gr = s.sb("gr", [P, half + 1, C2])
        gi = s.sb("gi", [P, half + 1, C2]) if R > 2 else None
        tab = s.sb("tab", [P, 2, 2, 2 * P])
        ht, wf, bf = s.sb("ht", [P, 2, P]), s.sb("wf", [P, 2, C2]), s.sb("bf", [P, 2])
        wcs = s.sb("wcs", [P, 2, 2, C2])
        ab = s.sb("ab", [P, 2, 2, N])
        if R > 2:
            t8 = s.sb("t8", [P, 16, C2])
            t4 = s.sb("t4", [P, 8, C2])
            pq = s.sb("pq", [P, 6, C2])
        gate, ob = s.sb("gate", [P, 2, N]), s.sb("ob", [P, 2, 2, CH])
        psA = s.ps("A", [P, 4, CH])
        psW = s.ps("W", [P, 4, CH])
        u_in, const_in, gate_in = s.sem("u_in"), s.sem("const_in"), s.sem("gate_in")
        tab_in, stored = s.sems("tab_in", 2), s.sems("stored", 2)
        chain, bins, prod, wdone, wmoved = (s.sem(x) for x in ("chain", "bins", "prod", "wdone", "wmoved"))
        moved, mixed, gated = s.sem("moved"), s.sem("mixed"), s.sem("gated")
        block = s.block()
        NORM = 1.0 / np.sqrt(N * FH)

        @block.sync
        def _(sp):
            sp.dma_start(u[:], u_d.rearrange("r p c -> p r c")).then_inc(u_in, 16)
            sp.dma_start(ht[:], headtab_d).then_inc(const_in, 16)
            sp.dma_start(wf[:], wf_d.rearrange("(a p) n -> p a n", p=P)).then_inc(const_in, 16)
            sp.dma_start(bf[:], bf_d).then_inc(const_in, 16)

            def load(b, q):
                wait(sp, prod, b - 1)
                sp.dma_start(tab[:, q], tab_d[b].rearrange("p (a c) -> p a c", a=2)).then_inc(tab_in[q], 16)
            for b in range(2):
                load(b, b)
            sp.dma_start(gate[:], gate_d.rearrange("a p t -> p a t")).then_inc(gate_in, 16)
            for b in range(2, R):
                load(b, b % 2)
            for c in range(NCH):
                for m in range(2):
                    n = 2 * c + m
                    sp.wait_ge(gated, n + 1)
                    sp.dma_start(out_d[m, :, c * W:(c + 1) * W], ob[:, c % 2, m, :W]).then_inc(stored[c % 2], 16)
            for q in range(min(2, NCH)):
                sp.wait_ge(stored[q], 32 * ((NCH + 1 - q) // 2))

        @block.vector
        def _(dve):
            n = [0]

            def step(ins):
                n[0] += 1
                ins.then_inc(chain, 1)

            def settle():
                dve.wait_ge(chain, n[0])

            dve.wait_ge(u_in, 16)
            tt, stt, ts = nc.vector.tensor_tensor, nc.vector.scalar_tensor_tensor, nc.vector.tensor_scalar
            add, sub, mul = ALU.add, ALU.subtract, ALU.mult
            if R == 2:
                tt(gr[:, 0], u[:, 0], u[:, 1], add).then_inc(bins, 1)
                tt(gr[:, 1], u[:, 0], u[:, 1], sub).then_inc(bins, 1)
            else:
                step(tt(t8[:, 0:8], u[:, 0:8], u[:, 8:16], add))
                step(tt(t8[:, 8:16], u[:, 0:8], u[:, 8:16], sub))
                settle()
                step(tt(t4[:, 0:4], t8[:, 0:4], t8[:, 4:8], add))
                step(tt(t4[:, 4:8], t8[:, 0:4], t8[:, 4:8], sub))
                for m in (1, 2, 3):
                    step(tt(pq[:, m - 1], t8[:, 8 + m], t8[:, 16 - m], sub))
                    step(tt(pq[:, m + 2], t8[:, 8 + m], t8[:, 16 - m], add))
                settle()
                c, d = (lambda m: t4[:, m]), (lambda m: t4[:, 4 + m])
                step(tt(t8[:, 0], c(0), c(2), add))
                step(tt(t8[:, 1], c(1), c(3), add))
                step(tt(gr[:, 4], c(0), c(2), sub))
                step(tt(gi[:, 4], c(3), c(1), sub))
                step(tt(t8[:, 2], d(1), d(3), sub))
                step(tt(t8[:, 3], d(1), d(3), add))
                settle()
                r = float(np.sqrt(0.5))
                step(tt(gr[:, 0], t8[:, 0], t8[:, 1], add))
                step(tt(gr[:, 8], t8[:, 0], t8[:, 1], sub))
                step(stt(gr[:, 2], t8[:, 2], r, d(0), mul, add))
                step(stt(gr[:, 6], t8[:, 2], -r, d(0), mul, add))
                step(stt(gi[:, 2], t8[:, 3], -r, d(2), mul, sub))
                step(stt(gi[:, 6], t8[:, 3], -r, d(2), mul, add))
                for m in (1, 2, 3):
                    for k in (1, 3, 5, 7):
                        co, si = float(np.cos(np.pi * m * k / 8)), float(np.sin(np.pi * m * k / 8))
                        step(stt(gr[:, k], pq[:, m - 1], co, t8[:, 8] if m == 1 else gr[:, k], mul, add))
                        s4 = int(round(np.sin(np.pi * k / 2)))
                        if m == 1:
                            step(stt(gi[:, k], pq[:, m + 2], -si, t8[:, 12], mul, sub if s4 > 0 else add))
                        else:
                            step(stt(gi[:, k], pq[:, m + 2], -si, gi[:, k], mul, add))
                    settle()
                dve.engine_nop().then_inc(bins, 2)
            for b in range(1, R, 2):
                dve.wait_ge(prod, b + 1)
                for ct in range(2):
                    last = nc.vector.tensor_copy(ab[:, ct].rearrange("p a (k r) -> p a k r", r=R)[:, :, :, b],
                                                 psA[:, 2 + ct, 0:2 * P].rearrange("p (a k) -> p a k", a=2))
                last.then_inc(moved, 1)
            dve.wait_ge(gate_in, 16)
            dve.wait_ge(const_in, 48)
            for c in range(NCH):
                for m in range(2):
                    k = 2 * c + m
                    dve.wait_ge(mixed, k + 1)
                    if c >= 2:
                        dve.wait_ge(stored[c % 2], 32 * (c // 2))
                    stt(ob[:, c % 2, m, :W], psW[:, k % 4, :W], bf[:, m:m + 1], gate[:, m, c * W:(c + 1) * W], add, mul).then_inc(gated, 1)

        @block.scalar
        def _(act):
            act.wait_ge(wdone, 1)
            for cs in range(2):
                for ct in range(2):
                    last = nc.scalar.activation(wcs[:, cs, ct], psW[:, 2 * cs + ct, 0:C2], ACT.Copy,
                                                scale=float(NORM if cs == 0 else -NORM))
            last.then_inc(wmoved, 1)
            for b in range(0, R, 2):
                act.wait_ge(prod, b + 1)
                for ct in range(2):
                    last = nc.scalar.copy(ab[:, ct].rearrange("p a (k r) -> p a k r", r=R)[:, :, :, b],
                                          psA[:, ct, 0:2 * P].rearrange("p (a k) -> p a k", a=2))
                last.then_inc(wmoved, 1)

        @block.tensor
        def _(pe):
            pe.wait_ge(const_in, 48)
            for cs in range(2):
                for ct in range(2):
                    mm = nc.tensor.matmul(psW[:, 2 * cs + ct, 0:C2], ht[:, cs], wf[:, ct], start=True, stop=True)
            mm.then_inc(wdone, 1)
            pe.wait_ge(bins, 2)
            for b in range(R):
                k, real = min(b, R - b), b in (0, half)
                pe.wait_ge(tab_in[b % 2], 16 * (b // 2 + 1))
                if b >= 2:
                    pe.wait_ge(wmoved if b % 2 == 0 else moved, b // 2 + (1 if b % 2 == 0 else 0))
                for ct in range(2):
                    o = psA[:, 2 * (b % 2) + ct, 0:2 * P]
                    mm = nc.tensor.matmul(o, gr[:, k, ct * P:(ct + 1) * P], tab[:, b % 2, 0], start=True, stop=real)
                    if not real:
                        mm = nc.tensor.matmul(o, gi[:, k, ct * P:(ct + 1) * P], tab[:, b % 2, 1], start=False, stop=True)
                mm.then_inc(prod, 1)
            pe.wait_ge(wmoved, 1 + (R + 1) // 2)
            pe.wait_ge(moved, R // 2)
            for c in range(NCH):
                for m in range(2):
                    k = 2 * c + m
                    if k >= 4:
                        pe.wait_ge(gated, k - 3)
                    for i in range(4):
                        ct, cs = i // 2, i % 2
                        mm = nc.tensor.matmul(psW[:, k % 4, :W], wcs[:, cs, ct, m * P:(m + 1) * P], ab[:, ct, cs, c * W:(c + 1) * W],
                                              start=(i == 0), stop=(i == 3))
                    mm.then_inc(mixed, 1)



def conformer(nc, name, N, y, lg_d, lb_d, gate_d, out_d):
    W = min(CH, N)
    NCH = N // W
    with Stage(nc, name) as s:
        sg = s.sb("sg", [P, 2, N])
        sq, xh = s.sb("sq", [P, 2, 2, CH]), s.sb("xh", [P, 2, 2, CH])
        par = s.sb("par", [P, 3, 2])
        ones, eps = s.sb("ones", [P, P]), s.sb("eps", [P, 1])
        root, rstd = s.sb("root", [P, 2, CH]), s.sb("rstd", [P, 2, CH])
        psM, psV = s.ps("M", [P, 2, CH]), s.ps("V", [P, 2, CH])
        g_in, const_in, stored = s.sem("g_in"), s.sem("const_in"), s.sem("stored")
        chain, const, mean, centred, squared, var, rooted, scaled, silued, gated = (
            s.sem(x) for x in ("chain", "const", "mean", "centred", "squared", "var", "rooted", "scaled", "silued", "gated"))
        block = s.block()

        @block.sync
        def _(sp):
            for i, v in enumerate((lg_d, lb_d)):
                sp.dma_start(par[:, i + 1], v).then_inc(const_in, 16)
            sp.dma_start(sg[:], gate_d.rearrange("a p t -> p a t")).then_inc(g_in, 16)
            for c in range(NCH):
                sp.wait_ge(gated, c + 1)
                sp.dma_start(out_d[:, :, c * W:(c + 1) * W].rearrange("a p t -> p a t"), y[:, :, c * W:(c + 1) * W]).then_inc(stored, 16)
            sp.wait_ge(stored, 16 * NCH)

        @block.vector
        def _(dve):
            n = [0]

            def step(ins):
                n[0] += 1
                ins.then_inc(chain, 1)
                dve.wait_ge(chain, n[0])

            nc.vector.memset(ones[:], 1.0 / (2 * P))
            step(nc.vector.memset(eps[:], EPS))
            dve.engine_nop().then_inc(const, 1)
            dve.wait_ge(const_in, 32)
            dve.wait_ge(g_in, 16)
            def centre(c):
                cc = slice(c * W, (c + 1) * W)
                dve.wait_ge(mean, c + 1)
                for t in range(2):
                    last = nc.vector.tensor_tensor(y[:, t, cc], y[:, t, cc], psM[:, c % 2, :W], ALU.subtract)
                last.then_inc(centred, 1)

            def apply_gate(c):
                cc = slice(c * W, (c + 1) * W)
                dve.wait_ge(silued, c + 1)
                for t in range(2):
                    last = nc.vector.tensor_tensor(y[:, t, cc], xh[:, c % 2, t, :W], sg[:, t, cc], ALU.mult)
                last.then_inc(gated, 1)

            centre(0)
            for c in range(NCH):
                cc = slice(c * W, (c + 1) * W)
                if c + 1 < NCH:
                    centre(c + 1)
                dve.wait_ge(rooted, c + 1)
                step(nc.vector.reciprocal(rstd[:, c % 2, :W], root[:, c % 2, :W]))
                wait(dve, gated, c - 1)
                for t in range(2):
                    last = nc.vector.scalar_tensor_tensor(xh[:, c % 2, t, :W], y[:, t, cc], par[:, 1, t:t + 1], rstd[:, c % 2, :W], ALU.mult, ALU.mult)
                last.then_inc(scaled, 1)
                if c >= 1:
                    apply_gate(c - 1)
            apply_gate(NCH - 1)

        @block.tensor
        def _(pe):
            pe.wait_ge(const, 1)

            def means(c):
                wait(pe, centred, c - 1)
                for t in range(2):
                    mm = nc.tensor.matmul(psM[:, c % 2, :W], ones[:], y[:, t, c * W:(c + 1) * W], start=(t == 0), stop=(t == 1))
                mm.then_inc(mean, 1)

            means(0)
            for c in range(NCH):
                if c + 1 < NCH:
                    means(c + 1)
                pe.wait_ge(squared, c + 1)
                wait(pe, rooted, c - 1)
                for t in range(2):
                    mm = nc.tensor.matmul(psV[:, c % 2, :W], ones[:], sq[:, c % 2, t, :W], start=(t == 0), stop=(t == 1))
                mm.then_inc(var, 1)

        @block.scalar
        def _(act):
            act.wait_ge(const, 1)
            act.wait_ge(const_in, 32)

            def square(c):
                act.wait_ge(centred, c + 1)
                wait(act, var, c - 1)
                for t in range(2):
                    last = nc.scalar.activation(sq[:, c % 2, t, :W], y[:, t, c * W:(c + 1) * W], ACT.Square)
                last.then_inc(squared, 1)

            square(0)
            for c in range(NCH):
                if c + 1 < NCH:
                    square(c + 1)
                act.wait_ge(var, c + 1)
                wait(act, scaled, c - 1)
                nc.scalar.activation(root[:, c % 2, :W], psV[:, c % 2, :W], ACT.Sqrt, bias=eps[:, 0:1]).then_inc(rooted, 1)
                act.wait_ge(scaled, c + 1)
                for t in range(2):
                    last = nc.scalar.activation(xh[:, c % 2, t, :W], xh[:, c % 2, t, :W], ACT.Silu, bias=par[:, 2, t:t + 1])
                last.then_inc(silued, 1)



def project_out(nc, name, N, y_d, w_d, gate, x_d, out_d, KY):
    W = min(CH, N)
    NN = min(N, SEQ * 4 // KY)
    NH2 = N // NN
    NCH = NN // W
    G = KY // 4
    NP = NCH * G
    with Stage(nc, name) as s:
        yr, y = s.sb("yr", [P, 2, 4, W]), s.sb("y", [P, 2, 2, NP, 4, W], F32R)
        wt, wp = s.sb("w", [P, 2, KY, P]), s.sb("wp", [P, 2, 2, KY, P], F32R)
        xb = s.sb("x", [P, 2, NN])
        ps = s.ps("ps", [P, 2, SEQ])
        w_in, y_in, x_in, stored = s.sems("w_in", 2), s.sems("y_in", 2), s.sems("x_in", 2), s.sems("stored", 2)
        yled, yparted, led, parted = s.sem("yled"), s.sem("yparted"), s.sem("led"), s.sem("parted")
        mm_done, added, passed = s.sem("mm_done"), s.sem("added"), s.sem("passed")
        block = s.block()

        def parts(eng, piece, tile, weights=None):
            def whole(hf, i, q):
                t = KT * hf + 2 * i + q
                if weights is not None and t:
                    weights(t, i, q)
                tile(hf, i, q)

            if weights is not None:
                weights(0, 0, 0)
            for p in range(NP):
                piece(0, p)
            for hf in range(NH2):
                for i in range(KT // 2):
                    whole(hf, i, 0)
                    if hf + 1 < NH2:
                        piece(hf + 1, i)
                    whole(hf, i, 1)
        assert NH2 == 1 or NP == KT // 2

        @block.sync
        def _(sp):
            def piece(hf, p):
                n = NP * hf + p
                wait(sp, yled, n - 1)
                wait(sp, yparted, n - 1)
                k, t = p % G * 4, hf * NN + p // G * W
                sp.dma_start(yr[:, n % 2], y_d[k:k + 4, :, t:t + W].rearrange("k p t -> p k t")).then_inc(y_in[n % 2], 16)

            def weights(t, i, q):
                wait(sp, parted, t - 1)
                sp.dma_start(wt[:, q], w_d[i * 2 + q]).then_inc(w_in[q], 16)

            def tile(hf, i, q):
                t = KT * hf + 2 * i + q
                wait(sp, stored[q], t // 2 * 16)
                sp.dma_start(xb[:, q], x_d[i * 2 + q, :, hf * NN:(hf + 1) * NN]).then_inc(x_in[q], 16)
            parts(sp, piece, tile, weights)

        @block.scalar
        def _(act):
            def piece(hf, p):
                n = NP * hf + p
                act.wait_ge(y_in[n % 2], 16 * (n // 2 + 1))
                wait(act, mm_done, KT * (hf - 1))
                nc.scalar.activation(y[:, hf % 2, 0, p], yr[:, n % 2], ACT.Copy).then_inc(yled, 1)

            def weights(t, i, q):
                act.wait_ge(w_in[q], 16 * (t // 2 + 1))
                wait(act, mm_done, t - 1)
                nc.scalar.activation(wp[:, q, 0], wt[:, q], ACT.Copy).then_inc(led, 1)
            parts(act, piece, lambda hf, i, q: None, weights)

        @block.gpsimd
        def _(pool):
            def tile(hf, i, q):
                t = KT * hf + 2 * i + q
                wait_apart(pool, led, t + 1, passed)
                pool.tensor_tensor(wp[:, q, 1], wt[:, q], wp[:, q, 0].bitcast(F32), ALU.subtract).then_inc(parted, 1)
                if t >= 1:
                    store(t - 1)

            def store(t):
                hf, n = t // KT, t % KT
                wait_apart(pool, added, t + 1, passed)
                pool.dma_start(out_d[n, :, hf * NN:(hf + 1) * NN], xb[:, t % 2]).then_inc(stored[t % 2], 16)
            parts(pool, lambda hf, p: None, tile)
            store(KT * NH2 - 1)
            for q in range(2):
                pool.wait_ge(stored[q], 16 * (KT // 2) * NH2)

        @block.tensor
        def _(pe):
            def tile(hf, i, q):
                t = KT * hf + 2 * i + q
                pe.wait_ge(parted, t + 1)
                wait(pe, added, t - 1)
                for c in range(NCH):
                    if i + q == 0:
                        pe.wait_ge(yparted, NP * hf + (c + 1) * G)
                    for n, (a, b) in enumerate(PARTS):
                        for k in range(KY):
                            mm = nc.tensor.matmul(ps[:, q, c * W:(c + 1) * W], wp[:, q, a, k], y[:, hf % 2, b, c * G + k // 4, k % 4],
                                                  start=(n + k == 0), stop=(n == 2 and k == KY - 1))
                mm.then_inc(mm_done, 1)
            parts(pe, lambda hf, p: None, tile)

        @block.vector
        def _(dve):
            def piece(hf, p):
                n = NP * hf + p
                dve.wait_ge(yled, n + 1)
                nc.vector.tensor_tensor(y[:, hf % 2, 1, p], yr[:, n % 2], y[:, hf % 2, 0, p].bitcast(F32), ALU.subtract).then_inc(yparted, 1)

            def tile(hf, i, q):
                t = KT * hf + 2 * i + q
                dve.wait_ge(mm_done, t + 1)
                dve.wait_ge(x_in[q], (t // 2 + 1) * 16)
                nc.vector.scalar_tensor_tensor(xb[:, q], ps[:, q, :NN], gate[:, i * 2 + q:i * 2 + q + 1], xb[:, q],
                                               ALU.mult, ALU.add).then_inc(added, 1)
            parts(dve, piece, tile)



def lru(nc, name, x_d, wa_d, ba_d, wx_d, bx_d, lam_d, gate_d, out_d):
    N, NT = SEQ, LW // P
    NCH = N // CH
    with Stage(nc, name) as s:
        x2 = s.sb("x", [P, 2, N])
        rs, ivs, as_, ts_, ms = (s.sb(n, [P, 2, N]) for n in ("r", "i", "a", "t", "m"))
        gate, ob = s.sb("gate", [P, 2, N]), s.sb("ob", [P, 2, N])
        wa, wx, par = s.sb("wa", [P, NT, P]), s.sb("wx", [P, NT, P]), s.sb("par", [P, 3, NT])
        dec, z = s.sb("dec", [P, 2, NT]), s.sb("z", [P, 6, NT])
        ps = s.ps("ps", [P, 2, SEQ])
        const_in, zeroed, chain, small = s.sem("const_in"), s.sem("zeroed"), s.sem("chain"), s.sem("small")
        u_in, g_in, stored = s.sems("u_in", 2), s.sems("g_in", 2), s.sems("stored", 2)
        gates, sig, expd, squared, summed, rooted, scanned = (
            s.sem(n) for n in ("gates", "sig", "expd", "squared", "summed", "rooted", "scanned"))
        block = s.block()

        @block.sync
        def _(sp):
            for dst, src in ((wa, wa_d), (wx, wx_d)):
                sp.dma_start(dst[:], src).then_inc(const_in, 16)
            for i, v in enumerate((ba_d, bx_d, lam_d)):
                sp.dma_start(par[:, i], v).then_inc(const_in, 16)

            def store(k):
                sp.wait_ge(scanned, k + 1)
                sp.dma_start(out_d[k], ob[:, k % 2]).then_inc(stored[k % 2], 16)

            for k in range(NT):
                if k >= 2:
                    store(k - 2)
                sp.dma_start(x2[:, k % 2], x_d[k]).then_inc(u_in[k % 2], 16)
                sp.dma_start(gate[:, k % 2], gate_d[k]).then_inc(g_in[k % 2], 16)
            store(NT - 2)
            store(NT - 1)
            for q in range(2):
                sp.wait_ge(stored[q], 16 * (NT // 2))

        @block.vector
        def _(dve):
            n = [0]

            def step(ins):
                n[0] += 1
                ins.then_inc(chain, 1)
                dve.wait_ge(chain, n[0])

            ts, tt, stt = nc.vector.tensor_scalar, nc.vector.tensor_tensor, nc.vector.scalar_tensor_tensor
            dve.wait_ge(const_in, 16 * 5)
            dve.wait_ge(small, 1)
            e, zz, z2, acc = z[:, 0], z[:, 1], z[:, 2], z[:, 3]
            step(ts(zz, e, 2.0, None, ALU.add))
            step(nc.vector.reciprocal(z2, zz))
            step(tt(zz, z2, e, ALU.mult))
            step(tt(z2, zz, zz, ALU.mult))
            step(nc.vector.memset(acc, 1.0 / 17))
            for odd in range(15, 0, -2):
                step(tt(acc, acc, z2, ALU.mult))
                step(ts(acc, acc, 1.0 / odd, None, ALU.add))
            step(tt(acc, acc, zz, ALU.mult))
            step(ts(z[:, 4], par[:, 2], -1.0, 0.0, ALU.mult, ALU.max))
            step(stt(z[:, 5], acc, 2.0, z[:, 4], ALU.mult, ALU.add))
            step(ts(dec[:, 0], z[:, 5], -LRU_C, None, ALU.mult))
            ts(dec[:, 1], z[:, 5], LRU_C, None, ALU.mult).then_inc(zeroed, 1)
            for k in range(NT):
                q = k % 2
                iv, a, t, m = ivs[:, q], as_[:, q], ts_[:, q], ms[:, q]
                dve.wait_ge(squared, k + 1)
                stt(m, m, 1.0, t, ALU.add, ALU.mult).then_inc(summed, 1)
                dve.wait_ge(u_in[q], 16 * (k // 2 + 1))
                dve.wait_ge(sig, 2 * k + 2)
                step(tt(iv, iv, x2[:, q], ALU.mult))
                dve.wait_ge(rooted, k + 1)
                step(tt(m, m, iv, ALU.mult))
                step(nc.vector.tensor_tensor_scan(t, a, m, 0.0, ALU.mult, ALU.add))
                dve.wait_ge(g_in[q], 16 * (k // 2 + 1))
                if k >= 2:
                    dve.wait_ge(stored[q], 16 * (k // 2))
                tt(ob[:, q], t, gate[:, q], ALU.mult).then_inc(scanned, 1)

        @block.tensor
        def _(pe):
            pe.wait_ge(const_in, 16 * 5)
            for k in range(NT):
                pe.wait_ge(u_in[k % 2], 16 * (k // 2 + 1))
                if k >= 1:
                    pe.wait_ge(sig, 2 * k)
                for half, w in enumerate((wa, wx)):
                    for c in range(NCH):
                        mm = nc.tensor.matmul(ps[:, half, c * CH:(c + 1) * CH], w[:, k], x2[:, k % 2, c * CH:(c + 1) * CH],
                                              start=True, stop=True)
                mm.then_inc(gates, 1)

        @block.scalar
        def _(act):
            act.wait_ge(const_in, 16 * 5)
            nc.scalar.activation(z[:, 1], par[:, 2], ACT.Abs).then_inc(expd, 1)
            act.wait_ge(expd, 1)
            nc.scalar.activation(z[:, 0], z[:, 1], ACT.Exp, scale=-1.0).then_inc(small, 1)
            act.wait_ge(zeroed, 1)
            for k in range(NT):
                r, iv, a, t, m = rs[:, k % 2], ivs[:, k % 2], as_[:, k % 2], ts_[:, k % 2], ms[:, k % 2]
                act.wait_ge(gates, k + 1)
                wait(act, scanned, k - 1)
                nc.scalar.activation(r, ps[:, 0], ACT.Sigmoid, bias=par[:, 0, k:k + 1]).then_inc(sig, 1)
                nc.scalar.activation(iv, ps[:, 1], ACT.Sigmoid, bias=par[:, 1, k:k + 1]).then_inc(sig, 1)
                act.wait_ge(sig, 2 * k + 1)
                nc.scalar.activation(t, r, ACT.Tanh, scale=dec[:, 1, k:k + 1])
                nc.scalar.activation(a, r, ACT.Exp, scale=dec[:, 0, k:k + 1]).then_inc(expd, 1)
                act.wait_ge(expd, k + 2)
                nc.scalar.activation(m, a, ACT.Square).then_inc(squared, 1)
                act.wait_ge(summed, k + 1)
                nc.scalar.activation(m, m, ACT.Sqrt).then_inc(rooted, 1)


def shifted(eng, pairs, ahead, behind):
    ahead(0, 0)

    def pair(i, last):
        ahead(i, 1)
        behind(i, 0)
        if not last:
            ahead(i + 1, 0)
        behind(i, 1)
    pair(0, pairs == 1)
    if pairs > 2:
        with eng.Fori(1, pairs - 1, 1) as i:
            pair(i, False)
    if pairs > 1:
        pair(pairs - 1, True)



LEVELS = 7


def hgrn(nc, name, q_d, k_d, cum_d, v_d, mask_d, out_d):
    N, H = SEQ, HGH
    C = N // P
    NX = LEVELS + 2
    NA = NX + 2
    with Stage(nc, name) as s:
        qs, ks, cum = s.sb("q", [P, H, N]), s.sb("k", [P, H, N]), s.sb("cum", [P, H, N])
        X = s.sb("X", [P, 2, NX, H, P])
        S, kd = s.sb("S", [P, 2, H, P]), s.sb("kd", [P, 2, H, P])
        state, last = s.sb("state", [P, 2, H, P]), s.sb("last", [P, 2, H])
        v, ktok, ob = s.sb("v", [P, 2, H * P]), s.sb("ktok", [P, 2, H * P]), s.sb("o", [P, 2, H, P])
        mask, ident = s.sb("mask", [P, LEVELS + 1, P], I32), s.sb("ident", [P, P])
        psL, psO, psK, psU = (s.ps(n, [P, 2, H * P]) for n in ("L", "O", "K", "U"))
        const_in, const, eye, inputs = s.sem("const_in"), s.sem("const"), s.sem("eye"), s.sem("inputs")
        dve_passed, pool_passed = s.sem("dve_passed"), s.sem("pool_passed")
        v_in, stored = s.sems("v_in", 2), s.sems("stored", 2)
        differed, expd, mult, levelled, picked = (s.sem(n) for n in ("differed", "expd", "mult", "levelled", "picked"))
        turned, kmoved, updated, stated, outed, omoved = (s.sem(n) for n in ("turned", "kmoved", "updated", "stated", "outed", "omoved"))
        block = s.block()

        @block.sync
        def _(sp):
            def quarter(g):
                tt = slice(g * 4 * P, (g + 1) * 4 * P)
                for dst, src in ((cum, cum_d), (ks, k_d), (qs, q_d)):
                    sp.dma_start(dst[:, :, tt], src[:, :, tt].rearrange("h p t -> p h t")).then_inc(inputs, 16)
                sp.wait_ge(inputs, 48 * (g + 1))

            quarter(0)
            sp.dma_start(mask[:], mask_d).then_inc(const_in, 16)
            for g in range(1, C // 4):
                quarter(g)

            def load(c, q):
                wait(sp, outed, c - 1)
                wait(sp, updated, c - 1)
                sp.dma_start(v[:, q], v_d[c]).then_inc(v_in[q], 16)
            steps(sp, C, load)

        @block.scalar
        def _(act):
            def exps(i, q):
                at = ds((i * 2 + q) * P, P)
                c = i * 2 + q
                for n in range(NX):
                    if n == LEVELS:
                        nc.scalar.activation(X[:, q, n], cum[:, :, at], ACT.Exp).then_inc(expd, 1)
                    else:
                        k = n if n < LEVELS else LEVELS
                        act.wait_ge(differed, c * (LEVELS + 1) + (k + 1))
                        nc.scalar.activation(X[:, q, n], X[:, q, n], ACT.Exp).then_inc(expd, 1)
                nc.scalar.activation(last[:, q], cum[:, :, ds(c * P + (P - 1), 1)].rearrange("p h o -> p (h o)"), ACT.Exp).then_inc(expd, 1)
                nc.scalar.copy(kd[:, q], ks[:, :, at]).then_inc(expd, 1)

            def moves(i, q):
                c = i * 2 + q
                act.wait_ge(turned, c + 1)
                wait(act, updated, c - 1)
                nc.scalar.copy(ktok[:, q], psK[:, q]).then_inc(kmoved, 1)
                act.wait_ge(outed, c + 1)
                if not (isinstance(i, int) and i == 0):
                    act.wait_ge(stored[q], i * 16)
                nc.scalar.copy(ob[:, q].rearrange("p h t -> p (h t)"), psO[:, q]).then_inc(omoved, 1)
            shifted(act, C // 2, exps, moves)

        @block.vector
        def _(dve):
            nc.vector.memset(S[:], 0.0).then_inc(const, 1)
            nc.vector.memset(state[:], 0.0).then_inc(const, 1)
            dve.wait_ge(const, 2)
            dve.wait_ge(const_in, 16)

            def differences(i, q, n):
                c = i * 2 + q
                if n == 0:
                    dve.wait_ge(inputs, i // 2 * 48 + 48)
                    wait(dve, outed, c - 1)
                cc = cum[:, :, ds(c * P, P)]
                if n == LEVELS:
                    nc.vector.tensor_tensor(X[:, q, n + 1], cc[:, :, P - 1:P].broadcast_to([P, H, P]), cc, ALU.subtract).then_inc(differed, 1)
                    return
                m = P >> (n + 1)
                pair = cc.rearrange("p h (g b m) -> p h g b m", b=2, m=m)
                x = X[:, q, n].rearrange("p h (g b m) -> p h g b m", b=2, m=m)
                if m == 1:
                    nc.vector.tensor_tensor(x[:, :, :, 1, 0], pair[:, :, :, 1, 0], pair[:, :, :, 0, 0], ALU.subtract)
                    nc.vector.memset(x[:, :, :, 0, 0], 0.0).then_inc(differed, 1)
                elif m == P // 2:
                    edge = pair[:, :, 0, 0, m - 1:m].broadcast_to([P, H, m])
                    nc.vector.tensor_tensor(x[:, :, 0, 1], pair[:, :, 0, 1], edge, ALU.subtract)
                    nc.vector.tensor_tensor(x[:, :, 0, 0], edge, pair[:, :, 0, 0], ALU.subtract).then_inc(differed, 1)
                else:
                    edge = pair[:, :, :, 0, m - 1:m].broadcast_to([P, H, P // (2 * m), m])
                    nc.vector.tensor_tensor(x[:, :, :, 1], pair[:, :, :, 1], edge, ALU.subtract)
                    nc.vector.tensor_tensor(x[:, :, :, 0], edge, pair[:, :, :, 0], ALU.subtract).then_inc(differed, 1)

            def pick(i, q, n):
                c = i * 2 + q
                dve.wait_ge(levelled, c * (LEVELS + 1) + (n + 1))
                wait(dve, outed, c - 1)
                wait_apart(dve, picked, c * (LEVELS + 1) + n, dve_passed)
                nc.vector.copy_predicated(S[:, q], bcast(mask[:, n], H), psL[:, n % 2].rearrange("p (h t) -> p h t", h=H)).then_inc(picked, 1)

            def update(i, q):
                c = i * 2 + q
                dve.wait_ge(updated, c + 1)
                dve.wait_ge(expd, c * NA + (NX + 1))
                wait(dve, stated, c)
                for h in range(H):
                    ins = nc.vector.scalar_tensor_tensor(state[:, q, h], state[:, 1 - q, h], last[:, q, h:h + 1],
                                                         psU[:, q, h * P:(h + 1) * P], ALU.mult, ALU.add)
                ins.then_inc(stated, 1)

            def pair(i, last_pair):
                for q in range(2):
                    for n in range(LEVELS + 1):
                        if q == 0:
                            differences(i, 1, n)
                        elif not last_pair:
                            differences(i + 1, 0, n)
                        pick(i, q, n)
                    update(i, q)
            for n in range(LEVELS + 1):
                differences(0, 0, n)
            pair(0, False)
            with dve.Fori(1, C // 2 - 1, 1) as i:
                pair(i, False)
            pair(C // 2 - 1, True)

        @block.gpsimd
        def _(pool):
            pool.memset(ident[:], 0.0).then_inc(eye, 1)
            pool.wait_ge(eye, 1)
            pool.affine_select(out=ident[:], in_=ident[:], compare_op=ALU.not_equal, fill=1.0, base=0,
                               pattern=[[-1, P]], channel_multiplier=1).then_inc(eye, 1)

            def products(i, q):
                c = i * 2 + q
                at = ds(c * P, P)
                for n in range(NX):
                    wait_apart(pool, expd, c * NA + (n + 1), pool_passed)
                    if n >= LEVELS:
                        pool.tensor_tensor(X[:, q, n], X[:, q, n], (qs, ks)[n - LEVELS][:, :, at], ALU.mult).then_inc(mult, 1)
                        continue
                    m = P >> (n + 1)
                    x = X[:, q, n].rearrange("p h (g b m) -> p h g b m", b=2, m=m)
                    for b, src in ((1, qs), (0, ks)):
                        part = src[:, :, at].rearrange("p h (g b m) -> p h g b m", b=2, m=m)
                        if m == 1:
                            o, w = x[:, :, :, b, 0], part[:, :, :, b, 0]
                        elif m == P // 2:
                            o, w = x[:, :, 0, b], part[:, :, 0, b]
                        else:
                            o, w = x[:, :, :, b], part[:, :, :, b]
                        ins = pool.tensor_tensor(o, o, w, ALU.mult)
                    ins.then_inc(mult, 1)

            def store(i, q):
                c = i * 2 + q
                wait_apart(pool, omoved, c + 1, pool_passed)
                pool.dma_start(out_d[:, :, ds(c * P, P)].rearrange("h p t -> p h t"), ob[:, q]).then_inc(stored[q], 16)
            shifted(pool, C // 2, products, store)
            for q in range(2):
                pool.wait_ge(stored[q], 16 * (C // 2))

        @block.tensor
        def _(pe):
            pe.wait_ge(eye, 2)
            pe.wait_ge(const, 2)

            def chunk(c, q):
                at = ds(c * P, P)
                half = c // 2 if isinstance(c, int) else (c - q) // 2
                for n in range(LEVELS + 1):
                    if n < LEVELS:
                        pe.wait_ge(mult, c * NX + (n + 1))
                    wait(pe, picked, c * (LEVELS + 1) + (n - 1))
                    for h in range(H):
                        o = psL[:, n % 2, h * P:(h + 1) * P]
                        if n < LEVELS:
                            mm = nc.tensor.matmul(o, X[:, q, n, h], X[:, q, n, h], start=True, stop=True)
                        else:
                            if h == 0:
                                pe.wait_ge(expd, c * NA + NA)
                            mm = nc.tensor.matmul(o, kd[:, q, h], qs[:, h, at], start=True, stop=True)
                    mm.then_inc(levelled, 1)
                pe.wait_ge(mult, c * NX + NX)
                wait(pe, kmoved, c - 1)
                for h in range(H):
                    tr = nc.tensor.transpose(psK[:, q, h * P:(h + 1) * P], X[:, q, NX - 1, h], ident[:])
                tr.then_inc(turned, 1)
                pe.wait_ge(v_in[q], half * 16 + 16)
                wait(pe, omoved, c - 1)
                wait(pe, stated, c)
                pe.wait_ge(picked, (c + 1) * (LEVELS + 1))
                for h in range(H):
                    o = psO[:, q, h * P:(h + 1) * P]
                    nc.tensor.matmul(o, v[:, q, h * P:(h + 1) * P], S[:, q, h], start=True, stop=False)
                    mm = nc.tensor.matmul(o, state[:, 1 - q, h], X[:, q, LEVELS, h], start=False, stop=True)
                mm.then_inc(outed, 1)
                pe.wait_ge(kmoved, c + 1)
                wait(pe, stated, c - 1)
                for h in range(H):
                    mm = nc.tensor.matmul(psU[:, q, h * P:(h + 1) * P], ktok[:, q, h * P:(h + 1) * P],
                                          v[:, q, h * P:(h + 1) * P], start=True, stop=True)
                mm.then_inc(updated, 1)
            steps(pe, C, chunk)



def ssd(nc, name, x_d, z_d, dt_d, bias_d, alog_d, skip_d, tri_d, out_d):
    N = SEQ
    C = N // P
    H = SH // SG
    HP = SW // SH
    GT = SW // SG // P
    NI = 4
    NB = 4
    with Stage(nc, name) as s:
        xs, Bt, Ct, zb = s.sb("x", [P, NB, GT, P]), s.sb("B", [P, NB, P]), s.sb("C", [P, NB, P]), s.sb("z", [P, NB, GT, P])
        dt, dA, ncum = s.sb("dt", [P, C, SH]), s.sb("dA", [P, C, SH]), s.sb("ncum", [P, C, SH])
        tmp, bias, alog = s.sb("tmp", [P, C, SH]), s.sb("bias", [P, SH]), s.sb("alog", [P, SH])
        skip, tri, ident = s.sb("skip", [P, SW // P]), s.sb("tri", [P, P]), s.sb("ident", [P, P])
        dtT = s.sb("dtT", [SH, N])
        dAu, wl = s.sb("dAu", [P, 2, H]), s.sb("wl", [P, 2, H])
        dec = s.sb("dec", [P, 2, H])
        CB, Btok = s.sb("CB", [P, 2, P]), s.sb("Btok", [P, 2, P])
        xdt, xw = s.sb("xdt", [P, 2, H, HP]), s.sb("xw", [P, 2, H, HP])
        L, EC = s.sb("L", [P, 2, H, P]), s.sb("EC", [P, 2, H, P])
        state, ob = s.sb("state", [P, 2, H, HP]), s.sb("o", [P, 2, GT, P])
        psB = s.ps("cumB", [P, 2, H, P])
        psM, psX = s.ps("psM", [P, CH]), s.ps("psX", [P, CH])
        psY, psU = s.ps("psY", [P, CH]), s.ps("psU", [P, CH])
        const_in, dt_in, eye, zero, small, dts, cums = (s.sem(n) for n in ("const_in", "dt_in", "eye", "zero", "small", "dts", "cums"))
        pool_passed, turnedT = s.sem("pool_passed"), s.sem("turnedT")
        unit_in, stored = s.sems("unit_in", NB), s.sems("stored", 2)
        copied, products, spread, clipped, expd, masked, widened = (
            s.sem(n) for n in ("copied", "products", "spread", "clipped", "expd", "masked", "widened"))
        bmoved, xtimed, wlog, wexp, weighted, ends = (s.sem(n) for n in ("bmoved", "xtimed", "wlog", "wexp", "weighted", "ends"))
        yed, updated, decayed, stated, skipped, gated = (s.sem(n) for n in ("yed", "updated", "decayed", "stated", "skipped", "gated"))
        block = s.block()

        def units(eng, ahead, behind, after=lambda i, q, r: None):
            def four(j, last):
                for r in range(NB):
                    follows = unit(j, r + 1) if r + 1 < NB else unit(j + 1, 0)
                    end = last and r == NB - 1
                    if not end:
                        ahead(*follows)
                    behind(*unit(j, r))
                    if not end:
                        after(*follows)

            def unit(j, r):
                return j * 2 + r // 2, r % 2, r
            ahead(*unit(0, 0))
            after(*unit(0, 0))
            four(0, False)
            with eng.Fori(1, C // 2 - 1, 1) as j:
                four(j, False)
            four(C // 2 - 1, True)

        @block.sync
        def _(sp):
            sp.dma_start(dtT[:], dt_d[0:SH]).then_inc(dt_in, 16)
            for dst, src in ((bias, bias_d), (alog, alog_d), (skip, skip_d), (tri, tri_d)):
                sp.dma_start(dst[:], src).then_inc(const_in, 16)

            def load(i, q, r):
                u = i * 2 + q
                wait(sp, gated, u + 1 - NB)
                wait(sp, updated, u + 1 - NB)
                at = ds(i * P, P)
                sp.dma_start(xs[:, r], x_d[q * GT:(q + 1) * GT, :, at].rearrange("a p t -> p a t")).then_inc(unit_in[r], 16)
                sp.dma_start(Bt[:, r], x_d[SG * GT + q, :, at]).then_inc(unit_in[r], 16)
                sp.dma_start(Ct[:, r], x_d[SG * GT + SG + q, :, at]).then_inc(unit_in[r], 16)
                sp.dma_start(zb[:, r], z_d[q * GT:(q + 1) * GT, :, at].rearrange("a p t -> p a t")).then_inc(unit_in[r], 16)
            units(sp, load, lambda i, q, r: None)

        @block.gpsimd
        def _(pool):
            pool.memset(ident[:], 0.0).then_inc(eye, 1)
            pool.wait_ge(eye, 1)
            pool.affine_select(out=ident[:], in_=ident[:], compare_op=ALU.not_equal, fill=1.0, base=0,
                               pattern=[[-1, P]], channel_multiplier=1).then_inc(eye, 1)

            def weights(i, q, r):
                u = i * 2 + q
                pool.wait_ge(masked, u + 1)
                wait_apart(pool, expd, 2 * u + 1, pool_passed)
                pool.tensor_tensor(L[:, q], L[:, q], bcast(CB[:, q], H), ALU.mult).then_inc(widened, 1)
                wait_apart(pool, expd, 2 * u + 2, pool_passed)
                pool.tensor_tensor(EC[:, q], EC[:, q], bcast(Ct[:, r], H), ALU.mult).then_inc(widened, 1)

            def store(i, q, r):
                wait_apart(pool, gated, i * 2 + (q + 1), pool_passed)
                pool.dma_start(out_d[q * GT:(q + 1) * GT, :, ds(i * P, P)].rearrange("a p t -> p a t"), ob[:, q]).then_inc(stored[q], 16)
            units(pool, weights, store)
            for q in range(2):
                pool.wait_ge(stored[q], 16 * C)

        @block.scalar
        def _(act):
            act.wait_ge(const_in, 64)
            nc.scalar.activation(alog[:], alog[:], ACT.Exp).then_inc(small, 1)
            act.wait_ge(dts, 1)
            nc.scalar.activation(tmp[:], dt[:], ACT.Abs).then_inc(small, 1)
            act.wait_ge(small, 2)
            nc.scalar.activation(tmp[:], tmp[:], ACT.Exp, scale=-1.0).then_inc(small, 1)
            act.wait_ge(small, 3)
            nc.scalar.activation(tmp[:], tmp[:], ACT.Ln, bias=1.0).then_inc(small, 1)

            def front(i, q, r):
                u = i * 2 + q
                act.wait_ge(clipped, u + 1)
                nc.scalar.activation(L[:, q], L[:, q], ACT.Exp).then_inc(expd, 1)
                act.wait_ge(wlog, u + 1)
                wait(act, yed, u - 1)
                nc.scalar.activation(EC[:, q], psB[:, q], ACT.Exp).then_inc(expd, 1)
                wait(act, decayed, u - 1)
                nc.scalar.activation(dec[:, q], psB[:, q, :, P - 1], ACT.Exp).then_inc(ends, 1)
                act.wait_ge(masked, u + 1)
                wait(act, updated, u - 1)
                nc.scalar.copy(Btok[:, q], psM[:, P:2 * P]).then_inc(bmoved, 1)
                nc.scalar.activation(wl[:, q], wl[:, q], ACT.Exp).then_inc(wexp, 1)
            units(act, front, lambda i, q, r: None)

        @block.vector
        def _(dve):
            ts, tt, stt = nc.vector.tensor_scalar, nc.vector.tensor_tensor, nc.vector.scalar_tensor_tensor
            nc.vector.memset(state[:], 0.0).then_inc(zero, 1)
            dve.wait_ge(const_in, 64)
            dve.wait_ge(turnedT, 1)
            tt(dt[:], psX[:, 0:C * SH].rearrange("p (c h) -> p c h", h=SH), bcast(bias[:], C), ALU.add).then_inc(dts, 1)
            dve.wait_ge(dts, 1)
            dve.wait_ge(small, 4)
            stt(dt[:], dt[:], 0.0, tmp[:], ALU.max, ALU.add).then_inc(dts, 1)
            dve.wait_ge(dts, 2)
            ts(alog[:], alog[:], -1.0, None, ALU.mult).then_inc(dts, 1)
            dve.wait_ge(dts, 3)
            tt(dA[:], dt[:], bcast(alog[:], C), ALU.mult).then_inc(dts, 1)
            dve.wait_ge(cums, 1)
            ts(ncum[:].rearrange("p c h -> p (c h)"), psX[:, 0:C * SH], -1.0, None, ALU.mult).then_inc(dts, 1)
            dve.wait_ge(dts, 5)

            def heads(t, i, q):
                return t[:, ds(i, 1), q * H:(q + 1) * H].rearrange("p a h -> p (a h)")

            def front(i, q, r):
                u = i * 2 + q
                wait(dve, spread, u - 1)
                nc.vector.tensor_copy(dAu[:, q], heads(dA, i, q)).then_inc(copied, 1)
                dve.wait_ge(products, u + 1)
                wait(dve, updated, u - 1)
                tt(CB[:, q], psM[:, 0:P], tri[:], ALU.mult).then_inc(masked, 1)
                tt(xdt[:, q], psX[:].rearrange("p (h e) -> p h e", h=H), bcast(heads(dt, i, q), HP, 2), ALU.mult).then_inc(xtimed, 1)
                dve.wait_ge(spread, u + 1)
                for h in range(H):
                    ins = ts(L[:, q, h], psB[:, q, h], heads(ncum, i, q)[:, h:h + 1], 0.0, ALU.add, ALU.min)
                ins.then_inc(clipped, 1)
                tt(wl[:, q], psB[:, q, :, P - 1], heads(ncum, i, q), ALU.add).then_inc(wlog, 1)

            def weigh(i, q, r):
                u = i * 2 + q
                dve.wait_ge(wexp, u + 1)
                dve.wait_ge(xtimed, u + 1)
                wait(dve, updated, u - 1)
                tt(xw[:, q], xdt[:, q], bcast(wl[:, q], HP, 2), ALU.mult).then_inc(weighted, 1)

            def back(i, q, r):
                u = i * 2 + q
                dve.wait_ge(yed, u + 1)
                dve.wait_ge(ends, u + 1)
                tt(state[:, q], state[:, q], bcast(dec[:, q], HP, 2), ALU.mult).then_inc(decayed, 1)
                dve.wait_ge(updated, u + 1)
                dve.wait_ge(decayed, u + 1)
                tt(state[:, q], state[:, q], psU[:].rearrange("p (h e) -> p h e", h=H), ALU.add).then_inc(stated, 1)
                if not (isinstance(i, int) and i == 0):
                    dve.wait_ge(stored[q], i * 16)
                for a in range(GT):
                    ins = stt(ob[:, q, a], xs[:, r, a], skip[:, q * GT + a:q * GT + a + 1], psY[:, a * P:(a + 1) * P], ALU.mult, ALU.add)
                ins.then_inc(skipped, 1)
                dve.wait_ge(skipped, u + 1)
                tt(ob[:, q], ob[:, q], zb[:, r], ALU.mult).then_inc(gated, 1)
            units(dve, front, back, weigh)

        @block.tensor
        def _(pe):
            pe.wait_ge(eye, 2)
            pe.wait_ge(const_in, 64)
            pe.wait_ge(zero, 1)
            pe.wait_ge(dt_in, 16)
            for c in range(C):
                tr = nc.tensor.transpose(psX[:, c * SH:(c + 1) * SH], dtT[:, c * P:(c + 1) * P], ident[0:SH, 0:SH])
            tr.then_inc(turnedT, 1)
            pe.wait_ge(dts, 4)
            nc.tensor.matmul(psX[:, 0:C * SH], tri[:], dA[:].rearrange("p c h -> p (c h)"), start=True, stop=True).then_inc(cums, 1)
            pe.wait_ge(dts, 5)

            def front(i, q, r):
                u = i * 2 + q
                pe.wait_ge(unit_in[r], ((i // 2) if isinstance(i, int) else (i - r // 2) // 2) * (16 * NI) + 16 * NI)
                wait(pe, masked, u)
                wait(pe, bmoved, u)
                wait(pe, xtimed, u)
                nc.tensor.matmul(psM[:, 0:P], Bt[:, r], Ct[:, r], start=True, stop=True)
                nc.tensor.transpose(psM[:, P:2 * P], Bt[:, r], ident[:])
                for a in range(GT):
                    mm = nc.tensor.transpose(psX[:, a * P:(a + 1) * P], xs[:, r, a], ident[:])
                mm.then_inc(products, 1)
                pe.wait_ge(copied, u + 1)
                wait(pe, expd, 2 * u - 2)
                wait(pe, ends, u - 1)
                for h in range(H):
                    mm = nc.tensor.matmul(psB[:, q, h], dAu[:, q, h:h + 1].broadcast_to([P, P]), tri[:], start=True, stop=True)
                mm.then_inc(spread, 1)

            def back(i, q, r):
                u = i * 2 + q
                pe.wait_ge(widened, 2 * u + 2)
                if not (isinstance(i, int) and i == 0):
                    pe.wait_ge(stated, u - 1)
                wait(pe, skipped, u)
                for h in range(H):
                    rows = slice(h % 2 * HP, h % 2 * HP + HP)
                    o = psY[rows, h // 2 * P:(h // 2 + 1) * P]
                    nc.tensor.matmul(o, xdt[:, q, h], L[:, q, h], start=True, stop=False)
                    mm = nc.tensor.matmul(o, state[:, q, h], EC[:, q, h], start=False, stop=True)
                mm.then_inc(yed, 1)
                pe.wait_ge(weighted, u + 1)
                wait(pe, stated, u)
                nc.tensor.matmul(psU[:], Btok[:, q], xw[:, q].rearrange("p h e -> p (h e)"), start=True, stop=True).then_inc(updated, 1)
            units(pe, front, back)



def load_constants(nc, loads, zeros):
    with Stage(nc, "init") as s:
        z = s.sb("z", [P, P])
        loaded, zeroed, padded = s.sem("loaded"), s.sem("zeroed"), s.sem("padded")
        block = s.block()

        @block.vector
        def _(dve):
            nc.vector.memset(z[:], 0.0).then_inc(zeroed, 1)

        @block.sync
        def _(sp):
            for dst, src in loads:
                sp.dma_start(dst, src).then_inc(loaded, 16)
            sp.wait_ge(loaded, 16 * len(loads))
            sp.wait_ge(zeroed, 1)
            for dst in zeros:
                sp.dma_start(dst, z[:]).then_inc(padded, 16)
            sp.wait_ge(padded, 16 * len(zeros))


def program(nc, t, out):
    def dram(name, shape):
        return nc.dram_tensor(name, shape, F32, kind="Internal").ap()

    kpad, vpad = dram("kpad", [P, SEQ + 2 * P]), dram("vpad", [SEQ // P + 2, P, P])
    with ExitStack() as keep:
        def sb(name, shape):
            return keep.enter_context(nc.sbuf_tensor(name, shape, F32))

        mods = [(sb(f"mod1{l}", [P, 3 * KT, 2]), sb(f"gain1{l}", [P, KT, 2])) for l in range(DEPTH)]
        mod2, gain2 = sb("mod2", [P, 3 * KT, 1]), sb("gain2", [P, KT, 1])
        final_g, final_g2 = sb("final_g", [P, KT]), sb("final_g2", [P, KT])
        hg_g, ssd_g = sb("hg_g", [P, HW // P]), sb("ssd_g", [P, SW // P])
        load_constants(nc, [(final_g[:], t["final_g"]), (final_g2[:], t["final_norm_w_2"]),
                            (hg_g[:], t["hg_norm_w_2"]), (ssd_g[:], t["ssd_norm_w_2"])],
                       [kpad[:, 0:P], kpad[:, P + SEQ:], vpad[0], vpad[SEQ // P + 1]])
        modulations(nc, "ada", [(t["cond"], t["w_ada"][l], t["b_ada"][l], t["norm_g"][l], *mods[l], 2) for l in range(DEPTH)]
                    + [(t["cond_2"], t["w_ada_2"], t["b_ada_2"], t["norm_w_2"], mod2, gain2, 1)])

        xT, ctxT = t["x"], t["ctx"]
        for l in range(DEPTH):
            mod1, gain1 = mods[l]
            kcT, vc = dram(f"kcT{l}", [1, P, CTX]), dram(f"vc{l}", [CTX // P, P, P])
            more = l < DEPTH - 1
            for part in ("c", ""):
                n = f"{part}{l}"
                N, src, which = (CTX, ctxT, 1) if part else (SEQ, xT, 0)
                full = not part or more
                with ExitStack() as mixer:
                    cy = mixer.enter_context(nc.sbuf_tensor(f"cy{n}", [P, 2, N], F32)) if full else None
                    with nc.sbuf_tensor(f"h{n}", [P, 2, KT, N], F32R) as h:
                        norm(nc, f"norm{n}", src, N, gain1[:, :, which], out_sb=h, shift=mod1[:, 0:KT, which])
                        if full:
                            q, u = dram(f"q{n}", [4, P, N]), dram(f"u{n}", [N // P, P, 2 * P])
                            gates = dram(f"gates{n}", [8, P, N])
                            turn = ACT.Copy if part else "rope"
                            kout = kcT if part else kpad[:, P:P + SEQ].unsqueeze(0)
                            vout = vc if part else vpad[1:SEQ // P + 1]
                            with nc.sbuf_tensor(f"cu{n}", [P, 2, N + CONV_K - 1], F32) as cu:
                                project(nc, f"in{n}", h, N, t["w_in"][l],
                                        [("sigmoid", 2, None, 1.0), ("glu", 2, None, 1.0), (ACT.Silu, 8, gates, 1.0),
                                         (turn, 4, q, SCALE), (turn, 1, kout, 1.0)], tables=None if part else t["rope"],
                                        glu=(cu, cy), taps31=(t["conv_w"][l], t["conv_b"][l]))
                            project_tokens(nc, f"tok{n}", h, N, t["w_vu"][l], 3 * P, [(vout, 0, P), (u, P, 2 * P)])
                        else:
                            project(nc, f"in{n}", h, N, t["w_in"][l][16:17], [(ACT.Copy, 1, kcT, 1.0)])
                            project_tokens(nc, f"tok{n}", h, N, t["w_vu"][l][:, :, 0:P], P, [(vc, 0, P)])
                    if not full:
                        continue
                    y = dram(f"y{n}", [8, P, N])
                    conformer(nc, f"conf{n}", N, cy, t["conv_ln_g"][l], t["conv_ln_b"][l], gates[4:6], y[4:6])
                if part:
                    attention(nc, f"att{n}", N, q, kcT[0], vc, t["attn_sink"][l], gates[0:4], y[0:4])
                else:
                    attention(nc, f"att{n}", N, q, kcT[0], vc, t["attn_sink"][l], gates[0:4], y[0:4],
                              kpad, vpad, t["window"])
                fourier(nc, f"four{n}", N, u, t[f"fourier{N}"], t["heads"], t["w_four"][l], t["b_four"][l], gates[6:8], y[6:8])
                new = dram(f"x{n}", [KT, P, N])
                project_out(nc, f"out{n}", N, y, t["w_out"][l], mod1[:, 2 * KT:, which], src, new, KT)
                if part:
                    ctxT = new
                else:
                    xT = new

        x2, x3 = dram("x2", [KT, P, SEQ]), dram("x3", [KT, P, SEQ])
        norm(nc, "mid", xT, SEQ, final_g, out_dram=x2)
        ax, hk, hcum, xbc = dram("ax", [4, P, SEQ]), dram("hk", [4, P, SEQ]), dram("hcum", [4, P, SEQ]), dram("xbc", [12, P, SEQ])
        gates = dram("gates_2", [20, P, SEQ])
        hi, dt = dram("hi", [SEQ // P, P, HW]), dram("dt", [1, P, SEQ])
        with nc.sbuf_tensor("h_2", [P, 2, KT, SEQ], F32R) as h:
            norm(nc, "norm_2", x2, SEQ, gain2[:, :, 0], out_sb=h, shift=mod2[:, 0:KT, 0])
            project(nc, "in_2", h, SEQ, t["w_in_2"], [("conv", 4, ax, 1.0), ("conv_silu", 12, xbc, 1.0), ("decay", 4, (hk, hcum), 1.0),
                                                      (ACT.Silu, 20, gates, 1.0), (ACT.Copy, 1, dt, 1.0)],
                    taps4=(t["taps_2"], t["tap_bias_2"]))
            project_tokens(nc, "hi_2", h, SEQ, t["w_hi_2"], HW, [(hi, 0, HW)])
        y = dram("y_2", [16, P, SEQ])
        lru(nc, "lru", ax, t["lru_wa_2"], t["lru_ba_2"], t["lru_wx_2"], t["lru_bx_2"],
            t["lru_lambda_2"], gates[0:4], y[0:4])
        o_hg, o_ssd = dram("o_hg", [4, P, SEQ]), dram("o_ssd", [8, P, SEQ])
        hgrn(nc, "hgrn", gates[4:8], hk, hcum, hi, t["levels"], o_hg)
        norm(nc, "hgnorm", o_hg, SEQ, hg_g, out_dram=y[4:8], gate_d=gates[8:12], K=HW // P)
        ssd(nc, "ssd", xbc, gates[12:20], dt[0], t["ssd_dt_bias_2"], t["ssd_a_log_2"], t["ssd_d_2"], t["causal"], o_ssd)
        norm(nc, "ssdnorm", o_ssd, SEQ, ssd_g, out_dram=y[8:16], K=SW // SG // P, groups=SG)
        project_out(nc, "out_2", SEQ, y, t["w_out_2"], mod2[:, 2 * KT:, 0], x2, x3, 16)
        norm(nc, "final", x3, SEQ, final_g2, out_dram=out)



def rope_tables():
    pos = np.arange(SEQ)
    f = 10000.0 ** (-np.arange(16, dtype=np.float32) / 16)
    row = (pos // 64).astype(np.float32)[None] * f[:, None].astype(np.float32)
    col = (pos % 64).astype(np.float32)[None] * f[:, None].astype(np.float32)
    c = np.concatenate([np.cos(row), np.cos(row), np.cos(col), np.cos(col)])
    s = np.concatenate([-np.sin(row), np.sin(row), -np.sin(col), np.sin(col)])
    return np.stack([np.tile(c, (2, 1)), np.tile(s, (2, 1))]).astype(np.float32)


def window_masks():
    q, r = np.arange(P)[:, None], np.arange(P)[None, :]
    m = [np.where(r >= q, 0.0, NEG), np.where(r <= q, 0.0, NEG), np.full((P, P), NEG)]
    return np.stack(m, axis=1).astype(np.float32)


def fourier_table(N):
    R = N // 128
    n1, k2, k1 = np.arange(128)[None, :, None], np.arange(R)[:, None, None], np.arange(128)[None, None, :]
    ang = 2 * np.pi * ((n1 * (R * k1 + k2)) % N) / N
    c, s = np.cos(ang), np.sin(ang)
    sign = np.where(k2 <= R // 2, 1.0, -1.0)
    return np.concatenate([c, s, sign * s, -sign * c], axis=2).astype(np.float32)


def head_table():
    d = np.arange(64)
    ang = 2 * np.pi * ((d[:, None] * d[None, :]) % 64) / 64
    eye = np.eye(2)
    return np.stack([np.kron(eye, np.cos(ang)), np.kron(eye, np.sin(ang))], axis=1).astype(np.float32)


def hgrn_masks():
    s, t = np.arange(P)[:, None], np.arange(P)[None, :]
    out = []
    for n in range(LEVELS):
        m = P >> (n + 1)
        out.append((s // (2 * m) == t // (2 * m)) & (s // m % 2 == 0) & (t // m % 2 == 1))
    return np.ascontiguousarray(np.stack(out + [s == t], axis=1).astype(np.int32))


def blockdiag(w):
    out = np.zeros((P, 4, P), w.dtype)
    for h in range(8):
        r = slice(h % 2 * 64, h % 2 * 64 + 64)
        out[r, h // 2, r] = w[h]
    return out



def tiles(w):
    return np.ascontiguousarray(w.reshape(w.shape[0] // P, P, -1, P).transpose(2, 1, 0, 3))


def wide_tiles(w):
    return np.ascontiguousarray(w.reshape(w.shape[0] // P, P, -1, CH).transpose(2, 1, 0, 3))


def columns(v):
    return np.ascontiguousarray(v.reshape(-1, P).T)


def transposed(x):
    return np.ascontiguousarray(x.T.reshape(-1, P, x.shape[0]))


def taps(w):
    return np.ascontiguousarray(w.T.reshape(-1, P, w.shape[0]).transpose(1, 0, 2))


def everywhere(v):
    return np.ascontiguousarray(np.broadcast_to(v.reshape(1, -1), (P, v.size)))


def head_order():
    heads = [g * GQ + j for j in range(GQ) for g in range(NKV)]
    return np.concatenate([np.arange(h * HD, (h + 1) * HD) for h in heads])


def layout(a):
    order = head_order()
    edge = np.cumsum([0, 512, 128, 128, 512, 256, 256, 256, 256, 256])
    q, k, v, g_att, c_a, c_b, g_conv, f_u, g_four = (np.arange(edge[i], edge[i + 1]) for i in range(9))
    cols = np.concatenate([c_b, c_a, g_att[order], g_conv, g_four, q[order], k])
    vu = np.concatenate([v, f_u])
    kmajor = lambda w: np.ascontiguousarray(w.reshape(KT, P, -1).transpose(1, 0, 2))
    layers = lambda f, name: np.stack([f(a[name][l]) for l in range(DEPTH)])
    t = {
        "x": transposed(a["x"][0]), "ctx": transposed(a["ctx"][0]),
        "cond": np.ascontiguousarray(np.stack([columns(a["c"][0]), columns(a["c_ctx"])], axis=2)),
        "cond_2": columns(a["c_2"][0])[:, :, None].copy(),
        "w_ada": layers(wide_tiles, "w_ada"), "b_ada": layers(columns, "b_ada"), "norm_g": layers(columns, "norm_g"),
        "w_in": np.stack([tiles(a["w_in"][l][:, cols]) for l in range(DEPTH)]),
        "w_vu": np.stack([kmajor(a["w_in"][l][:, vu]) for l in range(DEPTH)]),
        "attn_sink": a["attn_sink"].reshape(DEPTH, 1, NH),
        "conv_w": layers(taps, "conv_w"), "conv_b": layers(columns, "conv_b"),
        "conv_ln_g": layers(columns, "conv_ln_g"), "conv_ln_b": layers(columns, "conv_ln_b"),
        "w_four": a["w_four"], "b_four": layers(columns, "b_four"),
        "w_out": np.stack([tiles(np.concatenate([a["w_out"][l][order], a["w_out"][l][ATT:]])) for l in range(DEPTH)]),
        "final_g": columns(a["final_g"]),
        "rope": rope_tables(), "window": window_masks(), "heads": head_table(),
        "fourier2048": fourier_table(SEQ), "fourier256": fourier_table(CTX),
    }
    edge = np.cumsum([0, 512, 512, 512, 512, 512, 512, 1024, 1536, 16])
    a_x, a_g, hg_q, hg_f, hg_i, hg_g, z, xbc, dt = (np.arange(edge[i], edge[i + 1]) for i in range(9))
    w = a["w_in_2"][0]
    t.update({
        "w_ada_2": wide_tiles(a["w_ada_2"][0]), "b_ada_2": columns(a["b_ada_2"][0]), "norm_w_2": columns(a["norm_w_2"][0]),
        "w_in_2": tiles(np.pad(w[:, np.concatenate([a_x, xbc, hg_f, a_g, hg_q, hg_g, z, dt])], ((0, 0), (0, P - SH)))),
        "w_hi_2": kmajor(w[:, hg_i]),
        "taps_2": np.concatenate([taps(a["lru_conv_w_2"][0]), taps(a["ssd_conv_w_2"][0])], axis=1),
        "tap_bias_2": np.concatenate([columns(a["lru_conv_b_2"][0]), columns(a["ssd_conv_b_2"][0])], axis=1),
        "lru_wa_2": blockdiag(a["lru_wa_2"][0]), "lru_wx_2": blockdiag(a["lru_wx_2"][0]),
        "lru_ba_2": columns(a["lru_ba_2"][0].reshape(-1)), "lru_bx_2": columns(a["lru_bx_2"][0].reshape(-1)),
        "lru_lambda_2": columns(a["lru_lambda_2"][0]), "hg_norm_w_2": columns(a["hg_norm_w_2"][0]),
        "ssd_dt_bias_2": everywhere(a["ssd_dt_bias_2"][0]), "ssd_a_log_2": everywhere(a["ssd_a_log_2"][0]),
        "ssd_d_2": columns(np.repeat(a["ssd_d_2"][0], SW // SH)), "ssd_norm_w_2": columns(a["ssd_norm_w_2"][0]),
        "w_out_2": tiles(a["w_out_2"][0]), "final_norm_w_2": columns(a["final_norm_w_2"]),
        "levels": hgrn_masks(), "causal": np.triu(np.ones((P, P), np.float32)),
    })
    return t


def kernel(**inputs):
    import concourse.bacc as bacc
    from concourse.bass_utils import run_bass_kernel_spmd

    arrays = {f"in_{n}": v for n, v in layout({n: np.asarray(v) for n, v in inputs.items()}).items()}
    nc = bacc.Bacc("TRN2", target_bir_lowering=False, num_devices=1)
    aps = {n[3:]: nc.dram_tensor(n, v.shape, mybir.dt.from_np(v.dtype), kind="ExternalInput").ap() for n, v in arrays.items()}
    out = nc.dram_tensor("out", (KT, P, SEQ), F32, kind="ExternalOutput").ap()
    program(nc, aps, out)
    r = run_bass_kernel_spmd(nc, [arrays], core_ids=[0])
    return np.ascontiguousarray(r.results[0]["out"].reshape(D, SEQ).T)[None]
```
